# Optimizing a Trainium2 kernel written in Bass

```python
import math
import jax, jax.numpy as jnp
from jax import lax
import numpy as np

D_MODEL = 2048
BATCH = 1
SEQ = 256
DEPTH = 1

HEAD_DIM = 128
GRID_W = 64
Q_BLOCK = 128
EPS = 1e-6
A_HEADS = D_MODEL // (2 * HEAD_DIM)
A_KV_HEADS = A_HEADS // 4
A_GROUP = A_HEADS // A_KV_HEADS
A_ROPE_THETA = 10000.0
AXIAL_DIM = HEAD_DIM // 2
B_VDIM = 2 * HEAD_DIM
B_HEADS = D_MODEL // (2 * B_VDIM)
PARTIAL_ROPE_DIM = HEAD_DIM // 4
PARTIAL_ROPE_THETA = 500000.0
A_Q = A_HEADS * HEAD_DIM
A_KV = A_KV_HEADS * HEAD_DIM
B_QK = B_HEADS * 2 * HEAD_DIM
B_V = B_HEADS * B_VDIM
D_IN = A_Q + 2 * A_KV + 2 * B_QK + B_V
D_MIX = A_Q + B_V
D_FF = 5632


def _rms_norm(x, gain):
    x32 = x.astype(jnp.float32)
    y = x32 * lax.rsqrt(jnp.mean(x32 * x32, axis=-1, keepdims=True) + EPS)
    return (y * gain.astype(jnp.float32)).astype(x.dtype)

def _rope_table(pos, dim, theta):
    inv_freq = theta ** (-jnp.arange(0, dim, 2, dtype=jnp.float32) / dim)
    ang = pos[:, None] * inv_freq[None, :]
    return jnp.cos(ang), jnp.sin(ang)

def _apply_rope(x, cos, sin):
    half = x.shape[-1] // 2
    shape = (1, x.shape[1]) + (1,) * (x.ndim - 3) + (half,)
    c = cos.reshape(shape).astype(x.dtype)
    s = sin.reshape(shape).astype(x.dtype)
    x1, x2 = x[..., :half], x[..., half:]
    return jnp.concatenate([x1 * c - x2 * s, x2 * c + x1 * s], axis=-1)

def _axial_rope(x, row_cs, col_cs):
    return jnp.concatenate([
        _apply_rope(x[..., :AXIAL_DIM], *row_cs),
        _apply_rope(x[..., AXIAL_DIM:], *col_cs)], axis=-1)

def _partial_rope(x, cs):
    return jnp.concatenate([
        _apply_rope(x[..., :PARTIAL_ROPE_DIM], *cs),
        x[..., PARTIAL_ROPE_DIM:]], axis=-1)

def _sweep_queries(fn, q):
    b, s = q.shape[0], q.shape[1]
    nb = s // Q_BLOCK
    qb = jnp.moveaxis(q.reshape((b, nb, Q_BLOCK) + q.shape[2:]), 1, 0)
    out = lax.map(fn, qb)
    return jnp.moveaxis(out, 0, 1).reshape(b, s, -1)

def _swiglu(h, w_gu, w_down):
    g, u = jnp.split(h @ w_gu, 2, axis=-1)
    return (jax.nn.silu(g) * u) @ w_down

def _gqa_axial(qa, ka, va):
    scale = HEAD_DIM ** -0.5
    b = qa.shape[0]

    def block(qb):
        qb = qb.reshape(b, Q_BLOCK, A_KV_HEADS, A_GROUP, HEAD_DIM)
        s = jnp.einsum('bqgrd,bkgd->bgrqk', qb, ka).astype(jnp.float32) * scale
        p = jax.nn.softmax(s, axis=-1).astype(va.dtype)
        o = jnp.einsum('bgrqk,bkgd->bqgrd', p, va)
        return o.reshape(b, Q_BLOCK, A_Q)

    return _sweep_queries(block, qa)

def _diff_attention(qd, kd, vd, lam, lambda_init, subln):
    scale = HEAD_DIM ** -0.5
    b = qd.shape[0]

    def block(qb):
        s = jnp.einsum('bqhcd,bkhcd->bhcqk', qb, kd).astype(jnp.float32) * scale
        p = jax.nn.softmax(s, axis=-1)
        attn = (p[:, :, 0] - lam * p[:, :, 1]).astype(vd.dtype)
        o = jnp.einsum('bhqk,bkhe->bqhe', attn, vd)
        o = _rms_norm(o, subln) * (1.0 - lambda_init)
        return o.reshape(b, Q_BLOCK, B_V)

    return _sweep_queries(block, qd)

def first_inputs(seed: int = 0) -> dict:
    key = jax.random.key(seed)
    ks = jax.random.split(key, 24)
    f32 = jnp.float32

    def w(k, shape, fan_in):
        return jax.random.normal(k, shape, f32) * (fan_in ** -0.5)

    def gain(k, shape):
        return 1.0 + 0.02 * jax.random.normal(k, shape, f32)

    return {
        "x": jax.random.normal(ks[0], (BATCH, SEQ, D_MODEL), f32),
        "ffn1_norm": gain(ks[1], (DEPTH, D_MODEL)),
        "ffn1_w_gu": w(ks[2], (DEPTH, D_MODEL, 2 * D_FF), D_MODEL),
        "ffn1_w_down": w(ks[3], (DEPTH, D_FF, D_MODEL), D_FF),
        "mix_norm": gain(ks[4], (DEPTH, D_MODEL)),
        "w_in": w(ks[5], (DEPTH, D_MODEL, D_IN), D_MODEL),
        "a_q_norm": gain(ks[6], (DEPTH, HEAD_DIM)),
        "a_k_norm": gain(ks[7], (DEPTH, HEAD_DIM)),
        "b_q_norm": gain(ks[8], (DEPTH, HEAD_DIM)),
        "b_k_norm": gain(ks[9], (DEPTH, HEAD_DIM)),
        "b_lambda_q1": 0.1 * jax.random.normal(ks[10], (DEPTH, HEAD_DIM), f32),
        "b_lambda_k1": 0.1 * jax.random.normal(ks[11], (DEPTH, HEAD_DIM), f32),
        "b_lambda_q2": 0.1 * jax.random.normal(ks[12], (DEPTH, HEAD_DIM), f32),
        "b_lambda_k2": 0.1 * jax.random.normal(ks[13], (DEPTH, HEAD_DIM), f32),
        "b_subln": gain(ks[14], (DEPTH, B_VDIM)),
        "w_out": w(ks[15], (DEPTH, D_MIX, D_MODEL), D_MIX),
        "ffn2_norm": gain(ks[16], (DEPTH, D_MODEL)),
        "ffn2_w_gu": w(ks[17], (DEPTH, D_MODEL, 2 * D_FF), D_MODEL),
        "ffn2_w_down": w(ks[18], (DEPTH, D_FF, D_MODEL), D_FF),
        "out_norm": gain(ks[19], (DEPTH, D_MODEL)),
    }

def first_block(x, ffn1_norm, ffn1_w_gu, ffn1_w_down, mix_norm, w_in,
              a_q_norm, a_k_norm, b_q_norm, b_k_norm,
              b_lambda_q1, b_lambda_k1, b_lambda_q2, b_lambda_k2, b_subln,
              w_out, ffn2_norm, ffn2_w_gu, ffn2_w_down, out_norm):
    b, s, _ = x.shape
    rows = s // GRID_W
    row_pos = jnp.broadcast_to(jnp.arange(rows, dtype=jnp.float32)[:, None], (rows, GRID_W)).reshape(-1)
    col_pos = jnp.broadcast_to(jnp.arange(GRID_W, dtype=jnp.float32)[None, :], (rows, GRID_W)).reshape(-1)
    lin_pos = jnp.arange(s, dtype=jnp.float32)
    row_cs = _rope_table(row_pos, AXIAL_DIM, A_ROPE_THETA)
    col_cs = _rope_table(col_pos, AXIAL_DIM, A_ROPE_THETA)
    part_cs = _rope_table(lin_pos, PARTIAL_ROPE_DIM, PARTIAL_ROPE_THETA)

    for l in range(DEPTH):
        x = x + 0.5 * _swiglu(_rms_norm(x, ffn1_norm[l]), ffn1_w_gu[l], ffn1_w_down[l])

        h = _rms_norm(x, mix_norm[l])
        proj = h @ w_in[l]
        i0 = A_Q; i1 = i0 + A_KV; i2 = i1 + A_KV; i3 = i2 + B_QK; i4 = i3 + B_QK
        qa = proj[..., :i0].reshape(b, s, A_HEADS, HEAD_DIM)
        ka = proj[..., i0:i1].reshape(b, s, A_KV_HEADS, HEAD_DIM)
        va = proj[..., i1:i2].reshape(b, s, A_KV_HEADS, HEAD_DIM)
        qd = proj[..., i2:i3].reshape(b, s, B_HEADS, 2, HEAD_DIM)
        kd = proj[..., i3:i4].reshape(b, s, B_HEADS, 2, HEAD_DIM)
        vd = proj[..., i4:].reshape(b, s, B_HEADS, B_VDIM)

        qa = _axial_rope(_rms_norm(qa, a_q_norm[l]), row_cs, col_cs)
        ka = _axial_rope(_rms_norm(ka, a_k_norm[l]), row_cs, col_cs)
        out_a = _gqa_axial(qa, ka, va)

        qd = _partial_rope(_rms_norm(qd, b_q_norm[l]), part_cs)
        kd = _partial_rope(_rms_norm(kd, b_k_norm[l]), part_cs)
        lambda_init = 0.8 - 0.6 * math.exp(-0.3 * l)
        lam = (jnp.exp(jnp.sum(b_lambda_q1[l].astype(jnp.float32) * b_lambda_k1[l].astype(jnp.float32)))
               - jnp.exp(jnp.sum(b_lambda_q2[l].astype(jnp.float32) * b_lambda_k2[l].astype(jnp.float32)))
               + lambda_init)
        out_b = _diff_attention(qd, kd, vd, lam, lambda_init, b_subln[l])

        x = x + jnp.concatenate([out_a, out_b], axis=-1) @ w_out[l]

        x = x + 0.5 * _swiglu(_rms_norm(x, ffn2_norm[l]), ffn2_w_gu[l], ffn2_w_down[l])

        x = _rms_norm(x, out_norm[l])
    return x


DEPTH_2 = 2

CTX_LEN = 256

POOL_WIDTH = D_MODEL // 4
CONV_WIDTH = D_MODEL // 4
NA_WIDTH = D_MODEL - POOL_WIDTH - CONV_WIDTH
MIX_WIDTH = POOL_WIDTH + NA_WIDTH + CONV_WIDTH
POOL_WINDOWS = (2, 4, 8, 16)
POOL_GROUP = POOL_WIDTH // len(POOL_WINDOWS)
NA_HEAD_DIM = 64
NA_HEADS = NA_WIDTH // NA_HEAD_DIM
NA_KH = 8
NA_KW = 16
ROPE_THETA = 10000.0
CONV_K = 31
NORM_EPS = 1e-6
LN_EPS = 1e-5

OFF_A_V = 0
OFF_A_G = OFF_A_V + POOL_WIDTH
OFF_B_Q = OFF_A_G + POOL_WIDTH
OFF_B_K = OFF_B_Q + NA_WIDTH
OFF_B_V = OFF_B_K + NA_WIDTH
OFF_B_G = OFF_B_V + NA_WIDTH
OFF_C_U = OFF_B_G + NA_WIDTH
OFF_C_G = OFF_C_U + 2 * CONV_WIDTH
PROJ_WIDTH = OFF_C_G + CONV_WIDTH


def rms_norm(x, g):
    xf = x.astype(jnp.float32)
    y = xf * lax.rsqrt(jnp.mean(xf * xf, axis=-1, keepdims=True) + NORM_EPS)
    return (y * g.astype(jnp.float32)).astype(x.dtype)

def to_heads(t):
    return t.reshape(t.shape[:-1] + (NA_HEADS, NA_HEAD_DIM))

def axial_rope(x, rows_pos, cols_pos):
    half = x.shape[-1] // 2
    freqs = ROPE_THETA ** (-jnp.arange(0, half, 2, dtype=jnp.float32) / half)

    def rot(xp, pos):
        ang = pos.astype(jnp.float32)[:, None] * freqs[None, :]
        cos = jnp.cos(ang)[None, :, None, :]
        sin = jnp.sin(ang)[None, :, None, :]
        xf = xp.astype(jnp.float32)
        x1, x2 = xf[..., : half // 2], xf[..., half // 2:]
        return jnp.concatenate([x1 * cos - x2 * sin, x1 * sin + x2 * cos], axis=-1)

    out = jnp.concatenate([rot(x[..., :half], rows_pos), rot(x[..., half:], cols_pos)], axis=-1)
    return out.astype(x.dtype)

def multiscale_pool(u, w_pool, pool_scale):
    B, L, _ = u.shape
    uf = u.astype(jnp.float32)
    cs = jnp.concatenate([jnp.zeros((B, 1, POOL_WIDTH), jnp.float32), jnp.cumsum(uf, axis=1)], axis=1)
    t = jnp.arange(L)
    means = []
    for g, w in enumerate(POOL_WINDOWS):
        lo = jnp.clip(t - w // 2, 0, L - 1)
        hi = jnp.clip(t + (w - w // 2) - 1, 0, L - 1)
        seg = cs[..., g * POOL_GROUP:(g + 1) * POOL_GROUP]
        total = jnp.take(seg, hi + 1, axis=1) - jnp.take(seg, lo, axis=1)
        means.append(total / (hi - lo + 1).astype(jnp.float32)[None, :, None])
    pooled = (jnp.concatenate(means, axis=-1) - uf).astype(u.dtype)
    y = jnp.einsum('blgc,gcd->blgd', pooled.reshape(B, L, len(POOL_WINDOWS), POOL_GROUP), w_pool)
    return y.reshape(B, L, POOL_WIDTH) * pool_scale

def neighbourhood_attention(q, k, v, kc, vc, rpb):
    B, L, H, hd = q.shape
    rows = L // GRID_W
    kh = min(NA_KH, rows)
    scale = hd ** -0.5
    qg = jnp.moveaxis((q * scale).reshape(B, rows, GRID_W, H, hd), 1, 0)
    kg = k.reshape(B, rows, GRID_W, H, hd)
    vg = v.reshape(B, rows, GRID_W, H, hd)
    kc_s = kc
    col = np.arange(GRID_W)
    col_start = np.clip(col - NA_KW // 2, 0, GRID_W - NA_KW)
    col_idx = col_start[:, None] + np.arange(NA_KW)[None, :]
    dc_idx = col_idx - col[:, None] + NA_KW - 1
    n_loc = kh * NA_KW

    def one_row(args):
        r, q_r = args
        rs = jnp.clip(r - kh // 2, 0, rows - kh)
        k_rows = lax.dynamic_slice_in_dim(kg, rs, kh, axis=1)
        v_rows = lax.dynamic_slice_in_dim(vg, rs, kh, axis=1)
        k_win = k_rows[:, :, col_idx]
        v_win = v_rows[:, :, col_idx]
        dr_idx = rs + jnp.arange(kh) - r + NA_KH - 1
        bias = rpb[:, dr_idx[None, :, None], dc_idx[:, None, :]]
        s_loc = jnp.einsum('bwhd,bawkhd->bhwak', q_r, k_win).astype(jnp.float32) + bias[None].astype(jnp.float32)
        s_ctx = jnp.einsum('bwhd,bchd->bhwc', q_r, kc_s).astype(jnp.float32)
        s = jnp.concatenate([s_loc.reshape(B, H, GRID_W, n_loc), s_ctx], axis=-1)
        p = jax.nn.softmax(s, axis=-1).astype(v.dtype)
        p_loc = p[..., :n_loc].reshape(B, H, GRID_W, kh, NA_KW)
        p_ctx = p[..., n_loc:]
        return (jnp.einsum('bhwak,bawkhd->bwhd', p_loc, v_win)
                + jnp.einsum('bhwc,bchd->bwhd', p_ctx, vc))

    out = lax.map(one_row, (jnp.arange(rows), qg))
    return jnp.moveaxis(out, 0, 1).reshape(B, L, H * hd)

def context_attention(qc, kc, vc):
    B, Lc, H, hd = qc.shape
    s = jnp.einsum('bqhd,bchd->bhqc', qc * (hd ** -0.5), kc).astype(jnp.float32)
    p = jax.nn.softmax(s, axis=-1).astype(vc.dtype)
    return jnp.einsum('bhqc,bchd->bqhd', p, vc).reshape(B, Lc, H * hd)

def conformer_conv(u, conv_dw, conv_dw_b, ln_g, ln_b, conv_pw, conv_pw_b):
    y = u[..., :CONV_WIDTH] * jax.nn.sigmoid(u[..., CONV_WIDTH:])
    y = lax.conv_general_dilated(
        y, conv_dw[:, None, :], window_strides=(1,),
        padding=((CONV_K // 2, CONV_K // 2),),
        dimension_numbers=('NWC', 'WIO', 'NWC'),
        feature_group_count=CONV_WIDTH) + conv_dw_b
    yf = y.astype(jnp.float32)
    mu = jnp.mean(yf, axis=-1, keepdims=True)
    var = jnp.mean(jnp.square(yf - mu), axis=-1, keepdims=True)
    yn = ((yf - mu) * lax.rsqrt(var + LN_EPS) * ln_g.astype(jnp.float32) + ln_b.astype(jnp.float32)).astype(y.dtype)
    return jax.nn.silu(yn) @ conv_pw + conv_pw_b

def mix_out(p, na_out, w_pool, pool_scale, conv_dw, conv_dw_b, conv_ln_g, conv_ln_b, conv_pw, conv_pw_b, w_out):
    ya = multiscale_pool(p[..., OFF_A_V:OFF_A_G], w_pool, pool_scale) * jax.nn.silu(p[..., OFF_A_G:OFF_B_Q])
    yb = na_out * jax.nn.silu(p[..., OFF_B_G:OFF_C_U])
    yc = conformer_conv(p[..., OFF_C_U:OFF_C_G], conv_dw, conv_dw_b, conv_ln_g, conv_ln_b,
                        conv_pw, conv_pw_b) * jax.nn.silu(p[..., OFF_C_G:PROJ_WIDTH])
    return jnp.concatenate([ya, yb, yc], axis=-1) @ w_out

def hybrid_layer(x, xc, c_act, cc_act, w_mod, b_mod, norm_g, w_in, w_pool, pool_scale, na_rpb,
                 conv_dw, conv_dw_b, conv_ln_g, conv_ln_b, conv_pw, conv_pw_b, w_out,
                 rows_pos, cols_pos, update_ctx):
    shift, scale, gate = jnp.split(c_act @ w_mod + b_mod, 3, axis=-1)
    shift_c, scale_c, gate_c = jnp.split(cc_act @ w_mod + b_mod, 3, axis=-1)

    hc = rms_norm(xc, norm_g) * (1 + scale_c) + shift_c
    if update_ctx:
        pc = hc @ w_in
        kv_c = pc[..., OFF_B_K:OFF_B_G]
    else:
        kv_c = hc @ w_in[:, OFF_B_K:OFF_B_G]
    kc = to_heads(kv_c[..., :NA_WIDTH])
    vc = to_heads(kv_c[..., NA_WIDTH:])

    h = rms_norm(x, norm_g) * (1 + scale[:, None, :]) + shift[:, None, :]
    p = h @ w_in
    q = axial_rope(to_heads(p[..., OFF_B_Q:OFF_B_K]), rows_pos, cols_pos)
    k = axial_rope(to_heads(p[..., OFF_B_K:OFF_B_V]), rows_pos, cols_pos)
    v = to_heads(p[..., OFF_B_V:OFF_B_G])
    na_lat = neighbourhood_attention(q, k, v, kc, vc, na_rpb)
    x_new = x + gate[:, None, :] * mix_out(p, na_lat, w_pool, pool_scale, conv_dw, conv_dw_b,
                                           conv_ln_g, conv_ln_b, conv_pw, conv_pw_b, w_out)
    if update_ctx:
        qc = to_heads(pc[..., OFF_B_Q:OFF_B_K])
        na_c = context_attention(qc, kc, vc)
        xc = xc + gate_c * mix_out(pc, na_c, w_pool, pool_scale, conv_dw, conv_dw_b,
                                   conv_ln_g, conv_ln_b, conv_pw, conv_pw_b, w_out)
    return x_new, xc

def second_inputs(seed: int = 0) -> dict:
    key = jax.random.key(seed)
    ks = jax.random.split(key, 24)
    f32 = jnp.float32
    nrm = lambda k, shape, s: jax.random.normal(k, shape, f32) * s
    return {
        "x": nrm(ks[0], (BATCH, SEQ, D_MODEL), 1.0),
        "c": nrm(ks[1], (BATCH, D_MODEL), 1.0),
        "ctx": nrm(ks[2], (BATCH, CTX_LEN, D_MODEL), 1.0),
        "c_ctx": nrm(ks[3], (D_MODEL,), 1.0),
        "w_mod": nrm(ks[4], (DEPTH_2, D_MODEL, 3 * D_MODEL), 0.5 * D_MODEL ** -0.5),
        "b_mod": nrm(ks[5], (DEPTH_2, 3 * D_MODEL), 0.01),
        "norm_g": 1.0 + nrm(ks[6], (DEPTH_2, D_MODEL), 0.02),
        "w_in": nrm(ks[7], (DEPTH_2, D_MODEL, PROJ_WIDTH), D_MODEL ** -0.5),
        "w_pool": nrm(ks[8], (DEPTH_2, len(POOL_WINDOWS), POOL_GROUP, POOL_GROUP), POOL_GROUP ** -0.5),
        "pool_scale": 1.0 + nrm(ks[9], (DEPTH_2, POOL_WIDTH), 0.1),
        "na_rpb": nrm(ks[10], (DEPTH_2, NA_HEADS, 2 * NA_KH - 1, 2 * NA_KW - 1), 0.1),
        "conv_dw": nrm(ks[11], (DEPTH_2, CONV_K, CONV_WIDTH), CONV_K ** -0.5),
        "conv_dw_b": nrm(ks[12], (DEPTH_2, CONV_WIDTH), 0.01),
        "conv_ln_g": 1.0 + nrm(ks[13], (DEPTH_2, CONV_WIDTH), 0.02),
        "conv_ln_b": nrm(ks[14], (DEPTH_2, CONV_WIDTH), 0.01),
        "conv_pw": nrm(ks[15], (DEPTH_2, CONV_WIDTH, CONV_WIDTH), CONV_WIDTH ** -0.5),
        "conv_pw_b": nrm(ks[16], (DEPTH_2, CONV_WIDTH), 0.01),
        "w_out": nrm(ks[17], (DEPTH_2, MIX_WIDTH, D_MODEL), MIX_WIDTH ** -0.5),
        "final_norm_g": 1.0 + nrm(ks[18], (D_MODEL,), 0.02),
    }

def second_block(x, c, ctx, c_ctx, w_mod, b_mod, norm_g, w_in, w_pool, pool_scale, na_rpb,
              conv_dw, conv_dw_b, conv_ln_g, conv_ln_b, conv_pw, conv_pw_b, w_out, final_norm_g):
    L = x.shape[1]
    t = jnp.arange(L)
    rows_pos = t // GRID_W
    cols_pos = t % GRID_W
    c_act = jax.nn.silu(c)
    cc_act = jax.nn.silu(c_ctx)
    xc = ctx
    for i in range(DEPTH_2):
        x, xc = hybrid_layer(
            x, xc, c_act, cc_act, w_mod[i], b_mod[i], norm_g[i], w_in[i], w_pool[i], pool_scale[i],
            na_rpb[i], conv_dw[i], conv_dw_b[i], conv_ln_g[i], conv_ln_b[i], conv_pw[i], conv_pw_b[i],
            w_out[i], rows_pos, cols_pos, i < DEPTH_2 - 1)
    return rms_norm(x, final_norm_g)


def setup_inputs(seed=0):
    out = dict(first_inputs(seed))
    for name, value in second_inputs(seed + 1).items():
        if name != "x":
            out[name + "_2"] = value
    return out


def reference(
    x, ffn1_norm, ffn1_w_gu, ffn1_w_down, mix_norm, w_in, a_q_norm, a_k_norm, b_q_norm,
    b_k_norm, b_lambda_q1, b_lambda_k1, b_lambda_q2, b_lambda_k2, b_subln, w_out, ffn2_norm,
    ffn2_w_gu, ffn2_w_down, out_norm, c_2, ctx_2, c_ctx_2, w_mod_2, b_mod_2, norm_g_2, w_in_2,
    w_pool_2, pool_scale_2, na_rpb_2, conv_dw_2, conv_dw_b_2, conv_ln_g_2, conv_ln_b_2,
    conv_pw_2, conv_pw_b_2, w_out_2, final_norm_g_2,
):
    x = first_block(
        x, ffn1_norm, ffn1_w_gu, ffn1_w_down, mix_norm, w_in, a_q_norm, a_k_norm, b_q_norm,
        b_k_norm, b_lambda_q1, b_lambda_k1, b_lambda_q2, b_lambda_k2, b_subln, w_out, ffn2_norm,
        ffn2_w_gu, ffn2_w_down, out_norm,
    )
    return second_block(
        x, c_2, ctx_2, c_ctx_2, w_mod_2, b_mod_2, norm_g_2, w_in_2, w_pool_2, pool_scale_2,
        na_rpb_2, conv_dw_2, conv_dw_b_2, conv_ln_g_2, conv_ln_b_2, conv_pw_2, conv_pw_b_2,
        w_out_2, final_norm_g_2,
    )


_drawn_inputs = setup_inputs


def setup_inputs(seed=0):
    import zlib

    import numpy as np

    out = dict(_drawn_inputs(seed))
    spreads = {}
    factors = {'ffn1_norm': 5.081,
     'mix_norm': 3.025,
     'a_q_norm': 8.0,
     'a_k_norm': 8.0,
     'b_q_norm': 4.934,
     'b_k_norm': 4.578,
     'b_subln': 5.887,
     'ffn2_norm': 8.0,
     'out_norm': 2.875,
     'ctx_2': 2.794,
     'b_mod_2': 8.0,
     'norm_g_2': 8.0,
     'pool_scale_2': 4.243,
     'na_rpb_2': 24.703,
     'conv_dw_b_2': 57.762,
     'conv_ln_g_2': 42.021,
     'conv_ln_b_2': 64.0,
     'conv_pw_b_2': 60.247,
     'final_norm_g_2': 21.201}
    for name, (base, spread) in spreads.items():
        noise = np.random.default_rng([zlib.crc32(name.encode()), seed]).standard_normal(out[name].shape)
        drawn = base * np.exp(spread * noise) if base else spread * noise
        out[name] = __import__('jax').numpy.asarray(drawn.astype(out[name].dtype))
    for name, factor in factors.items():
        out[name] = (out[name] * factor).astype(out[name].dtype)
    return out
```

```python
from contextlib import ExitStack

import numpy as np

import concourse.bass as bass
from concourse import mybir

F32 = mybir.dt.float32
F32R = mybir.dt.float32r
ACT = mybir.ActivationFunctionType
ALU = mybir.AluOpType
AX = mybir.AxisListType.X

P = 128
D = 2048
KT = D // P
L = 256
CH = 512
DFF = 5632
FT = DFF // P
EPS = 1e-6
LN_EPS = 1e-5
HD = 128
A_HEADS, A_KV, B_HEADS = 8, 2, 4
B_COL = (A_HEADS + 2 * A_KV) * HD
VA_COL = (A_HEADS + A_KV) * HD
VD_COL = B_COL + 4 * B_HEADS * HD
D_IN = VD_COL + 2 * B_HEADS * HD
SCALE = HD ** -0.5
LAMBDA_INIT = 0.2
NA_H, NA_D = 16, 64
GRID = 64
RPB_R, RPB_C = 15, 31
TAPS = 31
PAD = TAPS // 2
YW = L + TAPS
POOLS = (2, 4, 8, 16)
PROJ2 = 6656
RING = 4


def rope_tables():
    t = np.arange(L, dtype=np.float32)
    rows, cols = np.floor(t / GRID).astype(np.float32), (t % GRID).astype(np.float32)

    def table(pos, dim, theta):
        f = np.float32(theta) ** (-np.arange(0, dim, 2, dtype=np.float32) / np.float32(dim))
        a = (pos[:, None] * f[None, :]).astype(np.float32)
        return np.concatenate([np.cos(a), np.cos(a)], 1), np.concatenate([-np.sin(a), np.sin(a)], 1)

    def pair(dim):
        r, c = table(rows, dim, 10000.0), table(cols, dim, 10000.0)
        return [np.concatenate([r[k], c[k]], 1) for k in range(2)]

    a = pair(64)
    b = table(t, 32, 500000.0)
    n = [np.tile(m, (1, 2)) for m in pair(32)]
    return [m.astype(np.float32) for m in (*a, *b, *n)]


def pool_matrices():
    m = np.zeros((len(POOLS), L, L), np.float32)
    for g, w in enumerate(POOLS):
        for t in range(L):
            lo, hi = max(t - w // 2, 0), min(t + (w - w // 2) - 1, L - 1)
            m[g, lo:hi + 1, t] = np.float32(1.0) / np.float32(hi - lo + 1)
            m[g, t, t] -= np.float32(1.0)
    return m.reshape(len(POOLS), 2, P, L).transpose(2, 1, 0, 3).copy()


def window_mask():
    q = np.arange(GRID)
    start = np.clip(q - 8, 0, GRID - 16)
    k = np.arange(GRID)[None, :]
    inside = (k >= start[:, None]) & (k < start[:, None] + 16)
    return np.tile(np.where(inside, 0.0, -1e30).astype(np.float32)[::-1], (2, 1))


class Phase:

    def __init__(self, pieces, taken, groups):
        self.pieces, self.taken, self.groups = pieces, taken, groups


def build(nc, a, out, xs_dram):
    ctx = ExitStack()
    with ctx:
        sem_names = """raw0 raw1 raw2 raw3 hi_made lo_made pieces_used acc_done acc_taken tp_done tg_full
            tg_hi tg_lo ss_made var_made sd_made scaled const_in cols_made cols_taken gate_act u_made
            dve_step act_step pool_step x_in rope_in roped qk_ss qk_sd cg_done cg_taken s_done m_ready p_made
            pn_made o_done o_taken lam_e ob_made x4_in xs_out ctx_in mod0 mod1 mod2 mod3 mod_used row_done
            row_taken mt_done mt_taken silu_c ca_const_in glu_made gates_made yt_done yt_taken pl_done
            pl_taken py_done py_taken pad_made conv_step cf_in cf_done z_made cz_done s_made pw_done
            yc_made na_in bias_in bias_ready  st_dve st_act pt_done pt_taken gs_done
            gs_taken x4r_in fin_in y_out brow_in rs_made cf_sd cf_b
            tmp_made y_made""".split()
        S = {n: ctx.enter_context(nc.semaphore(n)) for n in sem_names}
        base = (nc.sbuf_base + 63) // 64 * 64
        top = [base]

        def at(name, offset, shape, dt=F32):
            top[0] = max(top[0], base + offset + 4 * int(np.prod(shape[1:])))
            return nc.alloc_sbuf_tensor_at(name, shape, dt, offset=base + offset)

        K1 = 1024
        raw = at("raw", 0, [P, RING, 2 * CH])
        hi = at("hi", 16 * K1, [P, RING, CH], F32R)
        lo = at("lo", 24 * K1, [P, RING, CH], F32R)
        H = 32 * K1
        Q = 96 * K1
        h1 = [at("h1_hi", H, [P, KT, L], F32R), at("h1_lo", H + 16 * K1, [P, KT, L], F32R)]
        x1 = at("x1", H + 32 * K1, [P, 2, D])
        ns1 = at("ns1", H + 48 * K1, [P, 2, D])
        uT = [at("uT_hi", Q, [P, FT, L], F32R), at("uT_lo", Q + 44 * K1, [P, FT, L], F32R)]
        ub = at("ub", Q + 88 * K1, [P, 2, CH])
        tm1 = at("tm1", Q + 92 * K1, [P, 2, CH])
        proj = at("proj", Q, [P, 2, D_IN])
        qkT = at("qkT", Q + 36 * K1, [P, 26, L])
        rt = at("rt", Q + 62 * K1, [P, 2, 2048])
        pr1 = at("pr1", Q + 78 * K1, [P, 2, 2, L])
        pt1 = at("pt1", Q + 82 * K1, [P, 2, 2, L])
        ob = at("ob", Q + 86 * K1, [P, 2, L])
        ropa = at("ropa", Q + 96 * K1, [P, 2, 2, P])
        ropb = at("ropb", Q + 98 * K1, [P, 2, 2, 32])
        gbc = at("gbc", Q + 99 * K1, [P, 4, P])
        lamv = at("lamv", Q + 101 * K1, [P, 4, P])
        sub_bc = at("sub_bc", Q + 103 * K1, [P, L])
        ogain = at("ogain", Q + 64 * K1, [P, D])
        hT = [at("hT_hi", H, [P, KT, 2 * L], F32R), at("hT_lo", H + 32 * K1, [P, KT, 2 * L], F32R)]
        x4 = at("x4", Q, [P, 4, D])
        tm2 = at("tm2", Q + 32 * K1, [P, 2, CH])
        ns2 = at("ns2", Q + 40 * K1, [P, 2, D])
        modr = at("modr", Q + 32 * K1, [P, 4, 4, CH])
        qkvg = at("qkvg", Q, [P, 8, 4, CH])
        ca = at("ca", Q, [P, 5, 4, CH])
        pmat = at("pmat", Q + 40 * K1, [P, 2, 4, L])
        wpool = at("wpool", Q + 48 * K1, [P, 4, P])
        psc = at("psc", Q + 50 * K1, [P, CH])
        pdT = at("pdT", Q + 52 * K1, [P, 4, 2 * L])
        gatb = at("gatb", Q + 48 * K1, [P, 2, D])
        fgain = at("fgain", Q + 32 * K1, [P, D])
        yT = at("yT", Q + 64 * K1, [P, 4, 2, YW])
        cv = at("cv", Q + 73 * K1, [P, 4, 2 * L])
        ya = at("ya", Q + 83 * K1, [P, 4, CH])
        gC = at("gC", Q + 91 * K1, [P, 4, CH])
        grow = at("grow", Q + 99 * K1, [2, D])
        rowb = at("rowb", Q + 81 * K1, [2, CH])
        selr = at("selr", Q + 81 * K1, [2, 2, P])
        st = at("st", H, [P, 8, P])
        T = at("T", H + 4 * K1, [P, 2 * CH])
        pr = at("pr", H + 8 * K1, [P, 2, CH])
        pt = at("pt", H + 12 * K1, [P, 2, CH])
        ropn = at("ropn", H + 16 * K1, [P, 2, 2, P])
        rn = at("rn", H + 18 * K1, [P, 2, 2, P])
        mask = at("mask", H + 20 * K1, [P, GRID])
        turn = at("turn", H + 20 * K1 + 256, [P, P])
        zb = at("zb", H + 32 * K1, [P, 2, CH])
        sT = at("sT", H + 36 * K1, [P, 2, CH])
        cpw = at("cpw", H + 24 * K1, [P, 4, CH])
        cpb = at("cpb", H + 22 * K1, [1, CH])
        bias = at("bias", H + 40 * K1, [P, NA_H, 6 * GRID])
        small = [Q + 107 * K1]

        def keep(name, shape):
            t = at(name, small[0], shape)
            small[0] += (4 * int(np.prod(shape[1:])) + 31) // 32 * 32
            return t

        ident = keep("ident", [P, P])
        NV = 5 * KT + 2 * KT
        vec = keep("vec", [P, NV])
        bmod = keep("bmod", [P, 96])
        cvec = keep("cvec", [P, 24])
        dw = keep("dw", [P, 2, 128])
        cT = keep("cT", [P, KT, 2])
        modT = keep("modT", [P, 32, 2])
        mA = keep("mA", [P, 2, KT])
        mB = keep("mB", [P, 2, KT])
        ss = keep("ss", [P, 4])
        rs = keep("rs", [P, 4])
        sd = keep("sd", [P, 4])
        qss = keep("qss", [P, 2, 26])
        qsd = keep("qsd", [P, 2, 26])
        lam = keep("lam", [P, 8])
        mx = keep("mx", [P, 2, 2])
        nm = keep("nm", [P, 2, 2])
        sm = keep("sm", [P, 2, 2])
        rr = keep("rr", [P, 2, 2])
        bn = keep("bn", [P, 6])
        mv = keep("mv", [P, 4])
        ones = keep("ones", [1, P])
        vrow = at("vrow", Q, [NV, P])
        brow = at("brow", Q + 512, [120, P])
        drow = at("drow", Q + 1024, [124, 2, P])
        assert top[0] <= nc.sbuf_usable_end, top[0] - nc.sbuf_usable_end

        acc = [ctx.enter_context(nc.psum_tensor(f"acc{i}", [P, CH], F32)) for i in range(4)]
        tp = [ctx.enter_context(nc.psum_tensor(f"tp{i}", [P, CH], F32)) for i in range(2)]
        cg = [ctx.enter_context(nc.psum_tensor(f"cg{i}", [P, CH], F32)) for i in range(2)]

        phases = {}
        total = [0, 0, 0]

        def phase(name, pieces, taken, groups):
            phases[name] = Phase(*total)
            for k, n in enumerate((pieces, taken, groups)):
                total[k] += n

        FC = DFF // CH
        phase("n1", 0, 0, 8)
        phase("g1", FC * 32, FC * 2, 2 * FC)
        phase("d1", 2 * 88, 8, 0)
        phase("n2", 0, 0, 8)
        phase("i1", 9 * 16, 18, 0)
        phase("at1", 0, 0, A_HEADS + B_HEADS)
        phase("o1", 4 * 16, 8, 0)
        phase("n3", 0, 0, 8)
        phase("g2", FC * 32, FC * 2, 2 * FC)
        phase("d2", 2 * 88, 8, 0)
        SEGS = [[("a", 0, 8, 4)], [("q", 0, 2, 2), ("kv", 2, 4, 4), ("g", 6, 2, 2)]]
        NT = [4, 2]
        for ly in range(2):
            phase(f"n4{ly}", 0, 0, 16)
            phase(f"ca{ly}", 5 * 16, 5 * NT[ly], 0)
            for nm_, _, n, nt in SEGS[ly]:
                phase(f"s{ly}{nm_}", n * 16, n * nt, 0)
            phase(f"mx{ly}", 0, 0, 4 * NT[ly])
            phase(f"o2{ly}", 4 * 16, 4 * NT[ly], 0)
        phase("end", 0, 0, 0)
        PIECES = total[0]

        class Link:

            def __init__(self, eng, sem):
                self.eng, self.sem, self.n, self.lap, self.per = eng, sem, 0, None, 0

            def __call__(self, ins):
                self.n += 1
                ins.then_inc(self.sem, 1)
                self.eng.wait_ge(self.sem, self.n if self.lap is None else self.n + self.lap * self.per)

            def start(self, lap, per):
                self.lap, self.per, self.was = lap, per, self.n

            def stop(self, laps):
                assert self.n - self.was == self.per, (self.n - self.was, self.per)
                self.n += self.per * (laps - 1)
                self.lap = None

        def wait(eng, name, value):
            if not isinstance(value, int) or value > 0:
                eng.wait_ge(S[name], value)

        def place(j):
            m, q = divmod(j, 4)
            return 2 * m + q % 2, q // 2

        def raw_piece(j):
            u, half = place(j)
            return raw[:, u % RING, half * CH:(half + 1) * CH]

        def hi_piece(act, p0, j):
            u, half = place(j)
            if half == 0:
                loads = (p0 // 8 + j // 8 + 1) * 16 if isinstance(p0, int) else \
                    At(p0.base // 8 * 16 + j // 8 * 16 + 16, p0.per * 2, p0.lap).value()
                act.wait_ge(S[f"raw{u % RING}"], loads)
            wait(act, "pieces_used", num(p0 + (j - RING + 1)))
            act.activation(hi[:, j % RING, :], raw_piece(j), ACT.Copy).then_inc(S["hi_made"], 1)

        def lo_piece(dve, p0, j):
            wait(dve, "hi_made", num(p0 + (j + 1)))
            dve.tensor_tensor(lo[:, j % RING, :], raw_piece(j), hi[:, j % RING, :].bitcast(F32),
                              ALU.subtract).then_inc(S["lo_made"], 1)

        class At:

            def __init__(self, base, per, lap):
                self.base, self.per, self.lap = base, per, lap

            def __add__(self, n):
                return At(self.base + n, self.per, self.lap)

            def __sub__(self, n):
                return At(self.base - n, self.per, self.lap)

            def value(self):
                return self.lap * self.per + self.base

        def num(v):
            return v.value() if isinstance(v, At) else v

        def mm3(pe, bank, act_hi, act_lo, slot, start, stop):
            pe.matmul(bank, act_hi, hi[:, slot, :], start=start, stop=False)
            pe.matmul(bank, act_lo, hi[:, slot, :], start=False, stop=False)
            return pe.matmul(bank, act_hi, lo[:, slot, :], start=False, stop=stop)

        def chunk_pieces(pe, src, nt, p0, taken, js):
            for j in js:
                u, half = place(j)
                kt = 2 * u + half
                pe.wait_ge(S["lo_made"], num(p0 + (j + 1)))
                for t in range(nt):
                    if j == 0:
                        wait(pe, "acc_taken", num(taken + (t + 1 - nt)))
                    last = mm3(pe, acc[t][:], src[0][:, kt, t * P:(t + 1) * P], src[1][:, kt, t * P:(t + 1) * P],
                               j % RING, j == 0, j == 15)
                    if j == 15 and t < nt - 1:
                        last.then_inc(S["acc_done"], 1)
                last.then_inc(S["pieces_used"], 1)

        def pair_pieces(pe, src, nk, p0, js, bank_free):
            for j in js:
                kt, half = place(j)
                pe.wait_ge(S["lo_made"], num(p0 + (j + 1)))
                for t in range(2):
                    if kt == 0:
                        bank_free(half, t)
                    last = mm3(pe, acc[2 * half + t][:], src[0][:, kt, t * P:(t + 1) * P],
                               src[1][:, kt, t * P:(t + 1) * P], j % RING, kt == 0, kt == nk - 1)
                    if kt == nk - 1 and t == 0:
                        last.then_inc(S["acc_done"], 1)
                last.then_inc(S["pieces_used"], 1)

        def pair_done(eng, ph, per, lap, half, t):
            if t == 0:
                eng.wait_ge(S["acc_done"], num(lap_at(ph.done + half + 1, 2, lap)))
            else:
                eng.wait_ge(S["pieces_used"], num(lap_at(ph.pieces + per - 2 + 2 * half, per, lap)))

        def lap_at(b, per, lap):
            return b + per * lap if isinstance(lap, int) else At(b, per, lap)

        def bank_done(eng, ph, nt, lap, t):
            if t < nt - 1:
                eng.wait_ge(S["acc_done"], num(lap_at(ph.done + t + 1, nt - 1, lap)))
            else:
                eng.wait_ge(S["pieces_used"], num(lap_at(ph.pieces + 16, 16, lap)))

        def turned(ph):
            return ph.groups - (A_HEADS if ph.groups > phases["at1"].groups else 0)

        n = 0
        for name in phases:
            phases[name].done = n
            if name[0] == "i" or name == "o1":
                n += {"i": 9, "o": 4}[name[0]]
            if name[0] in "gd":
                n += 2 * {"g": FC, "d": 2}[name[0]]
            if name[:2] == "ca":
                n += 5 * (NT[int(name[2])] - 1)
            if name[0] == "s":
                seg = [s for s in SEGS[int(name[1])] if s[0] == name[2:]][0]
                n += seg[2] * (seg[3] - 1)
            if name[:2] == "o2":
                n += 4 * (NT[int(name[2])] - 1)

        def gu_view(w):
            return w.rearrange("o (k p) (g c n) -> o c k p g n", p=P, g=2, n=CH)[0]

        def down_view(w):
            return w.rearrange("o (k p) (c n) -> o c k p n", p=P, n=2 * CH)[0]

        def wide_view(w, ly):
            return w.rearrange("o (k j p) (c n) -> o c k p j n", j=2, p=P, n=CH)[ly]

        gu = [gu_view(a["ffn1_w_gu"]), gu_view(a["ffn2_w_gu"])]
        down = [down_view(a["ffn1_w_down"]), down_view(a["ffn2_w_down"])]
        win1, wout1 = wide_view(a["w_in"], 0), wide_view(a["w_out"], 0)
        win2 = [wide_view(a["w_in_2"], ly) for ly in range(2)]
        wout2 = [wide_view(a["w_out_2"], ly) for ly in range(2)]
        modv = a["w_mod_2"].rearrange("l (k j p) (c n) -> l c k p j n", j=4, p=P, n=CH)
        bmodv = a["b_mod_2"]
        x_v = a["x"].rearrange("o (t p) d -> p (o t) d", p=P)
        ctx_v = a["ctx_2"].rearrange("o (t p) d -> p (o t) d", p=P)
        xs_v = xs_dram.rearrange("(t p) d -> p t d", p=P)
        out_v = out.rearrange("o (t p) d -> p (o t) d", p=P)

        def row_bc(ap, n):
            return bass.AP(tensor=ap.tensor, offset=ap.offset, ap=[[0, P], [1, n]])

        def o_total(n):
            return B_HEADS + 8 * (6 if n > 0 else 0) + 8 * (4 if n > 1 else 0)

        block = ctx.enter_context(nc.Block())

        @block.sync
        def _(sp):
            def unit(p0, u, src, shape=None):
                wait(sp, "lo_made", num(p0 + (4 * (u // 2) - 5 + u % 2)))
                dst = raw[:, u % RING, :]
                if shape == "wide":
                    dst = dst.rearrange("p (j n) -> p j n", j=2)
                sp.dma_start(dst, src).then_inc(S[f"raw{u % RING}"], 16)

            def load_gu(w, ph):
                for u in range(KT):
                    unit(ph.pieces, u, w[0, u], "wide")
                with sp.Fori(1, FC) as i:
                    for u in range(KT):
                        unit(At(ph.pieces, 32, i), u, w[i, u], "wide")

            def load_down(w, ph):
                with sp.Fori(0, 2) as i:
                    for u in range(FT):
                        unit(At(ph.pieces, 88, i), u, w[i, u])

            def ahead(w, ph, first):
                for u in range(RING):
                    unit(ph.pieces, u, w[first, u], "wide")

            def load_wide(w, ph, first, n, begun=False):
                if begun:
                    for u in range(RING, 8):
                        unit(ph.pieces, u, w[first, u], "wide")
                with sp.Fori(int(begun), n) as i:
                    for u in range(8):
                        unit(At(ph.pieces, 16, i), u, w[i + first, u], "wide")

            sp.dma_start(x1[:], x_v).then_inc(S["x_in"], 16)
            load_gu(gu[0], phases["g1"])
            load_down(down[0], phases["d1"])
            load_wide(win1, phases["i1"], 0, 9)
            load_wide(wout1, phases["o1"], 0, 4)
            load_gu(gu[1], phases["g2"])
            load_down(down[1], phases["d2"])
            for ly in range(2):
                nt = NT[ly]
                ph = phases[f"ca{ly}"]
                ahead(win2[ly], ph, 10)
                wait(sp, "acc_taken", phases[f"n4{ly}"].taken)
                for u in range(4):
                    if ly:
                        sp.wait_ge(S["row_done"], 12)
                    sp.dma_start(modr[:, u, :, :], modv[ly, 0, u]).then_inc(S[f"mod{u}"], 16)
                with sp.Fori(1, 12) as i:
                    for u in range(4):
                        if u < 3:
                            sp.wait_ge(S["mod_used"], i * 3 + (36 * ly + u - 2))
                        else:
                            sp.wait_ge(S["row_done"], i + 12 * ly)
                        sp.dma_start(modr[:, u, :, :], modv[ly, i, u]).then_inc(S[f"mod{u}"], 16)
                wait(sp, "tg_lo", phases[f"ca{ly}"].groups)
                sp.dma_start(pmat[:], a["pmat"]).then_inc(S["ca_const_in"], 16)
                sp.dma_start(wpool[:], a["w_pool_2"][ly].rearrange("g c d -> c g d")).then_inc(S["ca_const_in"], 16)
                sp.dma_start(psc[:], row_bc(a["pool_scale_2"][ly], CH)).then_inc(S["ca_const_in"], 16)
                load_wide(win2[ly], ph, 10, 3, True)
                with sp.Fori(0, 2) as i:
                    for u in range(8):
                        unit(At(ph.pieces + 48, 16, i), u, win2[ly][i, u], "wide")
                for nm_, c0, n_, _ in SEGS[ly]:
                    load_wide(win2[ly], phases[f"s{ly}{nm_}"], c0 + 2, n_)
                ahead(wout2[ly], phases[f"o2{ly}"], 0)
                last = phases[f"mx{ly}"]
                sp.wait_ge(S["pieces_used"], last.pieces)
                sp.dma_start(cpw[:], a["conv_pw_2"][ly].rearrange("(k p) n -> p k n", p=P)).then_inc(S["cf_in"], 16)
                sp.dma_start(cpb[:], a["conv_pw_b_2"][ly:ly + 1, :]).then_inc(S["cf_in"], 16)
                sp.dma_start(selr[:], a["selr"]).then_inc(S["cf_in"], 16)
                sp.dma_start(ropn[:, 0], a["cosn"].rearrange("(t p) n -> p t n", p=P)).then_inc(S["na_in"], 16)
                sp.dma_start(ropn[:, 1], a["sinn"].rearrange("(t p) n -> p t n", p=P)).then_inc(S["na_in"], 16)
                sp.dma_start(mask[:], a["mask"]).then_inc(S["na_in"], 16)
                sp.dma_start(turn[:], a["turn"]).then_inc(S["na_in"], 16)
                rpb = a["na_rpb_2"]
                for r2 in range(2):
                    for dr in range(6):
                        first = ly * NA_H * RPB_R * RPB_C + (5 - r2 + dr) * RPB_C + RPB_C // 2 - (GRID - 1)
                        sp.dma_start(bias[r2 * GRID:(r2 + 1) * GRID, :, dr * GRID:(dr + 1) * GRID],
                                     bass.AP(tensor=rpb.tensor, offset=first,
                                             ap=[[1, GRID], [RPB_R * RPB_C, NA_H], [1, GRID]]))\
                            .then_inc(S["bias_in"], 16)
                sp.wait_ge(S["o_taken"], o_total(ly + 1))
                sp.wait_ge(S["xs_out"], 16 * (ly + 1))
                sp.dma_start(x4[:, 0:2, :], xs_v).then_inc(S["x4r_in"], 16)
                if ly == 0:
                    sp.dma_start(x4[:, 2:4, :], ctx_v).then_inc(S["x4r_in"], 16)
                load_wide(wout2[ly], phases[f"o2{ly}"], 0, 4, True)

        @block.scalar
        def _(act):
            def consts():
                act.dma_start(ident[:], a["ident"]).then_inc(S["const_in"], 16)
                act.dma_start(vrow[:], a["vrows"]).then_inc(S["const_in"], 16)
                act.dma_start(brow[0:96, :], a["b_mod_2"].rearrange("l (k p) -> (l k) p", p=P)).then_inc(S["const_in"], 16)
                for k, nm_ in enumerate(("conv_dw_b_2", "conv_ln_g_2", "conv_ln_b_2")):
                    act.dma_start(brow[96 + 8 * k:104 + 8 * k, :],
                                  a[nm_].rearrange("l (k p) -> (l k) p", p=P)).then_inc(S["const_in"], 16)
                for ly in range(2):
                    act.dma_start(drow[:, ly, :],
                                  a["conv_dw_2"][ly].rearrange("k (c p) -> (k c) p", p=P)).then_inc(S["const_in"], 16)

            def at1_consts():
                act.dma_start(ropa[:, 0], a["cosa"].rearrange("(t p) n -> p t n", p=P)).then_inc(S["rope_in"], 16)
                act.dma_start(ropa[:, 1], a["sina"].rearrange("(t p) n -> p t n", p=P)).then_inc(S["rope_in"], 16)
                act.dma_start(ropb[:, 0], a["cosb"].rearrange("(t p) n -> p t n", p=P)).then_inc(S["rope_in"], 16)
                act.dma_start(ropb[:, 1], a["sinb"].rearrange("(t p) n -> p t n", p=P)).then_inc(S["rope_in"], 16)
                for k, nm_ in enumerate(("a_q_norm", "a_k_norm", "b_q_norm", "b_k_norm")):
                    act.dma_start(gbc[:, k], row_bc(a[nm_], P)).then_inc(S["rope_in"], 16)
                for k, nm_ in enumerate(("b_lambda_q1", "b_lambda_k1", "b_lambda_q2", "b_lambda_k2")):
                    act.dma_start(lamv[:, k], row_bc(a[nm_], P)).then_inc(S["rope_in"], 16)
                act.dma_start(sub_bc[:], row_bc(a["b_subln"], L)).then_inc(S["rope_in"], 16)

            norms = [0, 0]

            def root(src_x, ns, nt, x_ready):
                x_ready()
                for t in range(nt):
                    if t >= 2:
                        act.wait_ge(S["ss_made"], norms[1] + t - 1)
                    act.activation(ns[:, t % 2], src_x[:, t], ACT.Square,
                                   accum_out=ss[:, t:t + 1]).then_inc(S["ss_made"], 1)
                norms[0] += 1
                norms[1] += nt
                act.wait_ge(S["var_made"], norms[0])
                act.activation(sd[:, 0:nt], rs[:, 0:nt], ACT.Sqrt).then_inc(S["sd_made"], 1)
                act.wait_ge(S["rs_made"], norms[0])

            def group_hi(g, dst, src):
                act.wait_ge(S["tg_full"], num(g + 1))
                act.activation(dst, src, ACT.Copy).then_inc(S["tg_hi"], 1)

            def norm(ph, src_x, ns, tm, dst, nt, x_ready):
                root(src_x, ns, nt, x_ready)

                def scale(t):
                    act.activation(ns[:, t % 2], src_x[:, t], ACT.Copy, scale=rs[:, t:t + 1]).then_inc(S["scaled"], 1)
                scale(0)
                scale(1)
                for t in range(nt):
                    for g in range(4):
                        group_hi(ph.groups + 4 * t + g, dst[0][:, 4 * g:4 * g + 4, t * P:(t + 1) * P],
                                 tm[:, g % 2].rearrange("p (k n) -> p k n", n=P))
                    if t + 2 < nt:
                        scale(t + 2)

            def gate_up(ph):
                def u_hi(c, off):
                    for f in range(2):
                        cols = slice(4 * (c + off) + 2 * f, 4 * (c + off) + 2 * f + 2) if isinstance(c, int) else \
                            bass.ds(c * 4 + (4 * off + 2 * f), 2)
                        group_hi(lap_at(ph.groups + 2 * off + f, 2, c), uT[0][:, cols, :],
                                 tm1[:, f].rearrange("p (k n) -> p k n", n=L))

                def silus(c):
                    wait(act, "tp_done", num(lap_at(turned(ph), 2, c)))
                    for t in range(2):
                        pair_done(act, ph, 32, c, 0, t)
                        act.activation(ub[:, t], acc[t][:], ACT.Silu).then_inc(S["gate_act"], 1)

                for j in range(2, 34):
                    hi_piece(act, ph.pieces, j)
                silus(0)
                with act.Fori(1, FC) as i:
                    p0 = At(ph.pieces, 32, i)
                    for j in range(2, 6):
                        hi_piece(act, p0, j)
                    u_hi(i, -1)
                    for j in range(6, 34):
                        hi_piece(act, p0, j)
                    silus(i)
                u_hi(FC - 1, 0)

            def stream(p0_of, laps, per, last=False):
                n_ = laps - 1 if last else laps
                with act.Fori(0, n_) as i:
                    for j in range(2, per + 2):
                        hi_piece(act, At(p0_of, per, i), j)
                if last:
                    for j in range(2, per):
                        hi_piece(act, p0_of + per * n_, j)

            consts()
            at1_consts()
            for j in range(2):
                hi_piece(act, 0, j)
            norm(phases["n1"], x1, ns1, tm1, h1, 2, lambda: act.wait_ge(S["x_in"], 16))
            act.wait_ge(S["cols_taken"], 7)
            act.activation(cT[:].rearrange("p k c -> p c k"), vec[:, 5 * KT:7 * KT].rearrange("p (c k) -> p c k", c=2),
                           ACT.Silu).then_inc(S["silu_c"], 1)
            gate_up(phases["g1"])
            stream(phases["d1"].pieces, 2, 88)
            norm(phases["n2"], x1, ns1, tm1, h1, 2, lambda: act.wait_ge(S["acc_taken"], phases["n2"].taken))
            stream(phases["i1"].pieces, 9, 16)

            g0 = phases["at1"].groups
            act.wait_ge(S["lam_e"], 1)
            act.activation(lam[:, 2:4], lam[:, 0:2], ACT.Exp).then_inc(S["lam_e"], 1)
            act.wait_ge(S["qk_ss"], 1)
            act.activation(qsd[:], qss[:], ACT.Sqrt).then_inc(S["qk_sd"], 1)
            for g in range(13):
                act.wait_ge(S["cg_done"], g + 1)
                act.activation(qkT[:, 2 * g:2 * g + 2, :], cg[g % 2][:].rearrange("p (k n) -> p k n", n=L),
                               ACT.Copy).then_inc(S["cg_taken"], 1)

            def exps(q):
                act.wait_ge(S["m_ready"], q + 1)
                if q >= 2:
                    act.wait_ge(S["cg_done"], 13 + (q - 1 if q - 2 < 8 else 8 + (q - 8) // 2))
                for t in range(2):
                    ins = act.activation(pr1[:, q % 2, t], acc[q % 2][:, t * L:(t + 1) * L], ACT.Exp,
                                         bias=nm[:, q % 2, t:t + 1], scale=SCALE, accum_out=sm[:, q % 2, t:t + 1])
                ins.then_inc(S["p_made"], 1)

            def pt_copy(k):
                act.wait_ge(S["cg_done"], 14 + k)
                if k >= 2:
                    act.wait_ge(S["o_done"], k - 1)
                act.activation(pt1[:, k % 2], cg[(13 + k) % 2][:].rearrange("p (k n) -> p k n", n=L),
                               ACT.Copy).then_inc(S["cg_taken"], 1)

            exps(0)
            for q in range(8):
                exps(q + 1)
                pt_copy(q)
                group_hi(g0 + q, h1[0][:, q, :], tm1[:, q % 2, 0:L])
            for h in range(B_HEADS):
                exps(9 + 2 * h)
                pt_copy(8 + h)
                if h + 1 < B_HEADS:
                    exps(10 + 2 * h)
                act.wait_ge(S["ob_made"], 2 * h + 1)
                act.activation(lam[:, 6:8], lam[:, 4:6], ACT.Sqrt).then_inc(S["qk_sd"], 1)
                group_hi(g0 + 8 + h, h1[0][:, 8 + 2 * h:10 + 2 * h, :], tm1[:, h % 2].rearrange("p (k n) -> p k n", n=L))
            stream(phases["o1"].pieces, 4, 16)
            norm(phases["n3"], x1, ns1, tm1, h1, 2, lambda: act.wait_ge(S["acc_taken"], phases["n3"].taken))
            gate_up(phases["g2"])
            stream(phases["d2"].pieces, 2, 88)
            root(x1, ns1, 2, lambda: act.wait_ge(S["acc_taken"], phases["n40"].taken))
            units = 0
            cgs = 13 + 12
            for ly in range(2):
                nt = NT[ly]

                def x_ready(ly=ly):
                    if ly == 0:
                        act.wait_ge(S["x4_in"], 2)
                        act.wait_ge(S["ctx_in"], 16)
                    else:
                        act.wait_ge(S["acc_taken"], phases["n41"].taken)
                    act.wait_ge(S["mt_taken"], 9 * (ly + 1))
                norm(phases[f"n4{ly}"], x4, ns2, tm2, hT, 4, x_ready)
                stream(phases[f"ca{ly}"].pieces, 5, 16)
                act.wait_ge(S["acc_taken"], phases[f"ca{ly}"].taken + 5 * nt)
                act.activation(ca[:, 1, 0:nt], ca[:, 1, 0:nt], ACT.Sigmoid).then_inc(S["gates_made"], 1)
                act.activation(gC[:, 0:nt], ca[:, 2, 0:nt], ACT.Silu).then_inc(S["gates_made"], 1)
                act.activation(ca[:, 4, 0:nt], ca[:, 4, 0:nt], ACT.Silu).then_inc(S["gates_made"], 1)
                act.wait_ge(S["pad_made"], ly + 1)
                for c in range(4):
                    act.wait_ge(S["yt_done"], 4 * ly + c + 1)
                    act.activation(yT[:, c, 0:nt // 2, PAD:PAD + L],
                                   tp[c % 2][:, 0:nt * P].rearrange("p (s n) -> p s n", n=L),
                                   ACT.Copy).then_inc(S["yt_taken"], 1)
                for g in range(4):
                    act.wait_ge(S["pl_done"], 4 * ly + g + 1)
                    act.activation(pdT[:, g, 0:nt * P], cg[g % 2][:, 0:nt * P], ACT.Copy).then_inc(S["pl_taken"], 1)
                for nm_, _, n_, _ in SEGS[ly]:
                    stream(phases[f"s{ly}{nm_}"].pieces, n_, 16)

                for t in range(nt):
                    k = (4 if ly else 0) + t
                    act.wait_ge(S["z_made"], 2 * k + 1)
                    act.activation(mv[:, 3:4], mv[:, 2:3], ACT.Sqrt).then_inc(S["cf_sd"], 1)
                    act.wait_ge(S["cz_done"], k + 1)
                    if t >= 2:
                        act.wait_ge(S["pw_done"], k - 1)
                    for c in range(4):
                        ins = act.activation(sT[:, t % 2, c * P:(c + 1) * P], cg[t % 2][:, c * P:(c + 1) * P], ACT.Silu,
                                             scale=cvec[:, 8 + 4 * ly + c:9 + 4 * ly + c],
                                             bias=cvec[:, 16 + 4 * ly + c:17 + 4 * ly + c])
                    ins.then_inc(S["s_made"], 1)

                act.wait_ge(S["acc_taken"], phases[f"mx{ly}"].taken)
                act.activation(qkvg[:, 6:8, 0:nt], qkvg[:, 6:8, 0:nt], ACT.Silu).then_inc(S["gates_made"], 1)
                U = 6 if nt == 4 else 4
                u0, kinds = units, kinds_of(nt)
                with act.Fori(0, 2) as oa, act.Fori(0, 4) as ib:
                    lap = oa * 4 + ib
                    act.wait_ge(S["cg_done"], lap * 2 + cgs)
                    cols = bass.ds(ib * P, P)
                    ins = act.activation(st[:, 4:6], qkvg[:, oa + 2, 2:4, cols], ACT.Copy)
                    if nt == 4:
                        ins = act.activation(st[:, 6:8], qkvg[:, oa, 2:4, cols], ACT.Copy)
                    ins.then_inc(S["st_act"], 1)
                    act.wait_ge(S["cg_done"], lap * 2 + (cgs + 1))
                    act.activation(T[:, 0:nt * P], cg[0][:, 0:nt * P], ACT.Copy, scale=NA_D ** -0.5).then_inc(S["cg_taken"], 1)
                    act.wait_ge(S["cg_done"], lap * 2 + (cgs + 2))
                    act.activation(T[:, CH:2 * CH], cg[1][:], ACT.Copy).then_inc(S["cg_taken"], 1)

                    def na_exp(u):
                        act.wait_ge(S["m_ready"], lap * U + (16 + u0 + u + 1))
                        if kinds[u][1] < 2:
                            act.activation(pr[:, u % 2], acc[u % 2][:], ACT.Exp, bias=nm[:, u % 2, 0:1],
                                           accum_out=sm[:, u % 2, 0:1]).then_inc(S["p_made"], 1)
                        else:
                            for t in range(2):
                                ins = act.activation(pr[:, u % 2, t * L:(t + 1) * L], acc[u % 2][:, t * L:(t + 1) * L],
                                                     ACT.Exp, bias=nm[:, u % 2, t:t + 1],
                                                     accum_out=sm[:, u % 2, t:t + 1])
                            ins.then_inc(S["p_made"], 1)

                    def na_pt(u):
                        act.wait_ge(S["pt_done"], lap * U + (u0 + u + 1))
                        act.wait_ge(S["o_done"], lap * U + (12 + max(u0 + u - 1, 0)))
                        act.activation(pt[:, u % 2], tp[u % 2][:], ACT.Copy).then_inc(S["pt_taken"], 1)

                    na_exp(0)
                    for u in range(U):
                        if u + 1 < U:
                            na_exp(u + 1)
                        na_pt(u)
                units += 8 * U
                cgs += 16
                g0 = phases[f"mx{ly}"].groups
                for t in range(nt):
                    for g in range(4):
                        group_hi(g0 + 4 * t + g, hT[0][:, 4 * g:4 * g + 4, t * P:(t + 1) * P],
                                 tm2[:, g % 2].rearrange("p (k n) -> p k n", n=P))
                for k in range(8):
                    act.wait_ge(S["gs_done"], 8 * ly + k + 1)
                    act.activation(gatb[:, k % 2, k // 2 * CH:(k // 2 + 1) * CH], cg[k % 2][:],
                                   ACT.Copy).then_inc(S["gs_taken"], 1)
                stream(phases[f"o2{ly}"].pieces, 4, 16, last=ly == 1)
            root(x4, ns2, 2, lambda: act.wait_ge(S["acc_taken"], phases["end"].taken))
            act.wait_ge(S["y_made"], 1)
            act.dma_start(out_v, x4[:, 0:2, :]).then_inc(S["y_out"], 16)
            act.wait_ge(S["y_out"], 16)

        @block.vector
        def _(dve):
            link = Link(dve, S["dve_step"])
            norms = [0, 0]

            def var_root(nt):
                norms[0] += 1
                norms[1] += nt
                dve.wait_ge(S["ss_made"], norms[1])
                dve.tensor_scalar(rs[:, 0:nt], ss[:, 0:nt], 1.0 / D, EPS, ALU.mult, ALU.add).then_inc(S["var_made"], 1)
                dve.wait_ge(S["sd_made"], norms[0])
                dve.reciprocal(rs[:, 0:nt], sd[:, 0:nt]).then_inc(S["rs_made"], 1)

            def group_lo(g, dst, dst_hi, src):
                dve.wait_ge(S["tg_hi"], num(g + 1))
                dve.tensor_tensor(dst, src, dst_hi, ALU.subtract).then_inc(S["tg_lo"], 1)

            def take(turns, g, k, tm, gain, shift):
                dve.wait_ge(S["tp_done"], turns)
                wait(dve, "tg_lo", g - 1)
                src = tp[k % 2][:].rearrange("p (k n) -> p k n", n=P)
                tv = tm[:, k % 2].rearrange("p (k n) -> p k n", n=P)
                if gain is None:
                    dve.tensor_copy(tv, src).then_inc(S["tg_full"], 1)
                    return
                ins = dve.tensor_tensor(tv, src, gain[:, 4 * k:4 * k + 4].unsqueeze(2).broadcast_to([P, 4, P]), ALU.mult)
                if shift is not None:
                    link(ins)
                    ins = dve.tensor_tensor(tv, tv, shift[:, 4 * k:4 * k + 4].unsqueeze(2).broadcast_to([P, 4, P]), ALU.add)
                ins.then_inc(S["tg_full"], 1)

            def groups(ph, nt, tm, dst, gain_of):
                g0 = ph.groups

                def rest(m):
                    t, k = divmod(m, 4)
                    s = slice(4 * k, 4 * k + 4)
                    group_lo(g0 + m, dst[1][:, s, t * P:(t + 1) * P], dst[0][:, s, t * P:(t + 1) * P].bitcast(F32),
                             tm[:, k % 2].rearrange("p (k n) -> p k n", n=P))
                for m in range(4 * nt):
                    t, k = divmod(m, 4)
                    take(turned(ph) + m + 1, g0 + m, k, tm, *gain_of(t))
                    if m:
                        rest(m - 1)
                rest(4 * nt - 1)

            def norm(ph, tm, dst, nt, gain_of):
                var_root(nt)
                groups(ph, nt, tm, dst, gain_of)

            def gate_up(ph, gates):
                def u_split(c, off):
                    for f in range(2):
                        dve.wait_ge(S["tp_done"], num(lap_at(turned(ph) + 2 * off + f + 1, 2, c)))
                        dve.wait_ge(S["tg_lo"], num(lap_at(ph.groups + 2 * off + f - 1, 2, c)))
                        dve.tensor_copy(tm1[:, f], tp[f][:]).then_inc(S["tg_full"], 1)
                    for f in range(2):
                        cols = slice(4 * (c + off) + 2 * f, 4 * (c + off) + 2 * f + 2) if isinstance(c, int) else \
                            bass.ds(c * 4 + (4 * off + 2 * f), 2)
                        group_lo(lap_at(ph.groups + 2 * off + f, 2, c), uT[1][:, cols, :],
                                 uT[0][:, cols, :].bitcast(F32), tm1[:, f].rearrange("p (k n) -> p k n", n=L))

                def products(c):
                    for t in range(2):
                        dve.wait_ge(S["gate_act"], num(lap_at(gates + t + 1, 2, c)))
                        pair_done(dve, ph, 32, c, 1, t)
                        dve.tensor_tensor(ub[:, t], ub[:, t], acc[2 + t][:], ALU.mult).then_inc(S["acc_taken"], 1)

                for j in range(2, 34):
                    lo_piece(dve, ph.pieces, j)
                products(0)
                with dve.Fori(1, FC) as i:
                    p0 = At(ph.pieces, 32, i)
                    for j in range(2, 6):
                        lo_piece(dve, p0, j)
                    u_split(i, -1)
                    for j in range(6, 34):
                        lo_piece(dve, p0, j)
                    products(i)
                u_split(FC - 1, 0)

            def down_proj(ph):
                with dve.Fori(0, 2) as i:
                    p0 = At(ph.pieces, 88, i)
                    for j in range(2, 90):
                        lo_piece(dve, p0, j)
                    for b in range(4):
                        pair_done(dve, ph, 88, i, b // 2, b % 2)
                        xv = x1[:, b % 2, bass.ds(i * (2 * CH) + b // 2 * CH, CH)]
                        dve.scalar_tensor_tensor(out=xv, in0=acc[b][:], scalar=0.5, in1=xv, op0=ALU.mult,
                                                 op1=ALU.add).then_inc(S["acc_taken"], 1)

            def stream(ph, laps, nt, evac, last=False, extra=None):
                n_ = laps - 1 if last else laps

                def one(i, ahead):
                    for j in range(2, 18 if ahead else 16):
                        lo_piece(dve, At(ph.pieces, 16, i) if not isinstance(i, int) else ph.pieces + 16 * i, j)
                        if extra:
                            extra(i, j - 2)
                    for t in range(nt):
                        bank_done(dve, ph, nt, i, t)
                        evac(i, t)
                with dve.Fori(0, n_) as i:
                    one(i, True)
                if last:
                    one(n_, False)

            dve.memset(ones[:], 1.0).then_inc(S["cols_taken"], 1)
            dve.memset(dw[:], 0.0).then_inc(S["cols_taken"], 1)
            dve.wait_ge(S["cols_taken"], 2)
            for k, (dst, c0, c1) in enumerate(((vec[:], 0, NV), (bmod[:], 0, 96), (cvec[:], 96, 120),
                                               (dw[:, 0, 0:124], 0, 124), (dw[:, 1, 0:124], 0, 124))):
                bank = acc[(0, 1, 1, 2, 3)[k]]
                dve.wait_ge(S["cols_made"], (1, 2, 2, 3, 4)[k])
                dve.tensor_copy(dst, bank[:, c0:c1]).then_inc(S["cols_taken"], 1)
            for j in range(2):
                lo_piece(dve, 0, j)
            dve.wait_ge(S["cols_taken"], 7)
            norm(phases["n1"], tm1, h1, 2, lambda t: (vec[:, 0:KT], None))
            gate_up(phases["g1"], 0)
            down_proj(phases["d1"])
            norm(phases["n2"], tm1, h1, 2, lambda t: (vec[:, KT:2 * KT], None))

            def proj_take(i, t):
                dve.tensor_copy(proj[:, t, bass.ds(i * CH, CH)], acc[t][:]).then_inc(S["acc_taken"], 1)
            stream(phases["i1"], 9, 2, proj_take)

            dve.wait_ge(S["rope_in"], 16 * 13)
            for k in range(2):
                ins = dve.tensor_tensor_reduce(rt[:, 0, 0:P], lamv[:, 2 * k], lamv[:, 2 * k + 1], 1.0, 0.0, ALU.mult,
                                               ALU.add, lam[:, k:k + 1])
                if k == 0:
                    link(ins)
            ins.then_inc(S["lam_e"], 1)
            dve.wait_ge(S["lam_e"], 1)
            dve.wait_ge(S["acc_taken"], phases["at1"].taken)
            parts = ((0, 10, 0), (B_COL, 16, 10))
            for t in range(2):
                for c0, nh, s0 in parts:
                    xv = proj[:, t, c0:c0 + nh * HD].rearrange("p (h d) -> p h d", d=HD)
                    sq = rt[:, 0, 0:nh * HD].rearrange("p (h d) -> p h d", d=HD)
                    link(dve.tensor_tensor(sq, xv, xv, ALU.mult))
                    link(dve.tensor_reduce(qss[:, t, s0:s0 + nh], sq, AX, ALU.add))
            dve.tensor_scalar(qss[:], qss[:], 1.0 / HD, EPS, ALU.mult, ALU.add).then_inc(S["qk_ss"], 1)
            dve.wait_ge(S["qk_sd"], 1)
            link(dve.reciprocal(qsd[:], qsd[:]))
            for t in range(2):
                for c0, nh, s0 in parts:
                    xv = proj[:, t, c0:c0 + nh * HD].rearrange("p (h d) -> p h d", d=HD)
                    link(dve.tensor_tensor(xv, xv, qsd[:, t, s0:s0 + nh].unsqueeze(2).broadcast_to([P, nh, HD]), ALU.mult))
                    nq = 8
                    for k, (ha, hb) in enumerate(((0, nq), (nq, nh))):
                        g = gbc[:, (0 if s0 == 0 else 2) + k].unsqueeze(1).broadcast_to([P, hb - ha, HD])
                        link(dve.tensor_tensor(xv[:, ha:hb], xv[:, ha:hb], g, ALU.mult))
                    w = HD if s0 == 0 else 32
                    nb, half = (2, 32) if s0 == 0 else (1, 16)
                    cs = ropa if s0 == 0 else ropb
                    r1 = rt[:, 0, 0:nh * w].rearrange("p (h d) -> p h d", d=w)
                    r2 = rt[:, 1, 0:nh * w].rearrange("p (h d) -> p h d", d=w)
                    xw = xv[:, :, 0:w]
                    link(dve.tensor_tensor(r1, xw, cs[:, 0, t].unsqueeze(1).broadcast_to([P, nh, w]), ALU.mult))
                    for blk in range(nb):
                        for s in range(2):
                            d0 = blk * 2 * half + s * half
                            s1 = blk * 2 * half + (1 - s) * half
                            link(dve.tensor_tensor(r2[:, :, d0:d0 + half], xw[:, :, s1:s1 + half],
                                                   cs[:, 1, t, d0:d0 + half].unsqueeze(1).broadcast_to([P, nh, half]),
                                                   ALU.mult))
                    ins = dve.tensor_tensor(xw, r1, r2, ALU.add)
                    if (t, s0) == (1, 10):
                        ins.then_inc(S["roped"], 1)
                    else:
                        link(ins)
            dve.wait_ge(S["lam_e"], 2)
            link(dve.tensor_tensor(lam[:, 0:1], lam[:, 3:4], lam[:, 2:3], ALU.subtract))
            link(dve.tensor_scalar(lam[:, 0:1], lam[:, 0:1], LAMBDA_INIT, None, ALU.subtract))

            def maxes(q):
                dve.wait_ge(S["s_done"], q + 1)
                link(dve.tensor_reduce(mx[:, q % 2], acc[q % 2][:].rearrange("p (t n) -> p t n", n=L), AX, ALU.max))
                dve.tensor_scalar(nm[:, q % 2], mx[:, q % 2], -SCALE, None, ALU.mult).then_inc(S["m_ready"], 1)

            g0 = phases["at1"].groups
            maxes(0)
            for q in range(8):
                maxes(q + 1)
                dve.wait_ge(S["p_made"], q + 1)
                link(dve.reciprocal(rr[:, q % 2], sm[:, q % 2]))
                dve.tensor_tensor(pr1[:, q % 2], pr1[:, q % 2], rr[:, q % 2].unsqueeze(2).broadcast_to([P, 2, L]),
                                  ALU.mult).then_inc(S["pn_made"], 1)
                dve.wait_ge(S["o_done"], q + 1)
                dve.wait_ge(S["tg_lo"], g0 + q - 1)
                dve.tensor_copy(tm1[:, q % 2, 0:L], acc[2 + q % 2][:, 0:L]).then_inc(S["tg_full"], 1)
                group_lo(g0 + q, h1[1][:, q], h1[0][:, q].bitcast(F32), tm1[:, q % 2, 0:L])
            for h in range(B_HEADS):
                maxes(9 + 2 * h)
                dve.wait_ge(S["p_made"], 10 + 2 * h)
                link(dve.reciprocal(rr[:], sm[:]))
                link(dve.tensor_scalar(rr[:, 1], rr[:, 1], lam[:, 0:1], None, ALU.mult))
                for t in range(2):
                    link(dve.tensor_scalar(pr1[:, 1, t], pr1[:, 1, t], rr[:, 1, t:t + 1], None, ALU.mult))
                    ins = dve.scalar_tensor_tensor(out=pr1[:, 0, t], in0=pr1[:, 0, t], scalar=rr[:, 0, t:t + 1],
                                                   in1=pr1[:, 1, t], op0=ALU.mult, op1=ALU.add)
                    if t == 0:
                        link(ins)
                ins.then_inc(S["pn_made"], 1)
                if h + 1 < B_HEADS:
                    maxes(10 + 2 * h)
                dve.wait_ge(S["o_done"], 9 + h)
                dve.tensor_copy(ob[:], acc[2 + h % 2][:].rearrange("p (t n) -> p t n", n=L)).then_inc(S["o_taken"], 1)
                dve.wait_ge(S["o_taken"], h + 1)
                for t in range(2):
                    link(dve.tensor_tensor_reduce(rt[:, 0, 0:L], ob[:, t], ob[:, t], 1.0, 0.0, ALU.mult, ALU.add,
                                                  lam[:, 4 + t:5 + t]))
                dve.tensor_scalar(lam[:, 4:6], lam[:, 4:6], 1.0 / L, EPS, ALU.mult, ALU.add).then_inc(S["ob_made"], 1)
                dve.wait_ge(S["qk_sd"], 2 + h)
                link(dve.reciprocal(lam[:, 6:8], lam[:, 6:8]))
                for t in range(2):
                    link(dve.tensor_scalar(ob[:, t], ob[:, t], lam[:, 6 + t:7 + t], None, ALU.mult))
                dve.scalar_tensor_tensor(out=ob[:], in0=ob[:], scalar=1.0 - LAMBDA_INIT,
                                         in1=sub_bc[:].unsqueeze(1).broadcast_to([P, 2, L]), op0=ALU.mult,
                                         op1=ALU.mult).then_inc(S["ob_made"], 1)
                dve.wait_ge(S["tp_done"], g0 + h + 1)
                dve.wait_ge(S["tg_lo"], g0 + 8 + h - 1)
                dve.tensor_copy(tm1[:, h % 2], tp[h % 2][:]).then_inc(S["tg_full"], 1)
                ks = slice(8 + 2 * h, 10 + 2 * h)
                group_lo(g0 + 8 + h, h1[1][:, ks, :], h1[0][:, ks, :].bitcast(F32),
                         tm1[:, h % 2].rearrange("p (k n) -> p k n", n=L))

            def x_add(i, t):
                xv = x1[:, t, bass.ds(i * CH, CH)]
                dve.tensor_tensor(xv, acc[t][:], xv, ALU.add).then_inc(S["acc_taken"], 1)
            stream(phases["o1"], 4, 2, x_add)
            norm(phases["n3"], tm1, h1, 2, lambda t: (vec[:, 2 * KT:3 * KT], None))
            gate_up(phases["g2"], 2 * FC)
            down_proj(phases["d2"])
            var_root(2)
            dve.wait_ge(S["rs_made"], norms[0])
            dve.wait_ge(S["fin_in"], 16)
            for t in range(2):
                dve.scalar_tensor_tensor(out=x4[:, t], in0=x1[:, t], scalar=rs[:, t:t + 1], in1=ogain[:], op0=ALU.mult,
                                         op1=ALU.mult).then_inc(S["x4_in"], 1)

            units, convs = 0, 0
            ca_taken = 0
            for ly in range(2):
                nt = NT[ly]
                with dve.Fori(0, 8) as i:
                    dve.wait_ge(S["row_done"], i + (12 * ly + 1))
                    dve.tensor_copy(rowb[:], acc[0][0:2, :]).then_inc(S["row_taken"], 1)
                    dve.wait_ge(S["mt_done"], i + (8 * ly + 1))
                    dve.tensor_copy(modT[:, bass.ts(i, 4), :], acc[1][:, 0:8].rearrange("p (k c) -> p k c", c=2))\
                       .then_inc(S["mt_taken"], 1)
                dve.wait_ge(S["brow_in"], 16 * (ly + 1))
                with dve.Fori(0, 4) as i:
                    dve.wait_ge(S["row_done"], i + (12 * ly + 9))
                    gv = grow[:, bass.ds(i * CH, CH)]
                    dve.tensor_tensor(gv, acc[0][0:2, :], gv, ALU.add).then_inc(S["row_taken"], 1)
                dve.wait_ge(S["mt_taken"], 9 * ly + 8)
                for c in range(2):
                    b0 = 48 * ly
                    link(dve.tensor_tensor(mB[:, c], modT[:, 0:KT, c], bmod[:, b0:b0 + KT], ALU.add))
                    link(dve.tensor_tensor(mA[:, c], modT[:, KT:2 * KT, c], bmod[:, b0 + KT:b0 + 2 * KT], ALU.add))
                    ins = dve.scalar_tensor_tensor(out=mA[:, c], in0=mA[:, c], scalar=1.0,
                                                   in1=vec[:, (3 + ly) * KT:(4 + ly) * KT], op0=ALU.add, op1=ALU.mult)
                    if c == 0:
                        link(ins)
                ins.then_inc(S["mt_taken"], 1)
                dve.wait_ge(S["mt_taken"], 9 * (ly + 1))
                norm(phases[f"n4{ly}"], tm2, hT, 4, lambda t: (mA[:, t // 2], mB[:, t // 2]))

                dve.wait_ge(S["xs_out"], 16 * (ly + 1))

                def ca_take(i, t):
                    dve.tensor_copy(ca[:, i, t], acc[t][:]).then_inc(S["acc_taken"], 1)
                stream(phases[f"ca{ly}"], 5, nt, ca_take)
                dve.wait_ge(S["gates_made"], 4 * ly + 1)
                dve.tensor_tensor(ca[:, 0, 0:nt], ca[:, 0, 0:nt], ca[:, 1, 0:nt], ALU.mult).then_inc(S["glu_made"], 1)
                for c in range(4):
                    dve.memset(cv[:, c], 0.0).then_inc(S["conv_step"], 1)
                dve.wait_ge(S["ca_const_in"], 48 * (ly + 1))
                dve.wait_ge(S["gates_made"], 4 * ly + 3)
                for t in range(nt):
                    dve.wait_ge(S["py_done"], (4 if ly else 0) + t + 1)
                    link(dve.tensor_tensor(ya[:, t], acc[t][:], psc[:], ALU.mult))
                    dve.tensor_tensor(ya[:, t], ya[:, t], ca[:, 4, t], ALU.mult).then_inc(S["py_taken"], 1)
                dve.wait_ge(S["py_taken"], (4 if ly else 0) + nt)
                dve.wait_ge(S["yt_taken"], 4 * ly + 4)
                ns_ = nt // 2
                for nm_, c0, n_, snt in SEGS[ly]:
                    def tap(i, s, c0=c0):
                        j = i + c0
                        dve.wait_ge(S["conv_step"], j * 16 + (132 * ly + s + 1))
                        c, kk = s % 4, s // 4
                        yv = yT[:, c, 0:ns_, bass.ds(j * 4 + kk, L)]
                        av = cv[:, c, 0:nt * P].rearrange("p (s n) -> p s n", n=L)
                        dve.scalar_tensor_tensor(out=av, in0=yv, scalar=dw[:, ly, bass.ds(j * 16 + s, 1)], in1=av,
                                                 op0=ALU.mult, op1=ALU.add).then_inc(S["conv_step"], 1)

                    def take4(i, t, c0=c0):
                        dve.tensor_copy(qkvg[:, i + c0, t], acc[t][:]).then_inc(S["acc_taken"], 1)
                    stream(phases[f"s{ly}{nm_}"], n_, snt, take4, extra=tap)

                dve.wait_ge(S["conv_step"], 132 * (ly + 1))
                for c in range(4):
                    av = cv[:, c, 0:nt * P]
                    dve.tensor_scalar(av, av, cvec[:, 4 * ly + c:4 * ly + c + 1], None, ALU.add).then_inc(S["cf_b"], 1)
                for t in range(nt):
                    k = (4 if ly else 0) + t
                    dve.wait_ge(S["cf_done"], k + 1)
                    link(dve.bn_stats(bn[:], tp[t % 2][:]))
                    link(dve.bn_aggr(mv[:, 0:2], bn[:]))
                    dve.tensor_scalar(mv[:, 2:3], mv[:, 1:2], LN_EPS, None, ALU.add).then_inc(S["z_made"], 1)
                    dve.wait_ge(S["cf_sd"], k + 1)
                    link(dve.reciprocal(mv[:, 3:4], mv[:, 3:4]))
                    dve.tensor_scalar(zb[:, t % 2], tp[t % 2][:], mv[:, 0:1], mv[:, 3:4], ALU.subtract,
                                      ALU.mult).then_inc(S["z_made"], 1)
                    dve.wait_ge(S["pw_done"], k + 1)
                    dve.tensor_tensor(gC[:, t], acc[t % 2][:], gC[:, t], ALU.mult).then_inc(S["yc_made"], 1)

                U = 6 if nt == 4 else 4
                u0, kinds = units, kinds_of(nt)
                ot0 = B_HEADS + u0
                dve.wait_ge(S["na_in"], 64 * (ly + 1))
                dve.wait_ge(S["gates_made"], 4 * ly + 4)
                dve.wait_ge(S["acc_taken"], phases[f"mx{ly}"].taken)
                cg0 = 25 + 16 * ly
                with dve.Fori(0, 2) as oa, dve.Fori(0, 4) as ib:
                    lap = oa * 4 + ib
                    link.start(lap, 7 + 2 * U)
                    dve.wait_ge(S["cg_done"], lap * 2 + cg0)
                    for s in range(2):
                        xv = qkvg[:, oa + 2 * s, 0:2, bass.ds(ib * P, P)]
                        link(dve.tensor_tensor(rn[:, 0], xv, ropn[:, 0], ALU.mult))
                        for hf in range(2):
                            src = qkvg[:, oa + 2 * s, 0:2, bass.ds(ib * P, P)]\
                                .rearrange("p t (b h n) -> p t b h n", h=2, n=16)[:, :, :, 1 - hf, :]
                            dst = rn[:, 1].rearrange("p t (b h n) -> p t b h n", h=2, n=16)[:, :, :, hf, :]
                            sn = ropn[:, 1].rearrange("p t (b h n) -> p t b h n", h=2, n=16)[:, :, :, hf, :]
                            link(dve.tensor_tensor(dst, src, sn, ALU.mult))
                        ins = dve.tensor_tensor(st[:, 2 * s:2 * s + 2], rn[:, 0], rn[:, 1], ALU.add)
                        if s == 0:
                            link(ins)
                    ins.then_inc(S["st_dve"], 1)

                    def na_max(u):
                        e, t = kinds[u]
                        dve.wait_ge(S["s_done"], lap * U + (16 + u0 + u + 1))
                        if t < 2:
                            link(dve.tensor_reduce(mx[:, u % 2, 0:1], acc[u % 2][:], AX, ALU.max))
                            dve.tensor_scalar(nm[:, u % 2, 0:1], mx[:, u % 2, 0:1], -1.0, None,
                                              ALU.mult).then_inc(S["m_ready"], 1)
                        else:
                            link(dve.tensor_reduce(mx[:, u % 2], acc[u % 2][:].rearrange("p (t n) -> p t n", n=L), AX,
                                                   ALU.max))
                            dve.tensor_scalar(nm[:, u % 2], mx[:, u % 2], -1.0, None, ALU.mult).then_inc(S["m_ready"], 1)

                    def na_out(u):
                        e, t = kinds[u]
                        dve.wait_ge(S["p_made"], lap * U + (16 + u0 + u + 1))
                        dve.wait_ge(S["o_taken"], lap * U + (ot0 + u - 1))
                        link(dve.reciprocal(rr[:, u % 2], sm[:, u % 2]) if t == 2 else
                             dve.reciprocal(rr[:, u % 2, 0:1], sm[:, u % 2, 0:1]))
                        dve.wait_ge(S["o_done"], lap * U + (12 + u0 + u + 1))
                        for k, tt in enumerate((2, 3) if t == 2 else (t,)):
                            gv = qkvg[:, oa + 6, tt, bass.ds(ib * P + e * NA_D, NA_D)]
                            ins = dve.scalar_tensor_tensor(out=gv, in0=acc[2 + u % 2][:, k * NA_D:(k + 1) * NA_D],
                                                           scalar=rr[:, u % 2, k:k + 1], in1=gv, op0=ALU.mult,
                                                           op1=ALU.mult)
                        ins.then_inc(S["o_taken"], 1)

                    na_max(0)
                    for u in range(U):
                        if u + 1 < U:
                            na_max(u + 1)
                        na_out(u)
                link.stop(8)
                units += 8 * U
                groups(phases[f"mx{ly}"], nt, tm2, hT, lambda t: (None, None))
                dve.wait_ge(S["x4r_in"], 32 if ly == 0 else 48)
                dve.wait_ge(S["gs_taken"], 8 * (ly + 1))

                def add_gated(i, t):
                    cols = bass.ds(i * CH, CH)
                    dve.wait_ge(S["acc_taken"], num(lap_at(phases[f"o2{ly}"].taken + t - 1, nt, i)))
                    dve.tensor_tensor(tm2[:, t % 2], acc[t][:], gatb[:, t // 2, cols], ALU.mult)\
                       .then_inc(S["tmp_made"], 1)
                    v = lap_at((16 if ly else 0) + t + 1, nt, i)
                    dve.wait_ge(S["tmp_made"], num(v))
                    xv = x4[:, t, cols]
                    dve.tensor_tensor(xv, tm2[:, t % 2], xv, ALU.add).then_inc(S["acc_taken"], 1)
                stream(phases[f"o2{ly}"], 4, nt, add_gated, last=ly == 1)
            var_root(2)
            dve.wait_ge(S["rs_made"], norms[0])
            dve.wait_ge(S["fin_in"], 32)
            for t in range(2):
                ins = dve.scalar_tensor_tensor(out=x4[:, t], in0=x4[:, t], scalar=rs[:, t:t + 1], in1=fgain[:],
                                               op0=ALU.mult, op1=ALU.mult)
                if t == 0:
                    link(ins)
            ins.then_inc(S["y_made"], 1)

        @block.tensor
        def _(pe):
            def bank_free(g, m):
                wait(pe, "tg_full", g - 1 if m >= 2 else g)

            def turn4(g, m, src):
                for k in range(4):
                    ins = pe.transpose(tp[m % 2][:, k * P:(k + 1) * P], src(k), ident[:])
                ins.then_inc(S["tp_done"], 1)

            scaled = [0]

            def norm(ph, ns, nt):
                for t in range(nt):
                    scaled[0] += 1
                    pe.wait_ge(S["scaled"], scaled[0])
                    for g in range(4):
                        bank_free(ph.groups + 4 * t + g, 4 * t + g)
                        turn4(0, g, lambda k: ns[:, t % 2, (4 * g + k) * P:(4 * g + k + 1) * P])

            def begin(ph):
                pe.wait_ge(S["tg_lo"], ph.groups)
                wait(pe, "acc_taken", ph.taken)

            def gate_up(ph, gates):
                begin(ph)

                def u_turn(c, off):
                    pe.wait_ge(S["acc_taken"], num(lap_at(ph.taken + 2 * off + 2, 2, c)))
                    pe.wait_ge(S["tg_full"], num(lap_at(ph.groups + 2 * off, 2, c)))
                    for f in range(2):
                        for k in range(2):
                            for t in range(2):
                                ins = pe.transpose(tp[f][:, k * L + t * P:k * L + (t + 1) * P],
                                                   ub[:, t, (2 * f + k) * P:(2 * f + k + 1) * P], ident[:])
                        ins.then_inc(S["tp_done"], 1)

                pair_pieces(pe, h1, KT, ph.pieces, range(32), lambda half, t: None)
                with pe.Fori(1, FC) as i:
                    def bank_free(half, t):
                        if half == 0:
                            pe.wait_ge(S["gate_act"], num(At(gates + t - 1, 2, i)))
                        else:
                            pe.wait_ge(S["acc_taken"], num(At(ph.taken + t - 1, 2, i)))
                    p0 = At(ph.pieces, 32, i)
                    pair_pieces(pe, h1, KT, p0, range(4), bank_free)
                    u_turn(i, -1)
                    pair_pieces(pe, h1, KT, p0, range(4, 32), bank_free)
                u_turn(FC - 1, 0)

            def down_proj(ph):
                begin(ph)
                with pe.Fori(0, 2) as i:
                    pair_pieces(pe, uT, FT, At(ph.pieces, 88, i), range(88), lambda half, t: pe.wait_ge(
                        S["acc_taken"], num(At(ph.taken + 2 * half + t + 1 - 4, 4, i))))

            def stream(ph, src, laps, nt):
                begin(ph)
                with pe.Fori(0, laps) as i:
                    chunk_pieces(pe, src, nt, At(ph.pieces, 16, i), At(ph.taken, nt, i), range(16))

            pe.wait_ge(S["const_in"], 16 * 8)
            for k, (src, rows) in enumerate(((vrow[:], NV), (brow[:], 120), (drow[:, 0], 124), (drow[:, 1], 124))):
                pe.transpose(acc[k][:, 0:rows], src, ident[0:rows, 0:rows]).then_inc(S["cols_made"], 1)
            norm(phases["n1"], ns1, 2)
            pe.wait_ge(S["cols_taken"], 7)
            gate_up(phases["g1"], 0)
            down_proj(phases["d1"])
            norm(phases["n2"], ns1, 2)
            stream(phases["i1"], h1, 9, 2)

            pe.wait_ge(S["roped"], 1)

            def head_cols(hh):
                return hh * HD if hh < 10 else B_COL + (hh - 10) * HD
            for g in range(13):
                if g >= 2:
                    pe.wait_ge(S["cg_taken"], g - 1)
                for e in range(2):
                    for t in range(2):
                        c0 = head_cols(2 * g + e)
                        ins = pe.transpose(cg[g % 2][:, e * L + t * P:e * L + (t + 1) * P], proj[:, t, c0:c0 + HD], ident[:])
                ins.then_inc(S["cg_done"], 1)
            pe.wait_ge(S["cg_taken"], 13)
            wait(pe, "acc_taken", phases["at1"].taken)

            def scores(q):
                if q >= 2:
                    pe.wait_ge(S["p_made"], q - 1)
                qh, kh = (q, 8 + q // 4) if q < 8 else (10 + q - 8, 18 + q - 8)
                for t in range(2):
                    ins = pe.matmul(acc[q % 2][:, t * L:(t + 1) * L], qkT[:, qh, t * P:(t + 1) * P], qkT[:, kh, :],
                                    start=True, stop=True)
                ins.then_inc(S["s_done"], 1)

            def turn_p(k, pv):
                pe.wait_ge(S["pn_made"], k + 1)
                pe.wait_ge(S["cg_taken"], 12 + k)
                for j in range(2):
                    for t in range(2):
                        ins = pe.transpose(cg[(13 + k) % 2][:, j * L + t * P:j * L + (t + 1) * P],
                                           pv[:, t, j * P:(j + 1) * P], ident[:])
                ins.then_inc(S["cg_done"], 1)
                pe.wait_ge(S["cg_taken"], 14 + k)

            g0 = phases["at1"].groups
            scores(0)
            for q in range(8):
                scores(q + 1)
                turn_p(q, pr1[:, q % 2])
                if q >= 2:
                    pe.wait_ge(S["tg_full"], g0 + q - 1)
                c0 = VA_COL + q // 4 * HD
                for j in range(2):
                    ins = pe.matmul(acc[2 + q % 2][:, 0:L], proj[:, j, c0:c0 + HD], pt1[:, q % 2, j],
                                    start=(j == 0), stop=(j == 1))
                ins.then_inc(S["o_done"], 1)
            pe.wait_ge(S["tg_full"], g0 + 8)
            for h in range(B_HEADS):
                scores(9 + 2 * h)
                turn_p(8 + h, pr1[:, 0])
                if h + 1 < B_HEADS:
                    scores(10 + 2 * h)
                if h >= 2:
                    pe.wait_ge(S["o_taken"], h - 1)
                for t in range(2):
                    for j in range(2):
                        ins = pe.matmul(acc[2 + h % 2][:, t * L:(t + 1) * L], pt1[:, h % 2, j, t * P:(t + 1) * P],
                                        proj[:, j, VD_COL + h * L:VD_COL + (h + 1) * L], start=(j == 0), stop=(j == 1))
                ins.then_inc(S["o_done"], 1)
                pe.wait_ge(S["ob_made"], 2 * h + 2)
                if h >= 2:
                    pe.wait_ge(S["tg_full"], g0 + 8 + h - 1)
                for f in range(2):
                    for t in range(2):
                        ins = pe.transpose(tp[h % 2][:, f * L + t * P:f * L + (t + 1) * P], ob[:, t, f * P:(f + 1) * P],
                                           ident[:])
                ins.then_inc(S["tp_done"], 1)
            stream(phases["o1"], h1, 4, 2)
            norm(phases["n3"], ns1, 2)
            gate_up(phases["g2"], 2 * FC)
            down_proj(phases["d2"])

            units, cgs = 0, 25
            for ly in range(2):
                nt = NT[ly]
                wait(pe, "acc_taken", phases[f"n4{ly}"].taken)
                if ly == 0:
                    pe.wait_ge(S["silu_c"], 1)

                def row(i, n0):
                    if n0:
                        pe.wait_ge(S["row_taken"], i + (n0 + 12 * ly))
                    for u in range(4):
                        pe.wait_ge(S[f"mod{u}"], i * 16 + 16 * (n0 + 12 * ly + 1))
                        for k in range(4):
                            kt = 4 * u + k
                            ins = pe.matmul(acc[0][0:2, :], cT[:, kt, :], modr[:, u, k, :], start=(kt == 0),
                                            stop=(kt == KT - 1))
                        ins.then_inc(S["mod_used" if u < 3 else "row_done"], 1)
                with pe.Fori(0, 8) as i:
                    row(i, 0)
                    pe.wait_ge(S["row_taken"], i + (12 * ly + 1))
                    for k in range(4):
                        ins = pe.matmul(acc[1][:, 2 * k:2 * k + 2], rowb[:, k * P:(k + 1) * P], ident[0:2, 0:2],
                                        start=True, stop=True)
                    ins.then_inc(S["mt_done"], 1)
                with pe.Fori(0, 4) as i:
                    row(i, 8)
                norm(phases[f"n4{ly}"], ns2, 4)
                pe.wait_ge(S["row_taken"], 12 * (ly + 1))
                pe.wait_ge(S["mt_taken"], 9 * ly + 8)
                stream(phases[f"ca{ly}"], hT, 5, nt)
                pe.wait_ge(S["glu_made"], ly + 1)
                wait(pe, "tg_full", phases[f"ca{ly}"].groups)
                for c in range(4):
                    if c >= 2:
                        pe.wait_ge(S["yt_taken"], 4 * ly + c - 1)
                    for t in range(nt):
                        ins = pe.transpose(tp[c % 2][:, t * P:(t + 1) * P], ca[:, 0, t, c * P:(c + 1) * P], ident[:])
                    ins.then_inc(S["yt_done"], 1)
                pe.wait_ge(S["ca_const_in"], 48 * (ly + 1))
                pe.wait_ge(S["acc_taken"], phases[f"ca{ly}"].taken + 5 * nt)
                for g in range(4):
                    if g >= 2:
                        pe.wait_ge(S["pl_taken"], 4 * ly + g - 1)
                    for s in range(nt // 2):
                        for j in range(2):
                            ins = pe.matmul(cg[g % 2][:, s * L:(s + 1) * L], ca[:, 3, 2 * s + j, g * P:(g + 1) * P],
                                            pmat[:, j, g, :], start=(j == 0), stop=(j == 1))
                    ins.then_inc(S["pl_done"], 1)
                pe.wait_ge(S["pl_taken"], 4 * ly + 4)
                for t in range(nt):
                    for g in range(4):
                        ins = pe.matmul(acc[t][:, g * P:(g + 1) * P], pdT[:, g, t * P:(t + 1) * P], wpool[:, g, :],
                                        start=True, stop=True)
                    ins.then_inc(S["py_done"], 1)
                pe.wait_ge(S["py_taken"], (4 if ly else 0) + nt)
                for nm_, _, n_, snt in SEGS[ly]:
                    stream(phases[f"s{ly}{nm_}"], hT, n_, snt)

                pe.wait_ge(S["cf_b"], 4 * (ly + 1))
                pe.wait_ge(S["cf_in"], 48 * (ly + 1))
                wait(pe, "acc_taken", phases[f"mx{ly}"].taken)
                pe.wait_ge(S["yt_taken"], 4 * (ly + 1))

                def by_token(t):
                    k = (4 if ly else 0) + t
                    if t >= 2:
                        pe.wait_ge(S["z_made"], 2 * (k - 1))
                    for c in range(4):
                        ins = pe.transpose(tp[t % 2][:, c * P:(c + 1) * P], cv[:, c, t * P:(t + 1) * P], ident[:])
                    ins.then_inc(S["cf_done"], 1)
                by_token(0)
                for t in range(nt):
                    k = (4 if ly else 0) + t
                    if t + 1 < nt:
                        by_token(t + 1)
                    pe.wait_ge(S["z_made"], 2 * k + 2)
                    if t >= 2:
                        pe.wait_ge(S["s_made"], k - 1)
                    for c in range(4):
                        ins = pe.transpose(cg[t % 2][:, c * P:(c + 1) * P], zb[:, t % 2, c * P:(c + 1) * P], ident[:])
                    ins.then_inc(S["cz_done"], 1)
                    pe.wait_ge(S["s_made"], k + 1)
                    if t >= 2:
                        pe.wait_ge(S["yc_made"], k - 1)
                    for c in range(4):
                        pe.matmul(acc[t % 2][:], sT[:, t % 2, c * P:(c + 1) * P], cpw[:, c, :], start=(c == 0), stop=False)
                    pe.matmul(acc[t % 2][:], ones[:], cpb[:], start=False, stop=True).then_inc(S["pw_done"], 1)

                pe.wait_ge(S["bias_ready"], ly + 1)
                pe.wait_ge(S["yc_made"], (4 if ly else 0) + nt)
                pe.wait_ge(S["s_made"], (4 if ly else 0) + nt)
                U = 6 if nt == 4 else 4
                u0, kinds = units, kinds_of(nt)
                with pe.Fori(0, 2) as oa, pe.Fori(0, 4) as ib:
                    lap = oa * 4 + ib
                    pe.wait_ge(S["st_dve"], lap + (8 * ly + 1))
                    pe.wait_ge(S["st_act"], lap + (8 * ly + 1))
                    pe.wait_ge(S["cg_taken"], lap * 2 + cgs)
                    for m, tiles in enumerate(((0, 1, 6, 7)[:nt], (2, 3, 4, 5))):
                        for k, tt in enumerate(tiles):
                            ins = pe.transpose(cg[m][:, k * P:(k + 1) * P], st[:, tt], ident[:])
                        ins.then_inc(S["cg_done"], 1)
                    pe.wait_ge(S["cg_taken"], lap * 2 + (cgs + 2))

                    def na_scores(u):
                        e, t = kinds[u]
                        r = slice(e * NA_D, (e + 1) * NA_D)
                        pe.wait_ge(S["p_made"], lap * U + (16 + u0 + u - 1))
                        if t < 2:
                            pe.matmul(acc[u % 2][:], T[r, t * P:(t + 1) * P], T[r, CH:2 * CH], start=True, stop=False)
                            ins = pe.matmul(acc[u % 2][:, 0:L], turn[:],
                                            bias[:].rearrange("p h n -> p (h n)")[:, bass.ds(
                                                lap * (12 * GRID) + (6 * GRID * e + (2 - 2 * t) * GRID), L)],
                                            start=False, stop=True)
                        else:
                            for tt in range(2):
                                ins = pe.matmul(acc[u % 2][:, tt * L:(tt + 1) * L], T[r, L + tt * P:L + (tt + 1) * P],
                                                T[r, CH + L:2 * CH], start=True, stop=True)
                        ins.then_inc(S["s_done"], 1)

                    def na_values(u):
                        e, t = kinds[u]
                        pe.wait_ge(S["p_made"], lap * U + (16 + u0 + u + 1))
                        for j in range(4):
                            src = pr[:, u % 2, j * P:(j + 1) * P] if t < 2 else \
                                pr[:, u % 2, (j % 2) * L + j // 2 * P:(j % 2) * L + j // 2 * P + P]
                            ins = pe.transpose(tp[u % 2][:, j * P:(j + 1) * P], src, ident[:])
                        ins.then_inc(S["pt_done"], 1)
                        pe.wait_ge(S["pt_taken"], lap * U + (u0 + u + 1))
                        pe.wait_ge(S["o_taken"], lap * U + (B_HEADS + u0 + u - 1))
                        for k in range(1 if t < 2 else 2):
                            js = range(4) if t < 2 else range(2)
                            for j in js:
                                lh = pt[:, u % 2, j * P:(j + 1) * P] if t < 2 else \
                                    pt[:, u % 2, j * L + k * P:j * L + (k + 1) * P]
                                vt = j if t < 2 else 2 + j
                                ins = pe.matmul(acc[2 + u % 2][:, k * NA_D:(k + 1) * NA_D], lh,
                                                qkvg[:, oa + 4, vt, bass.ds(ib * P + e * NA_D, NA_D)],
                                                start=(j == 0), stop=(j == js[-1]))
                        ins.then_inc(S["o_done"], 1)

                    na_scores(0)
                    for u in range(U):
                        if u + 1 < U:
                            na_scores(u + 1)
                        na_values(u)
                units += 8 * U
                cgs += 16
                pe.wait_ge(S["o_taken"], B_HEADS + units)
                pe.wait_ge(S["pt_taken"], units)
                ph = phases[f"mx{ly}"]
                for t in range(nt):
                    for g in range(4):
                        m = 4 * t + g
                        bank_free(ph.groups + m, m)
                        src = (ya[:, t], qkvg[:, 6, t], qkvg[:, 7, t], gC[:, t])[g]
                        turn4(0, g, lambda k: src[:, k * P:(k + 1) * P])
                for k in range(8):
                    pe.wait_ge(S["gs_taken"], 8 * ly + k - 1) if 8 * ly + k - 1 > 0 else None
                    pe.matmul(cg[k % 2][:], selr[:, k % 2, :], grow[:, k // 2 * CH:(k // 2 + 1) * CH], start=True,
                              stop=True).then_inc(S["gs_done"], 1)
                stream(phases[f"o2{ly}"], hT, 4, nt)

        @block.gpsimd
        def _(pool):
            pool.wait_ge(S["pieces_used"], phases["n40"].pieces)
            pool.dma_start(ogain[:], row_bc(a["out_norm"], D)).then_inc(S["fin_in"], 16)
            pool.dma_start(x4[:, 2:4, :], ctx_v).then_inc(S["ctx_in"], 16)
            for ly in range(2):
                nt = NT[ly]
                pool.wait_ge(S["pieces_used"], phases[f"n4{ly}"].pieces)
                if ly == 1:
                    pool.wait_ge(S["gs_done"], 8)
                pool.dma_start(grow[:], bass.AP(tensor=bmodv.tensor, offset=ly * 3 * D + 2 * D, ap=[[0, 2], [1, D]]))\
                    .then_inc(S["brow_in"], 16)
                if ly == 0:
                    pool.wait_ge(S["x4_in"], 2)
                else:
                    pool.wait_ge(S["acc_taken"], phases["n41"].taken)
                pool.dma_start(xs_v, x4[:, 0:2, :]).then_inc(S["xs_out"], 16)
                if ly == 1:
                    pool.wait_ge(S["conv_step"], 132)
                pool.memset(yT[:, :, :, 0:PAD], 0.0).then_inc(S["pool_step"], 1)
                pool.memset(yT[:, :, :, PAD + L:YW], 0.0).then_inc(S["pad_made"], 1)
                pool.wait_ge(S["na_in"], 64 * (ly + 1))
                pool.wait_ge(S["bias_in"], 12 * 16 * (ly + 1))
                bv = bias[:].rearrange("p h (r n) -> p (h r) n", n=GRID)
                pool.tensor_tensor(bv, bv, mask[:].unsqueeze(1).broadcast_to([P, NA_H * 6, GRID]), ALU.add)\
                    .then_inc(S["bias_ready"], 1)
            pool.wait_ge(S["acc_taken"], phases["end"].taken)
            pool.dma_start(fgain[:], row_bc(a["final_norm_g_2"], D)).then_inc(S["fin_in"], 16)


def kinds_of(nt):
    return [(e, t) for e in range(2) for t in ((0, 1, 2) if nt == 4 else (0, 1))]


def kernel(**inputs):
    import concourse.bacc as bacc
    from concourse.bass_utils import run_bass_kernel_spmd

    cosa, sina, cosb, sinb, cosn, sinn = rope_tables()
    arrays = {k: np.ascontiguousarray(v) for k, v in inputs.items()}
    arrays["vrows"] = np.concatenate([np.asarray(inputs[k]).reshape(-1, P) for k in (
        "ffn1_norm", "mix_norm", "ffn2_norm", "norm_g_2", "c_2", "c_ctx_2")])
    arrays.update(cosa=cosa, sina=sina, cosb=cosb, sinb=sinb, cosn=cosn, sinn=sinn, pmat=pool_matrices(),
                  mask=window_mask(), turn=np.kron(np.eye(2), np.eye(GRID)[::-1]).astype(np.float32), ident=np.eye(P, dtype=np.float32),
                  selr=np.repeat(np.eye(2, dtype=np.float32)[:, :, None], P, 2))
    nc = bacc.Bacc("TRN2", target_bir_lowering=False, num_devices=1)
    aps = {k: nc.dram_tensor(k, v.shape, F32, kind="ExternalInput").ap() for k, v in arrays.items()}
    out = nc.dram_tensor("y", (1, L, D), F32, kind="ExternalOutput").ap()
    xs = nc.dram_tensor("x_rest", (L, D), F32, kind="Internal").ap()
    build(nc, aps, out, xs)
    r = run_bass_kernel_spmd(nc, [arrays], core_ids=[0])
    return r.results[0]["y"]
```

```python
from contextlib import ExitStack

import numpy as np

import concourse.bass as bass
from concourse import mybir

F32 = mybir.dt.float32
F32R = mybir.dt.float32r
ACT = mybir.ActivationFunctionType
ALU = mybir.AluOpType
AX = mybir.AxisListType.X

P = 128
D = 2048
KT = D // P
L = 256
CH = 512
DFF = 5632
FT = DFF // P
EPS = 1e-6
LN_EPS = 1e-5
HD = 128
A_HEADS, A_KV, B_HEADS = 8, 2, 4
B_COL = (A_HEADS + 2 * A_KV) * HD
VA_COL = (A_HEADS + A_KV) * HD
VD_COL = B_COL + 4 * B_HEADS * HD
D_IN = VD_COL + 2 * B_HEADS * HD
SCALE = HD ** -0.5
LAMBDA_INIT = 0.2
NA_H, NA_D = 16, 64
GRID = 64
RPB_R, RPB_C = 15, 31
TAPS = 31
PAD = TAPS // 2
YW = L + TAPS
POOLS = (2, 4, 8, 16)
PROJ2 = 6656
RING = 4


def rope_tables():
    t = np.arange(L, dtype=np.float32)
    rows, cols = np.floor(t / GRID).astype(np.float32), (t % GRID).astype(np.float32)

    def table(pos, dim, theta):
        f = np.float32(theta) ** (-np.arange(0, dim, 2, dtype=np.float32) / np.float32(dim))
        a = (pos[:, None] * f[None, :]).astype(np.float32)
        return np.concatenate([np.cos(a), np.cos(a)], 1), np.concatenate([-np.sin(a), np.sin(a)], 1)

    def pair(dim):
        r, c = table(rows, dim, 10000.0), table(cols, dim, 10000.0)
        return [np.concatenate([r[k], c[k]], 1) for k in range(2)]

    a = pair(64)
    b = table(t, 32, 500000.0)
    n = [np.tile(m, (1, 2)) for m in pair(32)]
    return [m.astype(np.float32) for m in (*a, *b, *n)]


def pool_matrices():
    m = np.zeros((len(POOLS), L, L), np.float32)
    for g, w in enumerate(POOLS):
        for t in range(L):
            lo, hi = max(t - w // 2, 0), min(t + (w - w // 2) - 1, L - 1)
            m[g, lo:hi + 1, t] = np.float32(1.0) / np.float32(hi - lo + 1)
            m[g, t, t] -= np.float32(1.0)
    return m.reshape(len(POOLS), 2, P, L).transpose(2, 1, 0, 3).copy()


def window_mask():
    q = np.arange(GRID)
    start = np.clip(q - 8, 0, GRID - 16)
    k = np.arange(GRID)[None, :]
    inside = (k >= start[:, None]) & (k < start[:, None] + 16)
    return np.tile(np.where(inside, 0.0, -1e30).astype(np.float32)[::-1], (2, 1))


class Phase:

    def __init__(self, pieces, taken, groups):
        self.pieces, self.taken, self.groups = pieces, taken, groups


def build(nc, a, out, xs_dram):
    ctx = ExitStack()
    with ctx:
        sem_names = """raw0 raw1 raw2 raw3 hi_made lo_made pieces_used acc_done acc_taken tp_done tg_full
            tg_hi tg_lo ss_made var_made sd_made scaled const_in cols_made cols_taken gate_act u_made
            dve_step act_step pool_step x_in rope_in roped qk_ss qk_sd cg_done cg_taken s_done m_ready p_made
            pn_made o_done o_taken lam_e ob_made x4_in xs_out ctx_in c_split
            row_taken mt_done mt_taken silu_c ca_const_in glu_made gates_made yt_done yt_taken pl_done
            pl_taken py_done py_taken pad_made conv_step cf_in cf_done z_made cz_done s_made pw_done
            yc_made na_in bias_in bias_ready  st_dve st_act pt_done pt_taken gs_done
            gs_taken x4r_in fin_in y_out gate_diag rs_made cf_sd cf_b
            tmp_made y_made""".split()
        S = {n: ctx.enter_context(nc.semaphore(n)) for n in sem_names}
        base = (nc.sbuf_base + 63) // 64 * 64
        top = [base]

        def at(name, offset, shape, dt=F32):
            top[0] = max(top[0], base + offset + 4 * int(np.prod(shape[1:])))
            return nc.alloc_sbuf_tensor_at(name, shape, dt, offset=base + offset)

        K1 = 1024
        raw = at("raw", 0, [P, RING, 2 * CH])
        hi = at("hi", 16 * K1, [P, RING, CH], F32R)
        lo = at("lo", 24 * K1, [P, RING, CH], F32R)
        H = 32 * K1
        Q = 96 * K1
        h1 = [at("h1_hi", H, [P, KT, L], F32R), at("h1_lo", H + 16 * K1, [P, KT, L], F32R)]
        x1 = at("x1", H + 32 * K1, [P, 2, D])
        ns1 = at("ns1", H + 48 * K1, [P, 2, D])
        uT = [at("uT_hi", Q, [P, FT, L], F32R), at("uT_lo", Q + 44 * K1, [P, FT, L], F32R)]
        ub = at("ub", Q + 88 * K1, [P, 2, CH])
        tm1 = at("tm1", Q + 92 * K1, [P, 2, CH])
        rowb = at("rowb", Q + 104 * K1, [4, CH])
        proj = at("proj", Q, [P, 2, D_IN])
        qkT = at("qkT", Q + 36 * K1, [P, 26, L])
        rt = at("rt", Q + 62 * K1, [P, 2, 2048])
        pr1 = at("pr1", Q + 78 * K1, [P, 2, 2, L])
        pt1 = at("pt1", Q + 82 * K1, [P, 2, 2, L])
        ob = at("ob", Q + 86 * K1, [P, 2, L])
        ropa = at("ropa", Q + 96 * K1, [P, 2, 2, P])
        ropb = at("ropb", Q + 98 * K1, [P, 2, 2, 32])
        gbc = at("gbc", Q + 99 * K1, [P, 4, P])
        lamv = at("lamv", Q + 101 * K1, [P, 4, P])
        sub_bc = at("sub_bc", Q + 103 * K1, [P, L])
        ogain = at("ogain", Q + 64 * K1, [P, D])
        hT = [at("hT_hi", H, [P, KT, 2 * L], F32R), at("hT_lo", H + 32 * K1, [P, KT, 2 * L], F32R)]
        x4 = at("x4", Q, [P, 4, D])
        tm2 = at("tm2", Q + 32 * K1, [P, 2, CH])
        ns2 = at("ns2", Q + 40 * K1, [P, 2, D])
        qkvg = at("qkvg", Q, [P, 4, 4, 2 * CH])
        ca = at("ca", Q, [P, 5, 4, CH])
        pmat = at("pmat", Q + 40 * K1, [P, 2, 4, L])
        wpool = at("wpool", Q + 48 * K1, [P, 4, P])
        psc = at("psc", Q + 50 * K1, [P, CH])
        pdT = at("pdT", Q + 52 * K1, [P, 4, 2 * L])
        gatb = at("gatb", Q + 48 * K1, [P, 2, D])
        fgain = at("fgain", Q + 32 * K1, [P, D])
        yT = at("yT", Q + 64 * K1, [P, 4, 2, YW])
        cv = at("cv", Q + 73 * K1, [P, 4, 2 * L])
        ya = at("ya", Q + 83 * K1, [P, 4, CH])
        gC = at("gC", Q + 91 * K1, [P, 4, CH])
        dg = at("dg", Q + 83 * K1, [P, 2, CH])
        st = at("st", H, [P, 8, P])
        T = at("T", H + 4 * K1, [P, 2 * CH])
        pr = at("pr", H + 8 * K1, [P, 2, CH])
        pt = at("pt", H + 12 * K1, [P, 2, CH])
        ropn = at("ropn", H + 16 * K1, [P, 2, 2, P])
        rn = at("rn", H + 18 * K1, [P, 2, 2, P])
        mask = at("mask", H + 20 * K1, [P, GRID])
        turn = at("turn", H + 20 * K1 + 256, [P, P])
        zb = at("zb", H + 32 * K1, [P, 2, CH])
        sT = at("sT", H + 36 * K1, [P, 2, CH])
        cpw = at("cpw", H + 24 * K1, [P, 4, CH])
        cpb = at("cpb", H + 22 * K1, [1, CH])
        bias = at("bias", H + 40 * K1, [P, NA_H, 6 * GRID])
        small = [Q + 106 * K1]

        def keep(name, shape, dt=F32):
            t = at(name, small[0], shape, dt)
            small[0] += (4 * int(np.prod(shape[1:])) + 31) // 32 * 32
            return t

        ident = keep("ident", [P, P])
        NV = 5 * KT + 2 * KT
        vec = keep("vec", [P, NV])
        bmod = keep("bmod", [P, 96])
        cvec = keep("cvec", [P, 24])
        dw = keep("dw", [P, 2, 128])
        cT = keep("cT", [P, KT, 2])
        c_in = keep("c_in", [P, KT, 4], F32R)
        sel = keep("sel", [4, 2])
        modT = keep("modT", [P, 96, 2])
        mA = keep("mA", [P, 2, KT])
        mB = keep("mB", [P, 2, KT])
        mG = keep("mG", [P, 2, KT])
        ss = keep("ss", [P, 4])
        rs = keep("rs", [P, 4])
        sd = keep("sd", [P, 4])
        qss = keep("qss", [P, 2, 26])
        qsd = keep("qsd", [P, 2, 26])
        lam = keep("lam", [P, 8])
        mx = keep("mx", [P, 2, 2])
        nm = keep("nm", [P, 2, 2])
        sm = keep("sm", [P, 2, 2])
        rr = keep("rr", [P, 2, 2])
        bn = keep("bn", [P, 6])
        mv = keep("mv", [P, 4])
        ones = keep("ones", [P, P])
        vrow = at("vrow", Q, [NV, P])
        brow = at("brow", Q + 512, [120, P])
        drow = at("drow", Q + 1024, [124, 2, P])
        assert top[0] <= nc.sbuf_usable_end, top[0] - nc.sbuf_usable_end

        acc = [ctx.enter_context(nc.psum_tensor(f"acc{i}", [P, CH], F32)) for i in range(4)]
        tp = [ctx.enter_context(nc.psum_tensor(f"tp{i}", [P, CH], F32)) for i in range(2)]
        cg = [ctx.enter_context(nc.psum_tensor(f"cg{i}", [P, CH], F32)) for i in range(2)]

        phases = {}
        total = [0, 0, 0]

        def phase(name, pieces, taken, groups):
            phases[name] = Phase(*total)
            for k, n in enumerate((pieces, taken, groups)):
                total[k] += n

        def mixed(nw, nm):
            order, every = [], nw // nm if nm else nw + 1
            for k in range(nw):
                order.append(("w", k))
                if k % every == 0 and k // every < nm:
                    order.append(("m", k // every))
            return order

        GATE_UP, DOWN_MOD, DOWN = mixed(8, 4), mixed(22, 4), mixed(22, 0)

        def row_at(order):
            return 4 * order.index(("m", 3)) + 4

        FC = DFF // CH
        phase("n1", 0, 0, 8)
        phase("g1", FC * 48, FC * 2, 2 * FC)
        phase("d1", 2 * 104, 8, 0)
        phase("n2", 0, 0, 8)
        phase("i1", 9 * 16, 18, 0)
        phase("at1", 0, 0, A_HEADS + B_HEADS)
        phase("o1", 4 * 16, 8, 0)
        phase("n3", 0, 0, 8)
        phase("g2", FC * 48, FC * 2, 2 * FC)
        phase("d2", 2 * 88, 8, 0)
        SEGS = [[(nm_, 2 * k, 2, 4) for k, nm_ in enumerate("qkvg")],
                [("q", 0, 2, 2), ("k", 2, 2, 4), ("v", 4, 2, 4), ("g", 6, 2, 2)]]
        NT = [4, 2]
        for ly in range(2):
            phase(f"n4{ly}", 0, 0, 16)
            phase(f"ca{ly}", 5 * 16, 5 * NT[ly], 0)
            for nm_, _, n, nt in SEGS[ly]:
                phase(f"s{ly}{nm_}", n * 16, n * nt, 0)
            phase(f"mx{ly}", 0, 0, 4 * NT[ly])
            phase(f"o2{ly}", 4 * 16, 4 * NT[ly], 0)
        phase("end", 0, 0, 0)
        PIECES = total[0]

        class Link:

            def __init__(self, eng, sem):
                self.eng, self.sem, self.n, self.lap, self.per = eng, sem, 0, None, 0

            def __call__(self, ins):
                self.n += 1
                ins.then_inc(self.sem, 1)
                self.eng.wait_ge(self.sem, self.n if self.lap is None else self.n + self.lap * self.per)

            def start(self, lap, per):
                self.lap, self.per, self.was = lap, per, self.n

            def stop(self, laps):
                assert self.n - self.was == self.per, (self.n - self.was, self.per)
                self.n += self.per * (laps - 1)
                self.lap = None

        def wait(eng, name, value):
            if not isinstance(value, int) or value > 0:
                eng.wait_ge(S[name], value)

        def place(j):
            m, q = divmod(j, 4)
            return 2 * m + q % 2, q // 2

        def raw_piece(j):
            u, half = place(j)
            return raw[:, u % RING, half * CH:(half + 1) * CH]

        def hi_piece(act, p0, j):
            u, half = place(j)
            if half == 0:
                loads = (p0 // 8 + j // 8 + 1) * 16 if isinstance(p0, int) else \
                    At(p0.base // 8 * 16 + j // 8 * 16 + 16, p0.per * 2, p0.lap).value()
                act.wait_ge(S[f"raw{u % RING}"], loads)
            wait(act, "pieces_used", num(p0 + (j - RING + 1)))
            act.activation(hi[:, j % RING, :], raw_piece(j), ACT.Copy).then_inc(S["hi_made"], 1)

        def lo_piece(dve, p0, j):
            wait(dve, "hi_made", num(p0 + (j + 1)))
            dve.tensor_tensor(lo[:, j % RING, :], raw_piece(j), hi[:, j % RING, :].bitcast(F32),
                              ALU.subtract).then_inc(S["lo_made"], 1)

        class At:

            def __init__(self, base, per, lap):
                self.base, self.per, self.lap = base, per, lap

            def __add__(self, n):
                return At(self.base + n, self.per, self.lap)

            def __sub__(self, n):
                return At(self.base - n, self.per, self.lap)

            def value(self):
                return self.lap * self.per + self.base

        def num(v):
            return v.value() if isinstance(v, At) else v

        def mm3(pe, bank, act_hi, act_lo, slot, start, stop):
            pe.matmul(bank, act_hi, hi[:, slot, :], start=start, stop=False)
            pe.matmul(bank, act_lo, hi[:, slot, :], start=False, stop=False)
            return pe.matmul(bank, act_hi, lo[:, slot, :], start=False, stop=stop)

        def chunk_pieces(pe, src, nt, p0, taken, js):
            for j in js:
                u, half = place(j)
                kt = 2 * u + half
                pe.wait_ge(S["lo_made"], num(p0 + (j + 1)))
                for t in range(nt):
                    if j == 0:
                        wait(pe, "acc_taken", num(taken + (t + 1 - nt)))
                    last = mm3(pe, acc[t][:], src[0][:, kt, t * P:(t + 1) * P], src[1][:, kt, t * P:(t + 1) * P],
                               j % RING, j == 0, j == 15)
                    if j == 15 and t < nt - 1:
                        last.then_inc(S["acc_done"], 1)
                last.then_inc(S["pieces_used"], 1)

        def mod_piece(pe, p0, j, jm, row):
            u, half = place(jm)
            kt = 2 * u + half
            pe.wait_ge(S["lo_made"], num(p0 + (j + 1)))
            if kt == 0:
                wait(pe, "row_taken", num(row))
                pe.matmul(cg[0][0:4, :], c_in[:, kt, :], hi[:, j % RING, :], start=True, stop=False)
                ins = pe.matmul(cg[0][0:2, :], c_in[:, kt, 0:2], lo[:, j % RING, :], start=False, stop=False)
            else:
                pe.matmul(cg[0][0:2, :], c_in[:, kt, 0:2], lo[:, j % RING, :], start=False, stop=False)
                ins = pe.matmul(cg[0][0:4, :], c_in[:, kt, :], hi[:, j % RING, :], start=False, stop=(kt == KT - 1))
            ins.then_inc(S["pieces_used"], 1)

        def mod_turn(pe, row):
            pe.wait_ge(S["row_taken"], num(row + 1))
            for k in range(4):
                ins = pe.matmul(cg[1][:, 2 * k:2 * k + 2], rowb[:, k * P:(k + 1) * P], sel[:], start=True, stop=True)
            ins.then_inc(S["mt_done"], 1)

        def mod_row(dve, order, p0, row):
            dve.wait_ge(S["pieces_used"], num(p0 + row_at(order)))
            dve.tensor_copy(rowb[:], cg[0][0:4, :]).then_inc(S["row_taken"], 1)

        def mod_cols(dve, row, dst):
            dve.wait_ge(S["mt_done"], num(row + 1))
            dve.tensor_copy(dst, cg[1][:, 0:8].rearrange("p (k c) -> p k c", c=2)).then_inc(S["mt_taken"], 1)

        def pair_pieces(pe, order, src, nk, p0, js, bank_free, row=None):
            for j in js:
                kind, m = order[j // 4]
                jm = 4 * m + j % 4
                if kind == "m":
                    mod_piece(pe, p0, j, jm, row)
                    continue
                kt, half = place(jm)
                pe.wait_ge(S["lo_made"], num(p0 + (j + 1)))
                for t in range(2):
                    if kt == 0:
                        bank_free(half, t)
                    last = mm3(pe, acc[2 * half + t][:], src[0][:, kt, t * P:(t + 1) * P],
                               src[1][:, kt, t * P:(t + 1) * P], j % RING, kt == 0, kt == nk - 1)
                    if kt == nk - 1 and t == 0:
                        last.then_inc(S["acc_done"], 1)
                last.then_inc(S["pieces_used"], 1)

        def pair_done(eng, ph, per, lap, half, t):
            if t == 0:
                eng.wait_ge(S["acc_done"], num(lap_at(ph.done + half + 1, 2, lap)))
            else:
                eng.wait_ge(S["pieces_used"], num(lap_at(ph.pieces + per - 2 + 2 * half, per, lap)))

        def lap_at(b, per, lap):
            return b + per * lap if isinstance(lap, int) else At(b, per, lap)

        def bank_done(eng, ph, nt, lap, t):
            if t < nt - 1:
                eng.wait_ge(S["acc_done"], num(lap_at(ph.done + t + 1, nt - 1, lap)))
            else:
                eng.wait_ge(S["pieces_used"], num(lap_at(ph.pieces + 16, 16, lap)))

        def turned(ph):
            return ph.groups - (A_HEADS if ph.groups > phases["at1"].groups else 0)

        n = 0
        for name in phases:
            phases[name].done = n
            if name[0] == "i" or name == "o1":
                n += {"i": 9, "o": 4}[name[0]]
            if name[0] in "gd":
                n += 2 * {"g": FC, "d": 2}[name[0]]
            if name[:2] == "ca":
                n += 5 * (NT[int(name[2])] - 1)
            if name[0] == "s":
                seg = [s for s in SEGS[int(name[1])] if s[0] == name[2:]][0]
                n += seg[2] * (seg[3] - 1)
            if name[:2] == "o2":
                n += 4 * (NT[int(name[2])] - 1)

        def pair_cols(lap, u, off, width):
            first = lap * P + (u * P + off)
            return slice(first, first + width) if isinstance(lap, int) else bass.ds(first, width)

        def na_laps(eng, step, nt, link=None):
            U = len(kinds_of(nt))
            with eng.Fori(0, 7) as lap:
                if link:
                    link.start(lap, 2 * U + 7)
                for k in range(1, U + 1):
                    step(lap, k, 2 * U)
            if link:
                link.stop(7)
            for k in range(1, U + 1):
                step(7, k, U)

        def gu_view(w):
            return w.rearrange("o (k p) (g c n) -> o c k p g n", p=P, g=2, n=CH)[0]

        def down_view(w):
            return w.rearrange("o (k p) (c n) -> o c k p n", p=P, n=2 * CH)[0]

        def wide_view(w, ly):
            return w.rearrange("o (k j p) (c n) -> o c k p j n", j=2, p=P, n=CH)[ly]

        gu = [gu_view(a["ffn1_w_gu"]), gu_view(a["ffn2_w_gu"])]
        down = [down_view(a["ffn1_w_down"]), down_view(a["ffn2_w_down"])]
        win1, wout1 = wide_view(a["w_in"], 0), wide_view(a["w_out"], 0)
        win2 = [wide_view(a["w_in_2"], ly) for ly in range(2)]
        wout2 = [wide_view(a["w_out_2"], ly) for ly in range(2)]
        modv = [wide_view(a["w_mod_2"], ly) for ly in range(2)]
        modl = a["w_mod_2"].rearrange("l (k j p) (c n) -> l c k p j n", j=2, p=P, n=CH)
        x_v = a["x"].rearrange("o (t p) d -> p (o t) d", p=P)
        ctx_v = a["ctx_2"].rearrange("o (t p) d -> p (o t) d", p=P)
        xs_v = xs_dram.rearrange("(t p) d -> p t d", p=P)
        out_v = out.rearrange("o (t p) d -> p (o t) d", p=P)

        def row_bc(ap, n):
            return bass.AP(tensor=ap.tensor, offset=ap.offset, ap=[[0, P], [1, n]])

        def o_total(n):
            return B_HEADS + 8 * (6 if n > 0 else 0) + 8 * (4 if n > 1 else 0)

        block = ctx.enter_context(nc.Block())

        @block.sync
        def _(sp):
            def unit(p0, u, src, shape=None):
                wait(sp, "lo_made", num(p0 + (4 * (u // 2) - 5 + u % 2)))
                dst = raw[:, u % RING, :]
                if shape == "wide":
                    dst = dst.rearrange("p (j n) -> p j n", j=2)
                sp.dma_start(dst, src).then_inc(S[f"raw{u % RING}"], 16)

            def load_lap(order, p0, main, mod, shape):
                for g, (kind, m) in enumerate(order):
                    for q in range(2):
                        if kind == "w":
                            unit(p0, 2 * g + q, main(2 * m + q), shape)
                        else:
                            unit(p0, 2 * g + q, mod(2 * m + q), "wide")

            def load_gu(w, ph, wm):
                load_lap(GATE_UP, ph.pieces, lambda u: w[0, u], lambda u: wm[0, u], "wide")
                with sp.Fori(1, FC) as i:
                    load_lap(GATE_UP, At(ph.pieces, 48, i), lambda u: w[i, u], lambda u: wm[i, u], "wide")

            def load_down(w, ph, order):
                with sp.Fori(0, 2) as i:
                    load_lap(order, At(ph.pieces, 4 * len(order), i), lambda u: w[i, u], lambda u: modl[i, FC, u], None)

            def ahead(w, ph, first):
                for u in range(RING):
                    unit(ph.pieces, u, w[first, u], "wide")

            def load_wide(w, ph, first, n, begun=False):
                if begun:
                    for u in range(RING, 8):
                        unit(ph.pieces, u, w[first, u], "wide")
                with sp.Fori(int(begun), n) as i:
                    for u in range(8):
                        unit(At(ph.pieces, 16, i), u, w[i + first, u], "wide")

            sp.dma_start(x1[:], x_v).then_inc(S["x_in"], 16)
            load_gu(gu[0], phases["g1"], modv[0])
            load_down(down[0], phases["d1"], DOWN_MOD)
            load_wide(win1, phases["i1"], 0, 9)
            load_wide(wout1, phases["o1"], 0, 4)
            load_gu(gu[1], phases["g2"], modv[1])
            load_down(down[1], phases["d2"], DOWN)
            for ly in range(2):
                nt = NT[ly]
                ph = phases[f"ca{ly}"]
                ahead(win2[ly], ph, 10)
                wait(sp, "tg_lo", phases[f"ca{ly}"].groups)
                sp.dma_start(pmat[:], a["pmat"]).then_inc(S["ca_const_in"], 16)
                sp.dma_start(wpool[:], a["w_pool_2"][ly].rearrange("g c d -> c g d")).then_inc(S["ca_const_in"], 16)
                sp.dma_start(psc[:], row_bc(a["pool_scale_2"][ly], CH)).then_inc(S["ca_const_in"], 16)
                load_wide(win2[ly], ph, 10, 3, True)
                with sp.Fori(0, 2) as i:
                    for u in range(8):
                        unit(At(ph.pieces + 48, 16, i), u, win2[ly][i, u], "wide")
                for nm_, c0, n_, _ in SEGS[ly]:
                    load_wide(win2[ly], phases[f"s{ly}{nm_}"], c0 + 2, n_)
                ahead(wout2[ly], phases[f"o2{ly}"], 0)
                last = phases[f"mx{ly}"]
                sp.wait_ge(S["pieces_used"], last.pieces)
                sp.dma_start(cpw[:], a["conv_pw_2"][ly].rearrange("(k p) n -> p k n", p=P)).then_inc(S["cf_in"], 16)
                sp.dma_start(cpb[:], a["conv_pw_b_2"][ly:ly + 1, :]).then_inc(S["cf_in"], 16)
                sp.dma_start(ropn[:, 0], a["cosn"].rearrange("(t p) n -> p t n", p=P)).then_inc(S["na_in"], 16)
                sp.dma_start(ropn[:, 1], a["sinn"].rearrange("(t p) n -> p t n", p=P)).then_inc(S["na_in"], 16)
                sp.dma_start(mask[:], a["mask"]).then_inc(S["na_in"], 16)
                sp.dma_start(turn[:], a["turn"]).then_inc(S["na_in"], 16)
                rpb = a["na_rpb_2"]
                for r2 in range(2):
                    for dr in range(6):
                        first = ly * NA_H * RPB_R * RPB_C + (5 - r2 + dr) * RPB_C + RPB_C // 2 - (GRID - 1)
                        sp.dma_start(bias[r2 * GRID:(r2 + 1) * GRID, :, dr * GRID:(dr + 1) * GRID],
                                     bass.AP(tensor=rpb.tensor, offset=first,
                                             ap=[[1, GRID], [RPB_R * RPB_C, NA_H], [1, GRID]]))\
                            .then_inc(S["bias_in"], 16)
                sp.wait_ge(S["o_taken"], o_total(ly + 1))
                sp.wait_ge(S["xs_out"], 16 * (ly + 1))
                sp.dma_start(x4[:, 0:2, :], xs_v).then_inc(S["x4r_in"], 16)
                if ly == 0:
                    sp.dma_start(x4[:, 2:4, :], ctx_v).then_inc(S["x4r_in"], 16)
                load_wide(wout2[ly], phases[f"o2{ly}"], 0, 4, True)

        @block.scalar
        def _(act):
            def consts():
                act.dma_start(ident[:], a["ident"]).then_inc(S["const_in"], 16)
                act.dma_start(sel[:], a["sel"]).then_inc(S["const_in"], 16)
                act.dma_start(vrow[:], a["vrows"]).then_inc(S["const_in"], 16)
                act.dma_start(brow[0:96, :], a["b_mod_2"].rearrange("l (k p) -> (l k) p", p=P)).then_inc(S["const_in"], 16)
                for k, nm_ in enumerate(("conv_dw_b_2", "conv_ln_g_2", "conv_ln_b_2")):
                    act.dma_start(brow[96 + 8 * k:104 + 8 * k, :],
                                  a[nm_].rearrange("l (k p) -> (l k) p", p=P)).then_inc(S["const_in"], 16)
                for ly in range(2):
                    act.dma_start(drow[:, ly, :],
                                  a["conv_dw_2"][ly].rearrange("k (c p) -> (k c) p", p=P)).then_inc(S["const_in"], 16)

            def at1_consts():
                act.dma_start(ropa[:, 0], a["cosa"].rearrange("(t p) n -> p t n", p=P)).then_inc(S["rope_in"], 16)
                act.dma_start(ropa[:, 1], a["sina"].rearrange("(t p) n -> p t n", p=P)).then_inc(S["rope_in"], 16)
                act.dma_start(ropb[:, 0], a["cosb"].rearrange("(t p) n -> p t n", p=P)).then_inc(S["rope_in"], 16)
                act.dma_start(ropb[:, 1], a["sinb"].rearrange("(t p) n -> p t n", p=P)).then_inc(S["rope_in"], 16)
                for k, nm_ in enumerate(("a_q_norm", "a_k_norm", "b_q_norm", "b_k_norm")):
                    act.dma_start(gbc[:, k], row_bc(a[nm_], P)).then_inc(S["rope_in"], 16)
                for k, nm_ in enumerate(("b_lambda_q1", "b_lambda_k1", "b_lambda_q2", "b_lambda_k2")):
                    act.dma_start(lamv[:, k], row_bc(a[nm_], P)).then_inc(S["rope_in"], 16)
                act.dma_start(sub_bc[:], row_bc(a["b_subln"], L)).then_inc(S["rope_in"], 16)

            norms = [0, 0]

            def root(src_x, ns, nt, x_ready):
                x_ready()
                for t in range(nt):
                    if t >= 2:
                        act.wait_ge(S["ss_made"], norms[1] + t - 1)
                    act.activation(ns[:, t % 2], src_x[:, t], ACT.Square,
                                   accum_out=ss[:, t:t + 1]).then_inc(S["ss_made"], 1)
                norms[0] += 1
                norms[1] += nt
                act.wait_ge(S["var_made"], norms[0])
                act.activation(sd[:, 0:nt], rs[:, 0:nt], ACT.Sqrt).then_inc(S["sd_made"], 1)
                act.wait_ge(S["rs_made"], norms[0])

            def group_hi(g, dst, src):
                act.wait_ge(S["tg_full"], num(g + 1))
                act.activation(dst, src, ACT.Copy).then_inc(S["tg_hi"], 1)

            def norm(ph, src_x, ns, tm, dst, nt, x_ready):
                root(src_x, ns, nt, x_ready)

                def scale(t):
                    act.activation(ns[:, t % 2], src_x[:, t], ACT.Copy, scale=rs[:, t:t + 1]).then_inc(S["scaled"], 1)
                scale(0)
                scale(1)
                for t in range(nt):
                    for g in range(4):
                        group_hi(ph.groups + 4 * t + g, dst[0][:, 4 * g:4 * g + 4, t * P:(t + 1) * P],
                                 tm[:, g % 2].rearrange("p (k n) -> p k n", n=P))
                    if t + 2 < nt:
                        scale(t + 2)

            def gate_up(ph):
                def u_hi(c, off):
                    for f in range(2):
                        cols = slice(4 * (c + off) + 2 * f, 4 * (c + off) + 2 * f + 2) if isinstance(c, int) else \
                            bass.ds(c * 4 + (4 * off + 2 * f), 2)
                        group_hi(lap_at(ph.groups + 2 * off + f, 2, c), uT[0][:, cols, :],
                                 tm1[:, f].rearrange("p (k n) -> p k n", n=L))

                def silus(c):
                    wait(act, "tp_done", num(lap_at(turned(ph), 2, c)))
                    for t in range(2):
                        pair_done(act, ph, 48, c, 0, t)
                        act.activation(ub[:, t], acc[t][:], ACT.Silu).then_inc(S["gate_act"], 1)

                for j in range(2, 50):
                    hi_piece(act, ph.pieces, j)
                silus(0)
                with act.Fori(1, FC) as i:
                    p0 = At(ph.pieces, 48, i)
                    for j in range(2, 6):
                        hi_piece(act, p0, j)
                    u_hi(i, -1)
                    for j in range(6, 50):
                        hi_piece(act, p0, j)
                    silus(i)
                u_hi(FC - 1, 0)

            def stream(p0_of, laps, per, last=False):
                n_ = laps - 1 if last else laps
                with act.Fori(0, n_) as i:
                    for j in range(2, per + 2):
                        hi_piece(act, At(p0_of, per, i), j)
                if last:
                    for j in range(2, per):
                        hi_piece(act, p0_of + per * n_, j)

            consts()
            at1_consts()
            for j in range(2):
                hi_piece(act, 0, j)
            norm(phases["n1"], x1, ns1, tm1, h1, 2, lambda: act.wait_ge(S["x_in"], 16))
            act.wait_ge(S["cols_taken"], 7)
            act.activation(cT[:].rearrange("p k c -> p c k"), vec[:, 5 * KT:7 * KT].rearrange("p (c k) -> p c k", c=2),
                           ACT.Silu).then_inc(S["silu_c"], 1)
            act.wait_ge(S["silu_c"], 1)
            act.activation(c_in[:, :, 0:2], cT[:], ACT.Copy).then_inc(S["silu_c"], 1)
            gate_up(phases["g1"])
            stream(phases["d1"].pieces, 2, 4 * len(DOWN_MOD))
            norm(phases["n2"], x1, ns1, tm1, h1, 2, lambda: act.wait_ge(S["acc_taken"], phases["n2"].taken))
            stream(phases["i1"].pieces, 9, 16)

            g0 = phases["at1"].groups
            act.wait_ge(S["lam_e"], 1)
            act.activation(lam[:, 2:4], lam[:, 0:2], ACT.Exp).then_inc(S["lam_e"], 1)
            act.wait_ge(S["qk_ss"], 1)
            act.activation(qsd[:], qss[:], ACT.Sqrt).then_inc(S["qk_sd"], 1)
            for g in range(13):
                act.wait_ge(S["cg_done"], g + 1)
                act.activation(qkT[:, 2 * g:2 * g + 2, :], cg[g % 2][:].rearrange("p (k n) -> p k n", n=L),
                               ACT.Copy).then_inc(S["cg_taken"], 1)

            def exps(q):
                act.wait_ge(S["m_ready"], q + 1)
                if q >= 2:
                    act.wait_ge(S["cg_done"], 13 + (q - 1 if q - 2 < 8 else 8 + (q - 8) // 2))
                for t in range(2):
                    ins = act.activation(pr1[:, q % 2, t], acc[q % 2][:, t * L:(t + 1) * L], ACT.Exp,
                                         bias=nm[:, q % 2, t:t + 1], scale=SCALE, accum_out=sm[:, q % 2, t:t + 1])
                ins.then_inc(S["p_made"], 1)

            def pt_copy(k):
                act.wait_ge(S["cg_done"], 14 + k)
                if k >= 2:
                    act.wait_ge(S["o_done"], k - 1)
                act.activation(pt1[:, k % 2], cg[(13 + k) % 2][:].rearrange("p (k n) -> p k n", n=L),
                               ACT.Copy).then_inc(S["cg_taken"], 1)

            exps(0)
            for q in range(8):
                exps(q + 1)
                pt_copy(q)
                group_hi(g0 + q, h1[0][:, q, :], tm1[:, q % 2, 0:L])
            for h in range(B_HEADS):
                exps(9 + 2 * h)
                pt_copy(8 + h)
                if h + 1 < B_HEADS:
                    exps(10 + 2 * h)
                act.wait_ge(S["ob_made"], 2 * h + 1)
                act.activation(lam[:, 6:8], lam[:, 4:6], ACT.Sqrt).then_inc(S["qk_sd"], 1)
                group_hi(g0 + 8 + h, h1[0][:, 8 + 2 * h:10 + 2 * h, :], tm1[:, h % 2].rearrange("p (k n) -> p k n", n=L))
            stream(phases["o1"].pieces, 4, 16)
            norm(phases["n3"], x1, ns1, tm1, h1, 2, lambda: act.wait_ge(S["acc_taken"], phases["n3"].taken))
            gate_up(phases["g2"])
            stream(phases["d2"].pieces, 2, 88)
            root(x1, ns1, 2, lambda: act.wait_ge(S["acc_taken"], phases["n40"].taken))
            units = 0
            cgs = 13 + 12
            for ly in range(2):
                nt = NT[ly]

                def x_ready(ly=ly):
                    if ly == 0:
                        act.wait_ge(S["x4_in"], 2)
                        act.wait_ge(S["ctx_in"], 16)
                    else:
                        act.wait_ge(S["acc_taken"], phases["n41"].taken)
                norm(phases[f"n4{ly}"], x4, ns2, tm2, hT, 4, x_ready)
                stream(phases[f"ca{ly}"].pieces, 5, 16)
                act.wait_ge(S["acc_taken"], phases[f"ca{ly}"].taken + 5 * nt)
                act.activation(ca[:, 1, 0:nt], ca[:, 1, 0:nt], ACT.Sigmoid).then_inc(S["gates_made"], 1)
                act.activation(gC[:, 0:nt], ca[:, 2, 0:nt], ACT.Silu).then_inc(S["gates_made"], 1)
                act.activation(ca[:, 4, 0:nt], ca[:, 4, 0:nt], ACT.Silu).then_inc(S["gates_made"], 1)
                act.wait_ge(S["pad_made"], ly + 1)
                for c in range(4):
                    act.wait_ge(S["yt_done"], 4 * ly + c + 1)
                    act.activation(yT[:, c, 0:nt // 2, PAD:PAD + L],
                                   tp[c % 2][:, 0:nt * P].rearrange("p (s n) -> p s n", n=L),
                                   ACT.Copy).then_inc(S["yt_taken"], 1)
                for g in range(4):
                    act.wait_ge(S["pl_done"], 4 * ly + g + 1)
                    act.activation(pdT[:, g, 0:nt * P], cg[g % 2][:, 0:nt * P], ACT.Copy).then_inc(S["pl_taken"], 1)
                for nm_, _, n_, _ in SEGS[ly]:
                    stream(phases[f"s{ly}{nm_}"].pieces, n_, 16)

                for t in range(nt):
                    k = (4 if ly else 0) + t
                    act.wait_ge(S["z_made"], 2 * k + 1)
                    act.activation(mv[:, 3:4], mv[:, 2:3], ACT.Sqrt).then_inc(S["cf_sd"], 1)
                    act.wait_ge(S["cz_done"], k + 1)
                    if t >= 2:
                        act.wait_ge(S["pw_done"], k - 1)
                    for c in range(4):
                        ins = act.activation(sT[:, t % 2, c * P:(c + 1) * P], cg[t % 2][:, c * P:(c + 1) * P], ACT.Silu,
                                             scale=cvec[:, 8 + 4 * ly + c:9 + 4 * ly + c],
                                             bias=cvec[:, 16 + 4 * ly + c:17 + 4 * ly + c])
                    ins.then_inc(S["s_made"], 1)

                act.wait_ge(S["acc_taken"], phases[f"mx{ly}"].taken)
                act.activation(qkvg[:, 3, 0:nt], qkvg[:, 3, 0:nt], ACT.Silu).then_inc(S["gates_made"], 1)
                U = 6 if nt == 4 else 4
                u0, kinds = units, kinds_of(nt)
                def stage_ctx(lap, n):
                    act.wait_ge(S["cg_done"], lap * 2 + (cgs + 2 * n))
                    cols = pair_cols(lap, n, 0, P)
                    ins = act.activation(st[:, 4:6], qkvg[:, 1, 2:4, cols], ACT.Copy)
                    if nt == 4:
                        ins = act.activation(st[:, 6:8], qkvg[:, 0, 2:4, cols], ACT.Copy)
                    ins.then_inc(S["st_act"], 1)

                def take_k(lap, n):
                    act.wait_ge(S["cg_done"], lap * 2 + (cgs + 2 * n + 2))
                    act.activation(T[:, CH:2 * CH], cg[1][:], ACT.Copy).then_inc(S["cg_taken"], 1)

                def na_exp(lap, u):
                    act.wait_ge(S["m_ready"], lap * U + (16 + u0 + u + 1))
                    if kinds[u % U][1] < 2:
                        act.activation(pr[:, u % 2], acc[u % 2][:], ACT.Exp, bias=nm[:, u % 2, 0:1],
                                       accum_out=sm[:, u % 2, 0:1]).then_inc(S["p_made"], 1)
                    else:
                        for t in range(2):
                            ins = act.activation(pr[:, u % 2, t * L:(t + 1) * L], acc[u % 2][:, t * L:(t + 1) * L],
                                                 ACT.Exp, bias=nm[:, u % 2, t:t + 1],
                                                 accum_out=sm[:, u % 2, t:t + 1])
                        ins.then_inc(S["p_made"], 1)

                def na_pt(lap, u):
                    act.wait_ge(S["pt_done"], lap * U + (u0 + u + 1))
                    act.wait_ge(S["o_done"], lap * U + (12 + max(u0 + u - 1, 0)))
                    act.activation(pt[:, u % 2], tp[u % 2][:], ACT.Copy).then_inc(S["pt_taken"], 1)

                def step(lap, k, end):
                    if k == 1 and end > U:
                        stage_ctx(lap, 1)
                    if k + 1 < end:
                        na_exp(lap, k + 1)
                    if k == U - 2 and end > U:
                        take_k(lap, 1)
                    if k < end:
                        na_pt(lap, k)

                stage_ctx(0, 0)
                take_k(0, 0)
                na_exp(0, 0)
                na_exp(0, 1)
                na_pt(0, 0)
                na_laps(act, step, nt)
                units += 8 * U
                cgs += 16
                g0 = phases[f"mx{ly}"].groups
                for t in range(nt):
                    for g in range(4):
                        group_hi(g0 + 4 * t + g, hT[0][:, 4 * g:4 * g + 4, t * P:(t + 1) * P],
                                 tm2[:, g % 2].rearrange("p (k n) -> p k n", n=P))
                for k in range(2 * nt):
                    act.wait_ge(S["gs_done"], 8 * ly + k + 1)
                    act.activation(gatb[:, k // 4, k % 4 * CH:(k % 4 + 1) * CH], cg[k % 2][:],
                                   ACT.Copy).then_inc(S["gs_taken"], 1)
                stream(phases[f"o2{ly}"].pieces, 4, 16, last=ly == 1)
            root(x4, ns2, 2, lambda: act.wait_ge(S["acc_taken"], phases["end"].taken))
            act.wait_ge(S["y_made"], 1)
            act.dma_start(out_v, x4[:, 0:2, :]).then_inc(S["y_out"], 16)
            act.wait_ge(S["y_out"], 16)

        @block.vector
        def _(dve):
            link = Link(dve, S["dve_step"])
            norms = [0, 0]

            def var_root(nt):
                norms[0] += 1
                norms[1] += nt
                dve.wait_ge(S["ss_made"], norms[1])
                dve.tensor_scalar(rs[:, 0:nt], ss[:, 0:nt], 1.0 / D, EPS, ALU.mult, ALU.add).then_inc(S["var_made"], 1)
                dve.wait_ge(S["sd_made"], norms[0])
                dve.reciprocal(rs[:, 0:nt], sd[:, 0:nt]).then_inc(S["rs_made"], 1)

            def group_lo(g, dst, dst_hi, src):
                dve.wait_ge(S["tg_hi"], num(g + 1))
                dve.tensor_tensor(dst, src, dst_hi, ALU.subtract).then_inc(S["tg_lo"], 1)

            def take(turns, g, k, tm, gain, shift):
                dve.wait_ge(S["tp_done"], turns)
                wait(dve, "tg_lo", g - 1)
                src = tp[k % 2][:].rearrange("p (k n) -> p k n", n=P)
                tv = tm[:, k % 2].rearrange("p (k n) -> p k n", n=P)
                if gain is None:
                    dve.tensor_copy(tv, src).then_inc(S["tg_full"], 1)
                    return
                ins = dve.tensor_tensor(tv, src, gain[:, 4 * k:4 * k + 4].unsqueeze(2).broadcast_to([P, 4, P]), ALU.mult)
                if shift is not None:
                    link(ins)
                    ins = dve.tensor_tensor(tv, tv, shift[:, 4 * k:4 * k + 4].unsqueeze(2).broadcast_to([P, 4, P]), ALU.add)
                ins.then_inc(S["tg_full"], 1)

            def groups(ph, nt, tm, dst, gain_of):
                g0 = ph.groups

                def rest(m):
                    t, k = divmod(m, 4)
                    s = slice(4 * k, 4 * k + 4)
                    group_lo(g0 + m, dst[1][:, s, t * P:(t + 1) * P], dst[0][:, s, t * P:(t + 1) * P].bitcast(F32),
                             tm[:, k % 2].rearrange("p (k n) -> p k n", n=P))
                for m in range(4 * nt):
                    t, k = divmod(m, 4)
                    take(turned(ph) + m + 1, g0 + m, k, tm, *gain_of(t))
                    if m:
                        rest(m - 1)
                rest(4 * nt - 1)

            def norm(ph, tm, dst, nt, gain_of):
                var_root(nt)
                groups(ph, nt, tm, dst, gain_of)

            def gate_up(ph, gates, ly, rows):
                def u_split(c, off):
                    for f in range(2):
                        dve.wait_ge(S["tp_done"], num(lap_at(turned(ph) + 2 * off + f + 1, 2, c)))
                        dve.wait_ge(S["tg_lo"], num(lap_at(ph.groups + 2 * off + f - 1, 2, c)))
                        dve.tensor_copy(tm1[:, f], tp[f][:]).then_inc(S["tg_full"], 1)
                    for f in range(2):
                        cols = slice(4 * (c + off) + 2 * f, 4 * (c + off) + 2 * f + 2) if isinstance(c, int) else \
                            bass.ds(c * 4 + (4 * off + 2 * f), 2)
                        group_lo(lap_at(ph.groups + 2 * off + f, 2, c), uT[1][:, cols, :],
                                 uT[0][:, cols, :].bitcast(F32), tm1[:, f].rearrange("p (k n) -> p k n", n=L))
                    first = 48 * ly + 4 * off
                    mod_cols(dve, lap_at(rows + off, 1, c), modT[:, first + 4 * c:first + 4 * c + 4, :]
                             if isinstance(c, int) else modT[:, bass.ds(c * 4 + first, 4), :])

                def products(c):
                    for t in range(2):
                        dve.wait_ge(S["gate_act"], num(lap_at(gates + t + 1, 2, c)))
                        pair_done(dve, ph, 48, c, 1, t)
                        dve.tensor_tensor(ub[:, t], ub[:, t], acc[2 + t][:], ALU.mult).then_inc(S["acc_taken"], 1)
                    mod_row(dve, GATE_UP, lap_at(ph.pieces, 48, c), lap_at(rows, 1, c))

                for j in range(2, 50):
                    lo_piece(dve, ph.pieces, j)
                products(0)
                with dve.Fori(1, FC) as i:
                    p0 = At(ph.pieces, 48, i)
                    for j in range(2, 6):
                        lo_piece(dve, p0, j)
                    u_split(i, -1)
                    for j in range(6, 50):
                        lo_piece(dve, p0, j)
                    products(i)
                u_split(FC - 1, 0)

            def down_proj(ph, order):
                per = 4 * len(order)
                with dve.Fori(0, 2) as i:
                    p0 = At(ph.pieces, per, i)
                    for j in range(2, per + 2):
                        lo_piece(dve, p0, j)
                    if order is DOWN_MOD:
                        mod_row(dve, order, p0, At(FC, 1, i))
                    for b in range(4):
                        pair_done(dve, ph, per, i, b // 2, b % 2)
                        xv = x1[:, b % 2, bass.ds(i * (2 * CH) + b // 2 * CH, CH)]
                        dve.scalar_tensor_tensor(out=xv, in0=acc[b][:], scalar=0.5, in1=xv, op0=ALU.mult,
                                                 op1=ALU.add).then_inc(S["acc_taken"], 1)
                    if order is DOWN_MOD:
                        mod_cols(dve, At(FC, 1, i), modT[:, bass.ds(i * 48 + 4 * FC, 4), :])

            def stream(ph, laps, nt, evac, last=False, extra=None):
                n_ = laps - 1 if last else laps

                def one(i, ahead):
                    for j in range(2, 18 if ahead else 16):
                        lo_piece(dve, At(ph.pieces, 16, i) if not isinstance(i, int) else ph.pieces + 16 * i, j)
                        if extra:
                            extra(i, j - 2)
                    for t in range(nt):
                        bank_done(dve, ph, nt, i, t)
                        evac(i, t)
                with dve.Fori(0, n_) as i:
                    one(i, True)
                if last:
                    one(n_, False)

            dve.memset(ones[:], 1.0).then_inc(S["cols_taken"], 1)
            dve.memset(dw[:], 0.0).then_inc(S["cols_taken"], 1)
            dve.wait_ge(S["cols_taken"], 2)
            for k, (dst, c0, c1) in enumerate(((vec[:], 0, NV), (bmod[:], 0, 96), (cvec[:], 96, 120),
                                               (dw[:, 0, 0:124], 0, 124), (dw[:, 1, 0:124], 0, 124))):
                bank = acc[(0, 1, 1, 2, 3)[k]]
                dve.wait_ge(S["cols_made"], (1, 2, 2, 3, 4)[k])
                dve.tensor_copy(dst, bank[:, c0:c1]).then_inc(S["cols_taken"], 1)
            for j in range(2):
                lo_piece(dve, 0, j)
            dve.wait_ge(S["cols_taken"], 7)
            norm(phases["n1"], tm1, h1, 2, lambda t: (vec[:, 0:KT], None))
            dve.wait_ge(S["silu_c"], 2)
            dve.tensor_tensor(c_in[:, :, 2:4], cT[:], c_in[:, :, 0:2].bitcast(F32), ALU.subtract).then_inc(S["c_split"], 1)
            gate_up(phases["g1"], 0, 0, 0)
            down_proj(phases["d1"], DOWN_MOD)
            norm(phases["n2"], tm1, h1, 2, lambda t: (vec[:, KT:2 * KT], None))

            def proj_take(i, t):
                dve.tensor_copy(proj[:, t, bass.ds(i * CH, CH)], acc[t][:]).then_inc(S["acc_taken"], 1)
            stream(phases["i1"], 9, 2, proj_take)

            dve.wait_ge(S["rope_in"], 16 * 13)
            for k in range(2):
                ins = dve.tensor_tensor_reduce(rt[:, 0, 0:P], lamv[:, 2 * k], lamv[:, 2 * k + 1], 1.0, 0.0, ALU.mult,
                                               ALU.add, lam[:, k:k + 1])
                if k == 0:
                    link(ins)
            ins.then_inc(S["lam_e"], 1)
            dve.wait_ge(S["lam_e"], 1)
            dve.wait_ge(S["acc_taken"], phases["at1"].taken)
            parts = ((0, 10, 0), (B_COL, 16, 10))
            for t in range(2):
                for c0, nh, s0 in parts:
                    xv = proj[:, t, c0:c0 + nh * HD].rearrange("p (h d) -> p h d", d=HD)
                    sq = rt[:, 0, 0:nh * HD].rearrange("p (h d) -> p h d", d=HD)
                    link(dve.tensor_tensor(sq, xv, xv, ALU.mult))
                    link(dve.tensor_reduce(qss[:, t, s0:s0 + nh], sq, AX, ALU.add))
            dve.tensor_scalar(qss[:], qss[:], 1.0 / HD, EPS, ALU.mult, ALU.add).then_inc(S["qk_ss"], 1)
            dve.wait_ge(S["qk_sd"], 1)
            link(dve.reciprocal(qsd[:], qsd[:]))
            for t in range(2):
                for c0, nh, s0 in parts:
                    xv = proj[:, t, c0:c0 + nh * HD].rearrange("p (h d) -> p h d", d=HD)
                    link(dve.tensor_tensor(xv, xv, qsd[:, t, s0:s0 + nh].unsqueeze(2).broadcast_to([P, nh, HD]), ALU.mult))
                    nq = 8
                    for k, (ha, hb) in enumerate(((0, nq), (nq, nh))):
                        g = gbc[:, (0 if s0 == 0 else 2) + k].unsqueeze(1).broadcast_to([P, hb - ha, HD])
                        link(dve.tensor_tensor(xv[:, ha:hb], xv[:, ha:hb], g, ALU.mult))
                    w = HD if s0 == 0 else 32
                    nb, half = (2, 32) if s0 == 0 else (1, 16)
                    cs = ropa if s0 == 0 else ropb
                    r1 = rt[:, 0, 0:nh * w].rearrange("p (h d) -> p h d", d=w)
                    r2 = rt[:, 1, 0:nh * w].rearrange("p (h d) -> p h d", d=w)
                    xw = xv[:, :, 0:w]
                    link(dve.tensor_tensor(r1, xw, cs[:, 0, t].unsqueeze(1).broadcast_to([P, nh, w]), ALU.mult))
                    for blk in range(nb):
                        for s in range(2):
                            d0 = blk * 2 * half + s * half
                            s1 = blk * 2 * half + (1 - s) * half
                            link(dve.tensor_tensor(r2[:, :, d0:d0 + half], xw[:, :, s1:s1 + half],
                                                   cs[:, 1, t, d0:d0 + half].unsqueeze(1).broadcast_to([P, nh, half]),
                                                   ALU.mult))
                    ins = dve.tensor_tensor(xw, r1, r2, ALU.add)
                    if (t, s0) == (1, 10):
                        ins.then_inc(S["roped"], 1)
                    else:
                        link(ins)
            dve.wait_ge(S["lam_e"], 2)
            link(dve.tensor_tensor(lam[:, 0:1], lam[:, 3:4], lam[:, 2:3], ALU.subtract))
            link(dve.tensor_scalar(lam[:, 0:1], lam[:, 0:1], LAMBDA_INIT, None, ALU.subtract))

            def maxes(q):
                dve.wait_ge(S["s_done"], q + 1)
                link(dve.tensor_reduce(mx[:, q % 2], acc[q % 2][:].rearrange("p (t n) -> p t n", n=L), AX, ALU.max))
                dve.tensor_scalar(nm[:, q % 2], mx[:, q % 2], -SCALE, None, ALU.mult).then_inc(S["m_ready"], 1)

            g0 = phases["at1"].groups
            maxes(0)
            for q in range(8):
                maxes(q + 1)
                dve.wait_ge(S["p_made"], q + 1)
                link(dve.reciprocal(rr[:, q % 2], sm[:, q % 2]))
                dve.tensor_tensor(pr1[:, q % 2], pr1[:, q % 2], rr[:, q % 2].unsqueeze(2).broadcast_to([P, 2, L]),
                                  ALU.mult).then_inc(S["pn_made"], 1)
                dve.wait_ge(S["o_done"], q + 1)
                dve.wait_ge(S["tg_lo"], g0 + q - 1)
                dve.tensor_copy(tm1[:, q % 2, 0:L], acc[2 + q % 2][:, 0:L]).then_inc(S["tg_full"], 1)
                group_lo(g0 + q, h1[1][:, q], h1[0][:, q].bitcast(F32), tm1[:, q % 2, 0:L])
            for h in range(B_HEADS):
                maxes(9 + 2 * h)
                dve.wait_ge(S["p_made"], 10 + 2 * h)
                link(dve.reciprocal(rr[:], sm[:]))
                link(dve.tensor_scalar(rr[:, 1], rr[:, 1], lam[:, 0:1], None, ALU.mult))
                for t in range(2):
                    link(dve.tensor_scalar(pr1[:, 1, t], pr1[:, 1, t], rr[:, 1, t:t + 1], None, ALU.mult))
                    ins = dve.scalar_tensor_tensor(out=pr1[:, 0, t], in0=pr1[:, 0, t], scalar=rr[:, 0, t:t + 1],
                                                   in1=pr1[:, 1, t], op0=ALU.mult, op1=ALU.add)
                    if t == 0:
                        link(ins)
                ins.then_inc(S["pn_made"], 1)
                if h + 1 < B_HEADS:
                    maxes(10 + 2 * h)
                dve.wait_ge(S["o_done"], 9 + h)
                dve.tensor_copy(ob[:], acc[2 + h % 2][:].rearrange("p (t n) -> p t n", n=L)).then_inc(S["o_taken"], 1)
                dve.wait_ge(S["o_taken"], h + 1)
                for t in range(2):
                    link(dve.tensor_tensor_reduce(rt[:, 0, 0:L], ob[:, t], ob[:, t], 1.0, 0.0, ALU.mult, ALU.add,
                                                  lam[:, 4 + t:5 + t]))
                dve.tensor_scalar(lam[:, 4:6], lam[:, 4:6], 1.0 / L, EPS, ALU.mult, ALU.add).then_inc(S["ob_made"], 1)
                dve.wait_ge(S["qk_sd"], 2 + h)
                link(dve.reciprocal(lam[:, 6:8], lam[:, 6:8]))
                for t in range(2):
                    link(dve.tensor_scalar(ob[:, t], ob[:, t], lam[:, 6 + t:7 + t], None, ALU.mult))
                dve.scalar_tensor_tensor(out=ob[:], in0=ob[:], scalar=1.0 - LAMBDA_INIT,
                                         in1=sub_bc[:].unsqueeze(1).broadcast_to([P, 2, L]), op0=ALU.mult,
                                         op1=ALU.mult).then_inc(S["ob_made"], 1)
                dve.wait_ge(S["tp_done"], g0 + h + 1)
                dve.wait_ge(S["tg_lo"], g0 + 8 + h - 1)
                dve.tensor_copy(tm1[:, h % 2], tp[h % 2][:]).then_inc(S["tg_full"], 1)
                ks = slice(8 + 2 * h, 10 + 2 * h)
                group_lo(g0 + 8 + h, h1[1][:, ks, :], h1[0][:, ks, :].bitcast(F32),
                         tm1[:, h % 2].rearrange("p (k n) -> p k n", n=L))

            def x_add(i, t):
                xv = x1[:, t, bass.ds(i * CH, CH)]
                dve.tensor_tensor(xv, acc[t][:], xv, ALU.add).then_inc(S["acc_taken"], 1)
            stream(phases["o1"], 4, 2, x_add)
            norm(phases["n3"], tm1, h1, 2, lambda t: (vec[:, 2 * KT:3 * KT], None))
            gate_up(phases["g2"], 2 * FC, 1, FC + 2)
            down_proj(phases["d2"], DOWN)
            var_root(2)
            dve.wait_ge(S["rs_made"], norms[0])
            dve.wait_ge(S["fin_in"], 16)
            for t in range(2):
                dve.scalar_tensor_tensor(out=x4[:, t], in0=x1[:, t], scalar=rs[:, t:t + 1], in1=ogain[:], op0=ALU.mult,
                                         op1=ALU.mult).then_inc(S["x4_in"], 1)

            units, convs = 0, 0
            ca_taken = 0
            for ly in range(2):
                nt = NT[ly]
                dve.wait_ge(S["mt_taken"], 24)
                for c in range(2):
                    b0 = 48 * ly
                    mod = modT[:, b0:b0 + 48, c]
                    link(dve.tensor_tensor(mB[:, c], mod[:, 0:KT], bmod[:, b0:b0 + KT], ALU.add))
                    link(dve.tensor_tensor(mG[:, c], mod[:, 2 * KT:3 * KT], bmod[:, b0 + 2 * KT:b0 + 3 * KT], ALU.add))
                    link(dve.tensor_tensor(mA[:, c], mod[:, KT:2 * KT], bmod[:, b0 + KT:b0 + 2 * KT], ALU.add))
                    link(dve.scalar_tensor_tensor(out=mA[:, c], in0=mA[:, c], scalar=1.0,
                                                  in1=vec[:, (3 + ly) * KT:(4 + ly) * KT], op0=ALU.add, op1=ALU.mult))
                norm(phases[f"n4{ly}"], tm2, hT, 4, lambda t: (mA[:, t // 2], mB[:, t // 2]))

                dve.wait_ge(S["xs_out"], 16 * (ly + 1))

                def ca_take(i, t):
                    dve.tensor_copy(ca[:, i, t], acc[t][:]).then_inc(S["acc_taken"], 1)
                stream(phases[f"ca{ly}"], 5, nt, ca_take)
                dve.wait_ge(S["gates_made"], 4 * ly + 1)
                dve.tensor_tensor(ca[:, 0, 0:nt], ca[:, 0, 0:nt], ca[:, 1, 0:nt], ALU.mult).then_inc(S["glu_made"], 1)
                for c in range(4):
                    dve.memset(cv[:, c], 0.0).then_inc(S["conv_step"], 1)
                dve.wait_ge(S["ca_const_in"], 48 * (ly + 1))
                dve.wait_ge(S["gates_made"], 4 * ly + 3)
                for t in range(nt):
                    dve.wait_ge(S["py_done"], (4 if ly else 0) + t + 1)
                    link(dve.tensor_tensor(ya[:, t], acc[t][:], psc[:], ALU.mult))
                    dve.tensor_tensor(ya[:, t], ya[:, t], ca[:, 4, t], ALU.mult).then_inc(S["py_taken"], 1)
                dve.wait_ge(S["py_taken"], (4 if ly else 0) + nt)
                dve.wait_ge(S["yt_taken"], 4 * ly + 4)
                ns_ = nt // 2
                for nm_, c0, n_, snt in SEGS[ly]:
                    def tap(i, s, c0=c0):
                        j = i + c0
                        dve.wait_ge(S["conv_step"], j * 16 + (132 * ly + s + 1))
                        c, kk = s % 4, s // 4
                        yv = yT[:, c, 0:ns_, bass.ds(j * 4 + kk, L)]
                        av = cv[:, c, 0:nt * P].rearrange("p (s n) -> p s n", n=L)
                        dve.scalar_tensor_tensor(out=av, in0=yv, scalar=dw[:, ly, bass.ds(j * 16 + s, 1)], in1=av,
                                                 op0=ALU.mult, op1=ALU.add).then_inc(S["conv_step"], 1)

                    def take4(i, t, c0=c0):
                        dve.tensor_copy(qkvg[:, c0 // 2, t, bass.ds(i * CH, CH)], acc[t][:]).then_inc(S["acc_taken"], 1)
                    stream(phases[f"s{ly}{nm_}"], n_, snt, take4, extra=tap)

                dve.wait_ge(S["conv_step"], 132 * (ly + 1))
                for c in range(4):
                    av = cv[:, c, 0:nt * P]
                    dve.tensor_scalar(av, av, cvec[:, 4 * ly + c:4 * ly + c + 1], None, ALU.add).then_inc(S["cf_b"], 1)
                for t in range(nt):
                    k = (4 if ly else 0) + t
                    dve.wait_ge(S["cf_done"], k + 1)
                    link(dve.bn_stats(bn[:], tp[t % 2][:]))
                    link(dve.bn_aggr(mv[:, 0:2], bn[:]))
                    dve.tensor_scalar(mv[:, 2:3], mv[:, 1:2], LN_EPS, None, ALU.add).then_inc(S["z_made"], 1)
                    dve.wait_ge(S["cf_sd"], k + 1)
                    link(dve.reciprocal(mv[:, 3:4], mv[:, 3:4]))
                    dve.tensor_scalar(zb[:, t % 2], tp[t % 2][:], mv[:, 0:1], mv[:, 3:4], ALU.subtract,
                                      ALU.mult).then_inc(S["z_made"], 1)
                    dve.wait_ge(S["pw_done"], k + 1)
                    dve.tensor_tensor(gC[:, t], acc[t % 2][:], gC[:, t], ALU.mult).then_inc(S["yc_made"], 1)

                U = 6 if nt == 4 else 4
                u0, kinds = units, kinds_of(nt)
                ot0 = B_HEADS + u0
                dve.wait_ge(S["na_in"], 64 * (ly + 1))
                dve.wait_ge(S["gates_made"], 4 * ly + 4)
                dve.wait_ge(S["acc_taken"], phases[f"mx{ly}"].taken)
                cg0 = 25 + 16 * ly
                def rope(lap, n, s):
                    if s == 0:
                        dve.wait_ge(S["cg_done"], lap * 2 + (cg0 + 2 * n))
                    xv = qkvg[:, s, 0:2, pair_cols(lap, n, 0, P)]
                    link(dve.tensor_tensor(rn[:, 0], xv, ropn[:, 0], ALU.mult))
                    xh, rh, sh = (v.rearrange("p t (b h n) -> p t b h n", h=2, n=16) for v in (xv, rn[:, 1], ropn[:, 1]))
                    for hf in range(2):
                        link(dve.tensor_tensor(rh[:, :, :, hf, :], xh[:, :, :, 1 - hf, :], sh[:, :, :, hf, :], ALU.mult))
                    ins = dve.tensor_tensor(st[:, 2 * s:2 * s + 2], rn[:, 0], rn[:, 1], ALU.add)
                    if s == 0:
                        link(ins)
                    else:
                        ins.then_inc(S["st_dve"], 1)

                def take_q(lap, n):
                    dve.wait_ge(S["cg_done"], lap * 2 + (cg0 + 2 * n + 1))
                    dve.tensor_scalar(T[:, 0:nt * P], cg[0][:, 0:nt * P], NA_D ** -0.5, None,
                                      ALU.mult).then_inc(S["cg_taken"], 1)

                def na_max(lap, u):
                    dve.wait_ge(S["s_done"], lap * U + (16 + u0 + u + 1))
                    if kinds[u % U][1] < 2:
                        link(dve.tensor_reduce(mx[:, u % 2, 0:1], acc[u % 2][:], AX, ALU.max))
                        dve.tensor_scalar(nm[:, u % 2, 0:1], mx[:, u % 2, 0:1], -1.0, None,
                                          ALU.mult).then_inc(S["m_ready"], 1)
                    else:
                        link(dve.tensor_reduce(mx[:, u % 2], acc[u % 2][:].rearrange("p (t n) -> p t n", n=L), AX,
                                               ALU.max))
                        dve.tensor_scalar(nm[:, u % 2], mx[:, u % 2], -1.0, None, ALU.mult).then_inc(S["m_ready"], 1)

                def na_sum(lap, u):
                    dve.wait_ge(S["p_made"], lap * U + (16 + u0 + u + 1))
                    dve.wait_ge(S["o_taken"], lap * U + (ot0 + u - 1))
                    link(dve.reciprocal(rr[:, u % 2], sm[:, u % 2]) if kinds[u % U][1] == 2 else
                         dve.reciprocal(rr[:, u % 2, 0:1], sm[:, u % 2, 0:1]))

                def na_out(lap, u):
                    e, t = kinds[u % U]
                    dve.wait_ge(S["o_done"], lap * U + (12 + u0 + u + 1))
                    for k, tt in enumerate((2, 3) if t == 2 else (t,)):
                        gv = qkvg[:, 3, tt, pair_cols(lap, u // U, e * NA_D, NA_D)]
                        ins = dve.scalar_tensor_tensor(out=gv, in0=acc[2 + u % 2][:, k * NA_D:(k + 1) * NA_D],
                                                       scalar=rr[:, u % 2, k:k + 1], in1=gv, op0=ALU.mult, op1=ALU.mult)
                    ins.then_inc(S["o_taken"], 1)

                def step(lap, k, end):
                    na_sum(lap, k - 1)
                    if k == 1 and end > U:
                        rope(lap, 1, 0)
                    if k + 1 < end:
                        na_max(lap, k + 1)
                    if k == U - 2 and end > U:
                        take_q(lap, 1)
                    na_out(lap, k - 1)
                    if k == 1 and end > U:
                        rope(lap, 1, 1)

                rope(0, 0, 0)
                rope(0, 0, 1)
                take_q(0, 0)
                na_max(0, 0)
                na_max(0, 1)
                na_laps(dve, step, nt, link)
                units += 8 * U
                groups(phases[f"mx{ly}"], nt, tm2, hT, lambda t: (None, None))
                for k in range(2 * nt):
                    wait(dve, "gs_done", 8 * ly + k - 1)
                    dve.tensor_tensor(dg[:, k % 2].rearrange("p (k n) -> p k n", n=P),
                                      ident[:].unsqueeze(1).broadcast_to([P, 4, P]),
                                      mG[:, k // 4, k % 4 * 4:k % 4 * 4 + 4].unsqueeze(2).broadcast_to([P, 4, P]),
                                      ALU.mult).then_inc(S["gate_diag"], 1)
                dve.wait_ge(S["x4r_in"], 32 if ly == 0 else 48)
                dve.wait_ge(S["gs_taken"], 8 * ly + 2 * nt)

                def add_gated(i, t):
                    cols = bass.ds(i * CH, CH)
                    dve.wait_ge(S["acc_taken"], num(lap_at(phases[f"o2{ly}"].taken + t - 1, nt, i)))
                    dve.tensor_tensor(tm2[:, t % 2], acc[t][:], gatb[:, t // 2, cols], ALU.mult)\
                       .then_inc(S["tmp_made"], 1)
                    v = lap_at((16 if ly else 0) + t + 1, nt, i)
                    dve.wait_ge(S["tmp_made"], num(v))
                    xv = x4[:, t, cols]
                    dve.tensor_tensor(xv, tm2[:, t % 2], xv, ALU.add).then_inc(S["acc_taken"], 1)
                stream(phases[f"o2{ly}"], 4, nt, add_gated, last=ly == 1)
            var_root(2)
            dve.wait_ge(S["rs_made"], norms[0])
            dve.wait_ge(S["fin_in"], 32)
            for t in range(2):
                ins = dve.scalar_tensor_tensor(out=x4[:, t], in0=x4[:, t], scalar=rs[:, t:t + 1], in1=fgain[:],
                                               op0=ALU.mult, op1=ALU.mult)
                if t == 0:
                    link(ins)
            ins.then_inc(S["y_made"], 1)

        @block.tensor
        def _(pe):
            def bank_free(g, m):
                wait(pe, "tg_full", g - 1 if m >= 2 else g)

            def turn4(g, m, src):
                for k in range(4):
                    ins = pe.transpose(tp[m % 2][:, k * P:(k + 1) * P], src(k), ident[:])
                ins.then_inc(S["tp_done"], 1)

            scaled = [0]

            def norm(ph, ns, nt):
                for t in range(nt):
                    scaled[0] += 1
                    pe.wait_ge(S["scaled"], scaled[0])
                    for g in range(4):
                        bank_free(ph.groups + 4 * t + g, 4 * t + g)
                        turn4(0, g, lambda k: ns[:, t % 2, (4 * g + k) * P:(4 * g + k + 1) * P])

            def begin(ph):
                pe.wait_ge(S["tg_lo"], ph.groups)
                wait(pe, "acc_taken", ph.taken)

            def gate_up(ph, gates, rows):
                begin(ph)

                def u_turn(c, off):
                    pe.wait_ge(S["acc_taken"], num(lap_at(ph.taken + 2 * off + 2, 2, c)))
                    pe.wait_ge(S["tg_full"], num(lap_at(ph.groups + 2 * off, 2, c)))
                    for f in range(2):
                        for k in range(2):
                            for t in range(2):
                                ins = pe.transpose(tp[f][:, k * L + t * P:k * L + (t + 1) * P],
                                                   ub[:, t, (2 * f + k) * P:(2 * f + k + 1) * P], ident[:])
                        ins.then_inc(S["tp_done"], 1)
                    mod_turn(pe, lap_at(rows + off, 1, c))

                pair_pieces(pe, GATE_UP, h1, KT, ph.pieces, range(48), lambda half, t: None, rows)
                with pe.Fori(1, FC) as i:
                    def bank_free(half, t):
                        if half == 0:
                            pe.wait_ge(S["gate_act"], num(At(gates + t - 1, 2, i)))
                        else:
                            pe.wait_ge(S["acc_taken"], num(At(ph.taken + t - 1, 2, i)))
                    p0 = At(ph.pieces, 48, i)
                    pair_pieces(pe, GATE_UP, h1, KT, p0, range(4), bank_free)
                    u_turn(i, -1)
                    pair_pieces(pe, GATE_UP, h1, KT, p0, range(4, 48), bank_free, At(rows, 1, i))
                u_turn(FC - 1, 0)

            def down_proj(ph, order):
                begin(ph)
                per = 4 * len(order)
                with pe.Fori(0, 2) as i:
                    pair_pieces(pe, order, uT, FT, At(ph.pieces, per, i), range(per), lambda half, t: pe.wait_ge(
                        S["acc_taken"], num(At(ph.taken + 2 * half + t + 1 - 4, 4, i))), At(FC, 1, i))
                    if order is DOWN_MOD:
                        mod_turn(pe, At(FC, 1, i))

            def stream(ph, src, laps, nt):
                begin(ph)
                with pe.Fori(0, laps) as i:
                    chunk_pieces(pe, src, nt, At(ph.pieces, 16, i), At(ph.taken, nt, i), range(16))

            pe.wait_ge(S["const_in"], 16 * 9)
            for k, (src, rows) in enumerate(((vrow[:], NV), (brow[:], 120), (drow[:, 0], 124), (drow[:, 1], 124))):
                pe.transpose(acc[k][:, 0:rows], src, ident[0:rows, 0:rows]).then_inc(S["cols_made"], 1)
            norm(phases["n1"], ns1, 2)
            pe.wait_ge(S["cols_taken"], 7)
            pe.wait_ge(S["c_split"], 1)
            gate_up(phases["g1"], 0, 0)
            down_proj(phases["d1"], DOWN_MOD)
            norm(phases["n2"], ns1, 2)
            stream(phases["i1"], h1, 9, 2)

            pe.wait_ge(S["roped"], 1)

            def head_cols(hh):
                return hh * HD if hh < 10 else B_COL + (hh - 10) * HD
            for g in range(13):
                if g >= 2:
                    pe.wait_ge(S["cg_taken"], g - 1)
                for e in range(2):
                    for t in range(2):
                        c0 = head_cols(2 * g + e)
                        ins = pe.transpose(cg[g % 2][:, e * L + t * P:e * L + (t + 1) * P], proj[:, t, c0:c0 + HD], ident[:])
                ins.then_inc(S["cg_done"], 1)
            pe.wait_ge(S["cg_taken"], 13)
            wait(pe, "acc_taken", phases["at1"].taken)

            def scores(q):
                if q >= 2:
                    pe.wait_ge(S["p_made"], q - 1)
                qh, kh = (q, 8 + q // 4) if q < 8 else (10 + q - 8, 18 + q - 8)
                for t in range(2):
                    ins = pe.matmul(acc[q % 2][:, t * L:(t + 1) * L], qkT[:, qh, t * P:(t + 1) * P], qkT[:, kh, :],
                                    start=True, stop=True)
                ins.then_inc(S["s_done"], 1)

            def turn_p(k, pv):
                pe.wait_ge(S["pn_made"], k + 1)
                pe.wait_ge(S["cg_taken"], 12 + k)
                for j in range(2):
                    for t in range(2):
                        ins = pe.transpose(cg[(13 + k) % 2][:, j * L + t * P:j * L + (t + 1) * P],
                                           pv[:, t, j * P:(j + 1) * P], ident[:])
                ins.then_inc(S["cg_done"], 1)
                pe.wait_ge(S["cg_taken"], 14 + k)

            g0 = phases["at1"].groups
            scores(0)
            for q in range(8):
                scores(q + 1)
                turn_p(q, pr1[:, q % 2])
                if q >= 2:
                    pe.wait_ge(S["tg_full"], g0 + q - 1)
                c0 = VA_COL + q // 4 * HD
                for j in range(2):
                    ins = pe.matmul(acc[2 + q % 2][:, 0:L], proj[:, j, c0:c0 + HD], pt1[:, q % 2, j],
                                    start=(j == 0), stop=(j == 1))
                ins.then_inc(S["o_done"], 1)
            pe.wait_ge(S["tg_full"], g0 + 8)
            for h in range(B_HEADS):
                scores(9 + 2 * h)
                turn_p(8 + h, pr1[:, 0])
                if h + 1 < B_HEADS:
                    scores(10 + 2 * h)
                if h >= 2:
                    pe.wait_ge(S["o_taken"], h - 1)
                for t in range(2):
                    for j in range(2):
                        ins = pe.matmul(acc[2 + h % 2][:, t * L:(t + 1) * L], pt1[:, h % 2, j, t * P:(t + 1) * P],
                                        proj[:, j, VD_COL + h * L:VD_COL + (h + 1) * L], start=(j == 0), stop=(j == 1))
                ins.then_inc(S["o_done"], 1)
                pe.wait_ge(S["ob_made"], 2 * h + 2)
                if h >= 2:
                    pe.wait_ge(S["tg_full"], g0 + 8 + h - 1)
                for f in range(2):
                    for t in range(2):
                        ins = pe.transpose(tp[h % 2][:, f * L + t * P:f * L + (t + 1) * P], ob[:, t, f * P:(f + 1) * P],
                                           ident[:])
                ins.then_inc(S["tp_done"], 1)
            stream(phases["o1"], h1, 4, 2)
            norm(phases["n3"], ns1, 2)
            gate_up(phases["g2"], 2 * FC, FC + 2)
            down_proj(phases["d2"], DOWN)

            units, cgs = 0, 25
            for ly in range(2):
                nt = NT[ly]
                norm(phases[f"n4{ly}"], ns2, 4)
                stream(phases[f"ca{ly}"], hT, 5, nt)
                pe.wait_ge(S["glu_made"], ly + 1)
                wait(pe, "tg_full", phases[f"ca{ly}"].groups)
                for c in range(4):
                    if c >= 2:
                        pe.wait_ge(S["yt_taken"], 4 * ly + c - 1)
                    for t in range(nt):
                        ins = pe.transpose(tp[c % 2][:, t * P:(t + 1) * P], ca[:, 0, t, c * P:(c + 1) * P], ident[:])
                    ins.then_inc(S["yt_done"], 1)
                pe.wait_ge(S["ca_const_in"], 48 * (ly + 1))
                pe.wait_ge(S["acc_taken"], phases[f"ca{ly}"].taken + 5 * nt)
                for g in range(4):
                    if g >= 2:
                        pe.wait_ge(S["pl_taken"], 4 * ly + g - 1)
                    for s in range(nt // 2):
                        for j in range(2):
                            ins = pe.matmul(cg[g % 2][:, s * L:(s + 1) * L], ca[:, 3, 2 * s + j, g * P:(g + 1) * P],
                                            pmat[:, j, g, :], start=(j == 0), stop=(j == 1))
                    ins.then_inc(S["pl_done"], 1)
                pe.wait_ge(S["pl_taken"], 4 * ly + 4)
                for t in range(nt):
                    for g in range(4):
                        ins = pe.matmul(acc[t][:, g * P:(g + 1) * P], pdT[:, g, t * P:(t + 1) * P], wpool[:, g, :],
                                        start=True, stop=True)
                    ins.then_inc(S["py_done"], 1)
                pe.wait_ge(S["py_taken"], (4 if ly else 0) + nt)
                for nm_, _, n_, snt in SEGS[ly]:
                    stream(phases[f"s{ly}{nm_}"], hT, n_, snt)

                pe.wait_ge(S["cf_b"], 4 * (ly + 1))
                pe.wait_ge(S["cf_in"], 32 * (ly + 1))
                wait(pe, "acc_taken", phases[f"mx{ly}"].taken)
                pe.wait_ge(S["yt_taken"], 4 * (ly + 1))

                def by_token(t):
                    k = (4 if ly else 0) + t
                    if t >= 2:
                        pe.wait_ge(S["z_made"], 2 * (k - 1))
                    for c in range(4):
                        ins = pe.transpose(tp[t % 2][:, c * P:(c + 1) * P], cv[:, c, t * P:(t + 1) * P], ident[:])
                    ins.then_inc(S["cf_done"], 1)
                by_token(0)
                for t in range(nt):
                    k = (4 if ly else 0) + t
                    if t + 1 < nt:
                        by_token(t + 1)
                    pe.wait_ge(S["z_made"], 2 * k + 2)
                    if t >= 2:
                        pe.wait_ge(S["s_made"], k - 1)
                    for c in range(4):
                        ins = pe.transpose(cg[t % 2][:, c * P:(c + 1) * P], zb[:, t % 2, c * P:(c + 1) * P], ident[:])
                    ins.then_inc(S["cz_done"], 1)
                    pe.wait_ge(S["s_made"], k + 1)
                    if t >= 2:
                        pe.wait_ge(S["yc_made"], k - 1)
                    for c in range(4):
                        pe.matmul(acc[t % 2][:], sT[:, t % 2, c * P:(c + 1) * P], cpw[:, c, :], start=(c == 0), stop=False)
                    pe.matmul(acc[t % 2][:], ones[0:1, :], cpb[:], start=False, stop=True).then_inc(S["pw_done"], 1)

                pe.wait_ge(S["bias_ready"], ly + 1)
                pe.wait_ge(S["yc_made"], (4 if ly else 0) + nt)
                pe.wait_ge(S["s_made"], (4 if ly else 0) + nt)
                U = 6 if nt == 4 else 4
                u0, kinds = units, kinds_of(nt)
                def staged(lap, n):
                    pe.wait_ge(S["st_dve"], lap + (8 * ly + n + 1))
                    pe.wait_ge(S["st_act"], lap + (8 * ly + n + 1))
                    pe.wait_ge(S["cg_taken"], lap * 2 + (cgs + 2 * n))
                    for m, tiles in enumerate(((0, 1, 6, 7)[:nt], (2, 3, 4, 5))):
                        for k, tt in enumerate(tiles):
                            ins = pe.transpose(cg[m][:, k * P:(k + 1) * P], st[:, tt], ident[:])
                        ins.then_inc(S["cg_done"], 1)

                def na_scores(lap, u):
                    e, t = kinds[u % U]
                    r = slice(e * NA_D, (e + 1) * NA_D)
                    if u % U == 0:
                        pe.wait_ge(S["cg_taken"], lap * 2 + (cgs + 2 * (u // U) + 2))
                    pe.wait_ge(S["p_made"], lap * U + (16 + u0 + u - 1))
                    if t < 2:
                        w = (6 * e + 2 - 2 * t) * GRID
                        pe.matmul(acc[u % 2][:], T[r, t * P:(t + 1) * P], T[r, CH:2 * CH], start=True, stop=False)
                        ins = pe.matmul(acc[u % 2][:, 0:L], turn[:], bias[:].rearrange("p h n -> p (h n)")[:, bass.ds(
                            lap * (12 * GRID) + (u // U * 12 * GRID + w), L)], start=False, stop=True)
                    else:
                        for tt in range(2):
                            ins = pe.matmul(acc[u % 2][:, tt * L:(tt + 1) * L], T[r, L + tt * P:L + (tt + 1) * P],
                                            T[r, CH + L:2 * CH], start=True, stop=True)
                    ins.then_inc(S["s_done"], 1)

                def na_turn(lap, u):
                    pe.wait_ge(S["p_made"], lap * U + (16 + u0 + u + 1))
                    for j in range(4):
                        src = pr[:, u % 2, j * P:(j + 1) * P] if kinds[u % U][1] < 2 else \
                            pr[:, u % 2, (j % 2) * L + j // 2 * P:(j % 2) * L + j // 2 * P + P]
                        ins = pe.transpose(tp[u % 2][:, j * P:(j + 1) * P], src, ident[:])
                    ins.then_inc(S["pt_done"], 1)

                def na_values(lap, u):
                    e, t = kinds[u % U]
                    pe.wait_ge(S["pt_taken"], lap * U + (u0 + u + 1))
                    pe.wait_ge(S["o_taken"], lap * U + (B_HEADS + u0 + u - 1))
                    for k in range(1 if t < 2 else 2):
                        js = range(4) if t < 2 else range(2)
                        for j in js:
                            lh = pt[:, u % 2, j * P:(j + 1) * P] if t < 2 else \
                                pt[:, u % 2, j * L + k * P:j * L + (k + 1) * P]
                            ins = pe.matmul(acc[2 + u % 2][:, k * NA_D:(k + 1) * NA_D], lh,
                                            qkvg[:, 2, j if t < 2 else 2 + j, pair_cols(lap, u // U, e * NA_D, NA_D)],
                                            start=(j == 0), stop=(j == js[-1]))
                    ins.then_inc(S["o_done"], 1)

                def step(lap, k, end):
                    if k + 1 < end:
                        na_scores(lap, k + 1)
                    if k == U - 2 and end > U:
                        staged(lap, 1)
                    if k < end:
                        na_turn(lap, k)
                    na_values(lap, k - 1)

                staged(0, 0)
                na_scores(0, 0)
                na_scores(0, 1)
                na_turn(0, 0)
                na_laps(pe, step, nt)
                units += 8 * U
                cgs += 16
                pe.wait_ge(S["o_taken"], B_HEADS + units)
                pe.wait_ge(S["pt_taken"], units)
                ph = phases[f"mx{ly}"]
                for t in range(nt):
                    for g in range(4):
                        m = 4 * t + g
                        bank_free(ph.groups + m, m)
                        src = (ya[:, t], qkvg[:, 3, t, 0:CH], qkvg[:, 3, t, CH:2 * CH], gC[:, t])[g]
                        turn4(0, g, lambda k: src[:, k * P:(k + 1) * P])
                for k in range(2 * nt):
                    pe.wait_ge(S["gate_diag"], 8 * ly + k + 1)
                    wait(pe, "gs_taken", 8 * ly + k - 1)
                    pe.matmul(cg[k % 2][:], ones[:], dg[:, k % 2], start=True, stop=True).then_inc(S["gs_done"], 1)
                stream(phases[f"o2{ly}"], hT, 4, nt)

        @block.gpsimd
        def _(pool):
            pool.wait_ge(S["pieces_used"], phases["n40"].pieces)
            pool.dma_start(ogain[:], row_bc(a["out_norm"], D)).then_inc(S["fin_in"], 16)
            pool.dma_start(x4[:, 2:4, :], ctx_v).then_inc(S["ctx_in"], 16)
            for ly in range(2):
                nt = NT[ly]
                if ly == 0:
                    pool.wait_ge(S["x4_in"], 2)
                else:
                    pool.wait_ge(S["acc_taken"], phases["n41"].taken)
                pool.dma_start(xs_v, x4[:, 0:2, :]).then_inc(S["xs_out"], 16)
                if ly == 1:
                    pool.wait_ge(S["conv_step"], 132)
                pool.memset(yT[:, :, :, 0:PAD], 0.0).then_inc(S["pool_step"], 1)
                pool.memset(yT[:, :, :, PAD + L:YW], 0.0).then_inc(S["pad_made"], 1)
                pool.wait_ge(S["na_in"], 64 * (ly + 1))
                pool.wait_ge(S["bias_in"], 12 * 16 * (ly + 1))
                bv = bias[:].rearrange("p h (r n) -> p (h r) n", n=GRID)
                pool.tensor_tensor(bv, bv, mask[:].unsqueeze(1).broadcast_to([P, NA_H * 6, GRID]), ALU.add)\
                    .then_inc(S["bias_ready"], 1)
            pool.wait_ge(S["acc_taken"], phases["end"].taken)
            pool.dma_start(fgain[:], row_bc(a["final_norm_g_2"], D)).then_inc(S["fin_in"], 16)


def kinds_of(nt):
    return [(e, t) for e in range(2) for t in ((0, 1, 2) if nt == 4 else (0, 1))]


def kernel(**inputs):
    import concourse.bacc as bacc
    from concourse.bass_utils import run_bass_kernel_spmd

    cosa, sina, cosb, sinb, cosn, sinn = rope_tables()
    arrays = {k: np.ascontiguousarray(v) for k, v in inputs.items()}
    arrays["vrows"] = np.concatenate([np.asarray(inputs[k]).reshape(-1, P) for k in (
        "ffn1_norm", "mix_norm", "ffn2_norm", "norm_g_2", "c_2", "c_ctx_2")])
    arrays.update(cosa=cosa, sina=sina, cosb=cosb, sinb=sinb, cosn=cosn, sinn=sinn, pmat=pool_matrices(),
                  mask=window_mask(), turn=np.kron(np.eye(2), np.eye(GRID)[::-1]).astype(np.float32), ident=np.eye(P, dtype=np.float32),
                  sel=np.tile(np.eye(2, dtype=np.float32), (2, 1)))
    nc = bacc.Bacc("TRN2", target_bir_lowering=False, num_devices=1)
    aps = {k: nc.dram_tensor(k, v.shape, F32, kind="ExternalInput").ap() for k, v in arrays.items()}
    out = nc.dram_tensor("y", (1, L, D), F32, kind="ExternalOutput").ap()
    xs = nc.dram_tensor("x_rest", (L, D), F32, kind="Internal").ap()
    build(nc, aps, out, xs)
    r = run_bass_kernel_spmd(nc, [arrays], core_ids=[0])
    return r.results[0]["y"]
```

```python
from contextlib import ExitStack

import numpy as np

import concourse.bass as bass
from concourse import mybir

F32 = mybir.dt.float32
F32R = mybir.dt.float32r
ACT = mybir.ActivationFunctionType
ALU = mybir.AluOpType
AX = mybir.AxisListType.X

P = 128
D = 2048
KT = D // P
L = 256
CH = 512
DFF = 5632
FT = DFF // P
EPS = 1e-6
LN_EPS = 1e-5
HD = 128
A_HEADS, A_KV, B_HEADS = 8, 2, 4
B_COL = (A_HEADS + 2 * A_KV) * HD
VA_COL = (A_HEADS + A_KV) * HD
VD_COL = B_COL + 4 * B_HEADS * HD
D_IN = VD_COL + 2 * B_HEADS * HD
SCALE = HD ** -0.5
LAMBDA_INIT = 0.2
NA_H, NA_D = 16, 64
GRID = 64
RPB_R, RPB_C = 15, 31
TAPS = 31
PAD = TAPS // 2
YW = L + TAPS
POOLS = (2, 4, 8, 16)
PROJ2 = 6656
LOOK = 2
RING = 4


def rope_tables():
    t = np.arange(L, dtype=np.float32)
    rows, cols = np.floor(t / GRID).astype(np.float32), (t % GRID).astype(np.float32)

    def table(pos, dim, theta):
        f = np.float32(theta) ** (-np.arange(0, dim, 2, dtype=np.float32) / np.float32(dim))
        a = (pos[:, None] * f[None, :]).astype(np.float32)
        return np.concatenate([np.cos(a), np.cos(a)], 1), np.concatenate([-np.sin(a), np.sin(a)], 1)

    def pair(dim):
        r, c = table(rows, dim, 10000.0), table(cols, dim, 10000.0)
        return [np.concatenate([r[k], c[k]], 1) for k in range(2)]

    a = pair(64)
    b = table(t, 32, 500000.0)
    n = [np.tile(m, (1, 2)) for m in pair(32)]
    return [m.astype(np.float32) for m in (*a, *b, *n)]


def pool_matrices():
    m = np.zeros((len(POOLS), L, L), np.float32)
    for g, w in enumerate(POOLS):
        for t in range(L):
            lo, hi = max(t - w // 2, 0), min(t + (w - w // 2) - 1, L - 1)
            m[g, lo:hi + 1, t] = np.float32(1.0) / np.float32(hi - lo + 1)
            m[g, t, t] -= np.float32(1.0)
    return m.reshape(len(POOLS), 2, P, L).transpose(2, 1, 0, 3).copy()


def window_mask():
    q = np.arange(GRID)
    start = np.clip(q - 8, 0, GRID - 16)
    k = np.arange(GRID)[None, :]
    inside = (k >= start[:, None]) & (k < start[:, None] + 16)
    return np.tile(np.where(inside, 0.0, -1e30).astype(np.float32)[::-1], (2, 1))


class Phase:

    def __init__(self, pieces, taken, groups):
        self.pieces, self.taken, self.groups = pieces, taken, groups


def build(nc, a, out, xs_dram):
    ctx = ExitStack()
    with ctx:
        sem_names = """raw0 raw1 raw2 raw3 hi_made lo_made pieces_used acc_done acc_taken tp_done tg_full tg_hi
            tg_lo ss_made var_made sd_made scaled const_in cols_made cols_taken gate_act dve_step
             x_in rope_in roped qk_ss qk_sd cg_done cg_taken s_done m_ready p_made pn_made
            o_done o_taken lam_e ob_made x4_in xs_out ctx_in c_split row_taken mt_done mt_taken silu_c
            ca_const_in glu_made gates_made yt_done yt_taken pl_done pl_taken py_done py_taken pad_made
            conv_step cf_in cf_done z_made cz_done s_made pw_done yc_made na_in bias_in bias_ready
            st_dve st_act pt_done pt_taken gs_done gs_taken x4r_in fin_in y_out gate_diag rs_made cf_sd
            cf_b tmp_made y_made""".split()
        S = {n: ctx.enter_context(nc.semaphore(n)) for n in sem_names}
        base = (nc.sbuf_base + 63) // 64 * 64
        top = [base]

        def at(name, offset, shape, dt=F32):
            top[0] = max(top[0], base + offset + 4 * int(np.prod(shape[1:])))
            return nc.alloc_sbuf_tensor_at(name, shape, dt, offset=base + offset)

        K1 = 1024
        raw = at("raw", 0, [P, RING, 2 * CH])
        hi = at("hi", 16 * K1, [P, RING, CH], F32R)
        lo = at("lo", 24 * K1, [P, RING, CH], F32R)
        H = 32 * K1
        Q = 96 * K1
        h1 = [at("h1_hi", H, [P, KT, L], F32R), at("h1_lo", H + 16 * K1, [P, KT, L], F32R)]
        x1 = at("x1", H + 32 * K1, [P, 2, D])
        ns1 = at("ns1", H + 48 * K1, [P, 2, D])
        uT = [at("uT_hi", Q, [P, FT, L], F32R), at("uT_lo", Q + 44 * K1, [P, FT, L], F32R)]
        ub = at("ub", Q + 88 * K1, [P, 2, CH])
        tm1 = at("tm1", Q + 92 * K1, [P, 2, CH])
        rowb = at("rowb", Q + 104 * K1, [4, CH])
        proj = at("proj", Q, [P, 2, D_IN])
        qkT = at("qkT", Q + 36 * K1, [P, 26, L])
        rt = at("rt", Q + 62 * K1, [P, 2, 2048])
        pr1 = at("pr1", Q + 78 * K1, [P, 2, 2, L])
        pt1 = at("pt1", Q + 82 * K1, [P, 2, 2, L])
        ob = at("ob", Q + 62 * K1, [P, B_HEADS, 2, L])
        ropa = at("ropa", Q + 96 * K1, [P, 2, 2, P])
        ropb = at("ropb", Q + 98 * K1, [P, 2, 2, 32])
        gbc = at("gbc", Q + 99 * K1, [P, 4, P])
        lamv = at("lamv", Q + 101 * K1, [P, 4, P])
        sub_bc = at("sub_bc", Q + 103 * K1, [P, L])
        ogain = at("ogain", Q + 64 * K1, [P, D])
        hT = [at("hT_hi", H, [P, KT, 2 * L], F32R), at("hT_lo", H + 32 * K1, [P, KT, 2 * L], F32R)]
        x4 = at("x4", Q, [P, 4, D])
        tm2 = at("tm2", Q + 32 * K1, [P, 2, CH])
        ns2 = at("ns2", Q + 40 * K1, [P, 2, D])
        qkvg = at("qkvg", Q, [P, 4, 4, 2 * CH])
        ca = at("ca", Q, [P, 5, 4, CH])
        pmat = at("pmat", Q + 40 * K1, [P, 2, 4, L])
        wpool = at("wpool", Q + 48 * K1, [P, 4, P])
        psc = at("psc", Q + 50 * K1, [P, CH])
        pdT = at("pdT", Q + 52 * K1, [P, 4, 2 * L])
        gatb = at("gatb", Q + 48 * K1, [P, 2, D])
        fgain = at("fgain", Q + 32 * K1, [P, D])
        yT = at("yT", Q + 64 * K1, [P, 4, 2, YW])
        cv = at("cv", Q + 73 * K1, [P, 4, 2 * L])
        ya = at("ya", Q + 83 * K1, [P, 4, CH])
        gC = at("gC", Q + 91 * K1, [P, 4, CH])
        dg = at("dg", Q + 83 * K1, [P, 2, CH])
        st = at("st", H, [P, 8, P])
        T = at("T", H + 4 * K1, [P, 2 * CH])
        pr = at("pr", H + 8 * K1, [P, 2, CH])
        pt = at("pt", H + 12 * K1, [P, 2, CH])
        ropn = at("ropn", H + 16 * K1, [P, 2, 2, P])
        rn = at("rn", H + 18 * K1, [P, 2, 2, P])
        mask = at("mask", H + 20 * K1, [P, GRID])
        turn = at("turn", H + 20 * K1 + 256, [P, P])
        zb = at("zb", H + 32 * K1, [P, 2, CH])
        sT = at("sT", H + 36 * K1, [P, 2, CH])
        cpw = at("cpw", H + 24 * K1, [P, 4, CH])
        cpb = at("cpb", H + 22 * K1, [1, CH])
        bias = at("bias", H + 40 * K1, [P, NA_H, 6 * GRID])
        small = [Q + 106 * K1]

        def keep(name, shape, dt=F32):
            t = at(name, small[0], shape, dt)
            small[0] += (4 * int(np.prod(shape[1:])) + 31) // 32 * 32
            return t

        ident = keep("ident", [P, P])
        NV = 5 * KT + 2 * KT
        vec = keep("vec", [P, NV])
        bmod = keep("bmod", [P, 96])
        cvec = keep("cvec", [P, 24])
        dw = keep("dw", [P, 2, 128])
        cT = keep("cT", [P, KT, 2])
        c_in = keep("c_in", [P, KT, 4], F32R)
        sel = keep("sel", [4, 2])
        modT = keep("modT", [P, 96, 2])
        mA = keep("mA", [P, 2, KT])
        mB = keep("mB", [P, 2, KT])
        mG = keep("mG", [P, 2, KT])
        ss = keep("ss", [P, 4])
        rs = keep("rs", [P, 4])
        obs = keep("obs", [P, 2 * B_HEADS])
        sd = keep("sd", [P, 4])
        qss = keep("qss", [P, 2, 26])
        qsd = keep("qsd", [P, 2, 26])
        lam = keep("lam", [P, 8])
        mx = keep("mx", [P, 2, 2])
        nm = keep("nm", [P, 2, 2])
        sm = keep("sm", [P, 2, 2])
        rr = keep("rr", [P, 2, 2])
        bn = keep("bn", [P, 4, 6])
        mv = keep("mv", [P, 4, 2])
        sv = keep("sv", [P, 4])
        ones = keep("ones", [P, P])
        vrow = at("vrow", Q, [NV, P])
        brow = at("brow", Q + 512, [120, P])
        drow = at("drow", Q + 1024, [124, 2, P])
        assert top[0] <= nc.sbuf_usable_end, top[0] - nc.sbuf_usable_end

        acc = [ctx.enter_context(nc.psum_tensor(f"acc{i}", [P, CH], F32)) for i in range(4)]
        tp = [ctx.enter_context(nc.psum_tensor(f"tp{i}", [P, CH], F32)) for i in range(2)]
        cg = [ctx.enter_context(nc.psum_tensor(f"cg{i}", [P, CH], F32)) for i in range(2)]

        phases = {}
        total = [0, 0, 0]

        def phase(name, pieces, taken, groups):
            phases[name] = Phase(*total)
            for k, n in enumerate((pieces, taken, groups)):
                total[k] += n

        def lap_units(groups):
            units, n = [], {"w": 0, "m": 0}
            for g in groups:
                for kind in "w" + g:
                    units.append((kind, n[kind]))
                    n[kind] += 1
            return units

        GATE_UP, DOWN_MOD, DOWN = lap_units("wmmwmmmwmmmw"), lap_units("wmw" * 8 + "ww"), lap_units("w" * 22)

        def row_at(order):
            return 4 * (order.index(("m", 7)) // 2) + 4

        FC = DFF // CH
        phase("n1", 0, 0, 8)
        phase("g1", FC * 48, FC * 2, 2 * FC)
        phase("d1", 2 * 104, 8, 0)
        phase("n2", 0, 0, 8)
        phase("i1", 9 * 16, 18, 0)
        phase("at1", 0, 0, A_HEADS + B_HEADS)
        phase("o1", 4 * 16, 8, 0)
        phase("n3", 0, 0, 8)
        phase("g2", FC * 48, FC * 2, 2 * FC)
        phase("d2", 2 * 88, 8, 0)
        SEGS = [[(nm_, 2 * k, 2, 4) for k, nm_ in enumerate("qkvg")],
                [("q", 0, 2, 2), ("k", 2, 2, 4), ("v", 4, 2, 4), ("g", 6, 2, 2)]]
        NT = [4, 2]
        for ly in range(2):
            phase(f"n4{ly}", 0, 0, 16)
            phase(f"ca{ly}", 5 * 16, 5 * NT[ly], 0)
            for nm_, _, n, nt in SEGS[ly]:
                phase(f"s{ly}{nm_}", n * 16, n * nt, 0)
            phase(f"mx{ly}", 0, 0, 4 * NT[ly])
            phase(f"o2{ly}", 4 * 16, 4 * NT[ly], 0)
        phase("end", 0, 0, 0)

        class Link:

            def __init__(self, eng, sem):
                self.eng, self.sem, self.n, self.lap, self.per = eng, sem, 0, None, 0

            def __call__(self, ins):
                self.n += 1
                ins.then_inc(self.sem, 1)
                self.eng.wait_ge(self.sem, self.n if self.lap is None else self.n + self.lap * self.per)

            def start(self, lap, per):
                self.lap, self.per, self.was = lap, per, self.n

            def stop(self, laps):
                assert self.n - self.was == self.per, (self.n - self.was, self.per)
                self.n += self.per * (laps - 1)
                self.lap = None

        def wait(eng, name, value):
            if not isinstance(value, int) or value > 0:
                eng.wait_ge(S[name], value)

        def place(j):
            m, q = divmod(j, 4)
            return 2 * m + q % 2, q // 2

        def raw_piece(j):
            u, half = place(j)
            return raw[:, u % RING, half * CH:(half + 1) * CH]

        def hi_piece(act, p0, j):
            u, half = place(j)
            if half == 0:
                loads = (p0 // 8 + j // 8 + 1) * 16 if isinstance(p0, int) else \
                    At(p0.base // 8 * 16 + j // 8 * 16 + 16, p0.per * 2, p0.lap).value()
                act.wait_ge(S[f"raw{u % RING}"], loads)
            wait(act, "pieces_used", num(p0 + (j - RING + 1)))
            act.activation(hi[:, j % RING, :], raw_piece(j), ACT.Copy).then_inc(S["hi_made"], 1)

        def lo_piece(dve, p0, j):
            wait(dve, "hi_made", num(p0 + (j + 1)))
            dve.tensor_tensor(lo[:, j % RING, :], raw_piece(j), hi[:, j % RING, :].bitcast(F32),
                              ALU.subtract).then_inc(S["lo_made"], 1)

        class At:

            def __init__(self, base, per, lap):
                self.base, self.per, self.lap = base, per, lap

            def __add__(self, n):
                return At(self.base + n, self.per, self.lap)

            def __sub__(self, n):
                return At(self.base - n, self.per, self.lap)

            def value(self):
                return self.lap * self.per + self.base

        def num(v):
            return v.value() if isinstance(v, At) else v

        def mm3(pe, bank, act_hi, act_lo, slot, start, stop):
            pe.matmul(bank, act_hi, hi[:, slot, :], start=start, stop=False)
            pe.matmul(bank, act_lo, hi[:, slot, :], start=False, stop=False)
            return pe.matmul(bank, act_hi, lo[:, slot, :], start=False, stop=stop)

        def chunk_pieces(pe, src, nt, p0, taken, js):
            for j in js:
                u, half = place(j)
                kt = 2 * u + half
                pe.wait_ge(S["lo_made"], num(p0 + (j + 1)))
                for t in range(nt):
                    if j == 0:
                        wait(pe, "acc_taken", num(taken + (t + 1 - nt)))
                    last = mm3(pe, acc[t][:], src[0][:, kt, t * P:(t + 1) * P], src[1][:, kt, t * P:(t + 1) * P],
                               j % RING, j == 0, j == 15)
                    if j == 15 and t < nt - 1:
                        last.then_inc(S["acc_done"], 1)
                last.then_inc(S["pieces_used"], 1)

        def mod_piece(pe, p0, j, kt, row):
            pe.wait_ge(S["lo_made"], num(p0 + (j + 1)))
            if kt == 0:
                wait(pe, "row_taken", num(row))
                pe.matmul(cg[0][0:4, :], c_in[:, kt, :], hi[:, j % RING, :], start=True, stop=False)
                ins = pe.matmul(cg[0][0:2, :], c_in[:, kt, 0:2], lo[:, j % RING, :], start=False, stop=False)
            else:
                pe.matmul(cg[0][0:2, :], c_in[:, kt, 0:2], lo[:, j % RING, :], start=False, stop=False)
                ins = pe.matmul(cg[0][0:4, :], c_in[:, kt, :], hi[:, j % RING, :], start=False, stop=(kt == KT - 1))
            ins.then_inc(S["pieces_used"], 1)

        def mod_turn(pe, row):
            pe.wait_ge(S["row_taken"], num(row + 1))
            for k in range(4):
                ins = pe.matmul(cg[1][:, 2 * k:2 * k + 2], rowb[:, k * P:(k + 1) * P], sel[:], start=True, stop=True)
            ins.then_inc(S["mt_done"], 1)

        def mod_row(dve, order, p0, row):
            dve.wait_ge(S["pieces_used"], num(p0 + row_at(order)))
            dve.tensor_copy(rowb[:], cg[0][0:4, :]).then_inc(S["row_taken"], 1)

        def mod_cols(dve, row, dst):
            dve.wait_ge(S["mt_done"], num(row + 1))
            dve.tensor_copy(dst, cg[1][:, 0:8].rearrange("p (k c) -> p k c", c=2)).then_inc(S["mt_taken"], 1)

        def pair_pieces(pe, order, src, nk, p0, js, bank_free, row=None):
            for j in js:
                u, half = place(j)
                kind, kt = order[u]
                if kind == "m":
                    mod_piece(pe, p0, j, 2 * kt + half, row)
                    continue
                pe.wait_ge(S["lo_made"], num(p0 + (j + 1)))
                for t in range(2):
                    if kt == 0:
                        bank_free(half, t)
                    last = mm3(pe, acc[2 * half + t][:], src[0][:, kt, t * P:(t + 1) * P],
                               src[1][:, kt, t * P:(t + 1) * P], j % RING, kt == 0, kt == nk - 1)
                    if kt == nk - 1 and t == 0:
                        last.then_inc(S["acc_done"], 1)
                last.then_inc(S["pieces_used"], 1)

        def pair_done(eng, ph, per, lap, half, t):
            if t == 0:
                eng.wait_ge(S["acc_done"], num(lap_at(ph.done + half + 1, 2, lap)))
            else:
                eng.wait_ge(S["pieces_used"], num(lap_at(ph.pieces + per - 2 + 2 * half, per, lap)))

        def lap_at(b, per, lap):
            return b + per * lap if isinstance(lap, int) else At(b, per, lap)

        def bank_done(eng, ph, nt, lap, t):
            if t < nt - 1:
                eng.wait_ge(S["acc_done"], num(lap_at(ph.done + t + 1, nt - 1, lap)))
            else:
                eng.wait_ge(S["pieces_used"], num(lap_at(ph.pieces + 16, 16, lap)))

        def turned(ph):
            return ph.groups - (A_HEADS if ph.groups > phases["at1"].groups else 0)

        n = 0
        for name in phases:
            phases[name].done = n
            if name[0] == "i" or name == "o1":
                n += {"i": 9, "o": 4}[name[0]]
            if name[0] in "gd":
                n += 2 * {"g": FC, "d": 2}[name[0]]
            if name[:2] == "ca":
                n += 5 * (NT[int(name[2])] - 1)
            if name[0] == "s":
                seg = [s for s in SEGS[int(name[1])] if s[0] == name[2:]][0]
                n += seg[2] * (seg[3] - 1)
            if name[:2] == "o2":
                n += 4 * (NT[int(name[2])] - 1)

        def pair_cols(lap, u, off, width):
            first = lap * P + (u * P + off)
            return slice(first, first + width) if isinstance(lap, int) else bass.ds(first, width)

        def na_laps(eng, step, nt, link=None):
            U = len(kinds_of(nt))
            with eng.Fori(0, 7) as lap:
                if link:
                    link.start(lap, 2 * U + 7)
                for k in range(1, U + 1):
                    step(lap, k, 2 * U)
            if link:
                link.stop(7)
            for k in range(1, U + 1):
                step(7, k, U)

        def gu_view(w):
            return w.rearrange("o (k p) (g c n) -> o c k p g n", p=P, g=2, n=CH)[0]

        def down_view(w):
            return w.rearrange("o (k p) (c n) -> o c k p n", p=P, n=2 * CH)[0]

        def wide_view(w, ly):
            return w.rearrange("o (k j p) (c n) -> o c k p j n", j=2, p=P, n=CH)[ly]

        gu = [gu_view(a["ffn1_w_gu"]), gu_view(a["ffn2_w_gu"])]
        down = [down_view(a["ffn1_w_down"]), down_view(a["ffn2_w_down"])]
        win1, wout1 = wide_view(a["w_in"], 0), wide_view(a["w_out"], 0)
        win2 = [wide_view(a["w_in_2"], ly) for ly in range(2)]
        wout2 = [wide_view(a["w_out_2"], ly) for ly in range(2)]
        modv = [wide_view(a["w_mod_2"], ly) for ly in range(2)]
        modl = a["w_mod_2"].rearrange("l (k j p) (c n) -> l c k p j n", j=2, p=P, n=CH)
        x_v = a["x"].rearrange("o (t p) d -> p (o t) d", p=P)
        ctx_v = a["ctx_2"].rearrange("o (t p) d -> p (o t) d", p=P)
        xs_v = xs_dram.rearrange("(t p) d -> p t d", p=P)
        out_v = out.rearrange("o (t p) d -> p (o t) d", p=P)

        def row_bc(ap, n):
            return bass.AP(tensor=ap.tensor, offset=ap.offset, ap=[[0, P], [1, n]])

        def o_total(n):
            return B_HEADS + 8 * (6 if n > 0 else 0) + 8 * (4 if n > 1 else 0)

        block = ctx.enter_context(nc.Block())

        @block.sync
        def _(sp):
            def unit(p0, u, src, shape=None):
                wait(sp, "lo_made", num(p0 + (4 * (u // 2) - 5 + u % 2)))
                dst = raw[:, u % RING, :]
                if shape == "wide":
                    dst = dst.rearrange("p (j n) -> p j n", j=2)
                sp.dma_start(dst, src).then_inc(S[f"raw{u % RING}"], 16)

            def load_lap(order, p0, main, mod, shape):
                for k, (kind, u) in enumerate(order):
                    if kind == "w":
                        unit(p0, k, main(u), shape)
                    else:
                        unit(p0, k, mod(u), "wide")

            def load_gu(w, ph, wm):
                load_lap(GATE_UP, ph.pieces, lambda u: w[0, u], lambda u: wm[0, u], "wide")
                with sp.Fori(1, FC) as i:
                    load_lap(GATE_UP, At(ph.pieces, 48, i), lambda u: w[i, u], lambda u: wm[i, u], "wide")

            def load_down(w, ph, order):
                with sp.Fori(0, 2) as i:
                    load_lap(order, At(ph.pieces, 2 * len(order), i), lambda u: w[i, u], lambda u: modl[i, FC, u], None)

            def ahead(w, ph, first):
                for u in range(RING):
                    unit(ph.pieces, u, w[first, u], "wide")

            def load_wide(w, ph, first, n, begun=False):
                if begun:
                    for u in range(RING, 8):
                        unit(ph.pieces, u, w[first, u], "wide")
                with sp.Fori(int(begun), n) as i:
                    for u in range(8):
                        unit(At(ph.pieces, 16, i), u, w[i + first, u], "wide")

            sp.dma_start(x1[:], x_v).then_inc(S["x_in"], 16)
            load_gu(gu[0], phases["g1"], modv[0])
            load_down(down[0], phases["d1"], DOWN_MOD)
            load_wide(win1, phases["i1"], 0, 9)
            load_wide(wout1, phases["o1"], 0, 4)
            load_gu(gu[1], phases["g2"], modv[1])
            load_down(down[1], phases["d2"], DOWN)
            for ly in range(2):
                nt = NT[ly]
                ph = phases[f"ca{ly}"]
                ahead(win2[ly], ph, 10)
                wait(sp, "tg_lo", phases[f"ca{ly}"].groups)
                sp.dma_start(pmat[:], a["pmat"]).then_inc(S["ca_const_in"], 16)
                sp.dma_start(wpool[:], a["w_pool_2"][ly].rearrange("g c d -> c g d")).then_inc(S["ca_const_in"], 16)
                sp.dma_start(psc[:], row_bc(a["pool_scale_2"][ly], CH)).then_inc(S["ca_const_in"], 16)
                load_wide(win2[ly], ph, 10, 3, True)
                with sp.Fori(0, 2) as i:
                    for u in range(8):
                        unit(At(ph.pieces + 48, 16, i), u, win2[ly][i, u], "wide")
                for nm_, c0, n_, _ in SEGS[ly]:
                    load_wide(win2[ly], phases[f"s{ly}{nm_}"], c0 + 2, n_)
                ahead(wout2[ly], phases[f"o2{ly}"], 0)
                last = phases[f"mx{ly}"]
                sp.wait_ge(S["pieces_used"], last.pieces)
                sp.dma_start(cpw[:], a["conv_pw_2"][ly].rearrange("(k p) n -> p k n", p=P)).then_inc(S["cf_in"], 16)
                sp.dma_start(cpb[:], a["conv_pw_b_2"][ly:ly + 1, :]).then_inc(S["cf_in"], 16)
                sp.dma_start(ropn[:, 0], a["cosn"].rearrange("(t p) n -> p t n", p=P)).then_inc(S["na_in"], 16)
                sp.dma_start(ropn[:, 1], a["sinn"].rearrange("(t p) n -> p t n", p=P)).then_inc(S["na_in"], 16)
                sp.dma_start(mask[:], a["mask"]).then_inc(S["na_in"], 16)
                sp.dma_start(turn[:], a["turn"]).then_inc(S["na_in"], 16)
                rpb = a["na_rpb_2"]
                for r2 in range(2):
                    for dr in range(6):
                        first = ly * NA_H * RPB_R * RPB_C + (5 - r2 + dr) * RPB_C + RPB_C // 2 - (GRID - 1)
                        sp.dma_start(bias[r2 * GRID:(r2 + 1) * GRID, :, dr * GRID:(dr + 1) * GRID],
                                     bass.AP(tensor=rpb.tensor, offset=first,
                                             ap=[[1, GRID], [RPB_R * RPB_C, NA_H], [1, GRID]]))\
                            .then_inc(S["bias_in"], 16)
                sp.wait_ge(S["o_taken"], o_total(ly + 1))
                sp.wait_ge(S["xs_out"], 16 * (ly + 1))
                sp.dma_start(x4[:, 0:2, :], xs_v).then_inc(S["x4r_in"], 16)
                if ly == 0:
                    sp.dma_start(x4[:, 2:4, :], ctx_v).then_inc(S["x4r_in"], 16)
                load_wide(wout2[ly], phases[f"o2{ly}"], 0, 4, True)

        @block.scalar
        def _(act):
            def consts():
                act.dma_start(ident[:], a["ident"]).then_inc(S["const_in"], 16)
                act.dma_start(sel[:], a["sel"]).then_inc(S["const_in"], 16)
                act.dma_start(vrow[:], a["vrows"]).then_inc(S["const_in"], 16)
                act.dma_start(brow[0:96, :], a["b_mod_2"].rearrange("l (k p) -> (l k) p", p=P)).then_inc(S["const_in"], 16)
                for k, nm_ in enumerate(("conv_dw_b_2", "conv_ln_g_2", "conv_ln_b_2")):
                    act.dma_start(brow[96 + 8 * k:104 + 8 * k, :],
                                  a[nm_].rearrange("l (k p) -> (l k) p", p=P)).then_inc(S["const_in"], 16)
                for ly in range(2):
                    act.dma_start(drow[:, ly, :],
                                  a["conv_dw_2"][ly].rearrange("k (c p) -> (k c) p", p=P)).then_inc(S["const_in"], 16)

            def at1_consts():
                act.dma_start(ropa[:, 0], a["cosa"].rearrange("(t p) n -> p t n", p=P)).then_inc(S["rope_in"], 16)
                act.dma_start(ropa[:, 1], a["sina"].rearrange("(t p) n -> p t n", p=P)).then_inc(S["rope_in"], 16)
                act.dma_start(ropb[:, 0], a["cosb"].rearrange("(t p) n -> p t n", p=P)).then_inc(S["rope_in"], 16)
                act.dma_start(ropb[:, 1], a["sinb"].rearrange("(t p) n -> p t n", p=P)).then_inc(S["rope_in"], 16)
                for k, nm_ in enumerate(("a_q_norm", "a_k_norm", "b_q_norm", "b_k_norm")):
                    act.dma_start(gbc[:, k], row_bc(a[nm_], P)).then_inc(S["rope_in"], 16)
                for k, nm_ in enumerate(("b_lambda_q1", "b_lambda_k1", "b_lambda_q2", "b_lambda_k2")):
                    act.dma_start(lamv[:, k], row_bc(a[nm_], P)).then_inc(S["rope_in"], 16)
                act.dma_start(sub_bc[:], row_bc(a["b_subln"], L)).then_inc(S["rope_in"], 16)

            norms = [0, 0]

            def root(src_x, ns, nt, x_ready, early=False):
                for k, t in enumerate((2, 3, 0, 1) if nt == 4 else (0, 1)):
                    if k == 0 and early:
                        act.wait_ge(S["ctx_in"], 16)
                    if k == (2 if early else 0):
                        x_ready()
                    if k >= 2:
                        act.wait_ge(S["ss_made"], norms[1] + k - 1)
                    act.activation(ns[:, t % 2], src_x[:, t], ACT.Square,
                                   accum_out=ss[:, t:t + 1]).then_inc(S["ss_made"], 1)
                norms[0] += 1
                norms[1] += nt
                act.wait_ge(S["var_made"], norms[0])
                act.activation(sd[:, 0:nt], rs[:, 0:nt], ACT.Sqrt).then_inc(S["sd_made"], 1)
                act.wait_ge(S["rs_made"], norms[0])

            def group_hi(g, dst, src):
                act.wait_ge(S["tg_full"], num(g + 1))
                act.activation(dst, src, ACT.Copy).then_inc(S["tg_hi"], 1)

            def norm(ph, src_x, ns, tm, dst, nt, x_ready, early=False):
                root(src_x, ns, nt, x_ready, early)

                def scale(t):
                    act.activation(ns[:, t % 2], src_x[:, t], ACT.Copy, scale=rs[:, t:t + 1]).then_inc(S["scaled"], 1)
                scale(0)
                scale(1)
                for t in range(nt):
                    for g in range(4):
                        group_hi(ph.groups + 4 * t + g, dst[0][:, 4 * g:4 * g + 4, t * P:(t + 1) * P],
                                 tm[:, g % 2].rearrange("p (k n) -> p k n", n=P))
                    if t + 2 < nt:
                        scale(t + 2)

            def gate_up(ph):
                def u_hi(c, off, f):
                    cols = slice(4 * (c + off) + 2 * f, 4 * (c + off) + 2 * f + 2) if isinstance(c, int) else \
                        bass.ds(c * 4 + (4 * off + 2 * f), 2)
                    group_hi(lap_at(ph.groups + 2 * off + f, 2, c), uT[0][:, cols, :],
                             tm1[:, f].rearrange("p (k n) -> p k n", n=L))

                def silus(c):
                    wait(act, "tp_done", num(lap_at(turned(ph), 2, c)))
                    for t in range(2):
                        pair_done(act, ph, 48, c, 0, t)
                        act.activation(ub[:, t], acc[t][:], ACT.Silu).then_inc(S["gate_act"], 1)

                for j in range(LOOK, 48 + LOOK):
                    hi_piece(act, ph.pieces, j)
                silus(0)
                with act.Fori(1, FC) as i:
                    p0 = At(ph.pieces, 48, i)
                    for j in range(LOOK, 48 + LOOK):
                        hi_piece(act, p0, j)
                        if j in (7, 9):
                            u_hi(i, -1, (7, 9).index(j))
                    silus(i)
                u_hi(FC - 1, 0, 0)
                u_hi(FC - 1, 0, 1)

            def stream(p0_of, laps, per, last=False):
                n_ = laps - 1 if last else laps
                with act.Fori(0, n_) as i:
                    for j in range(LOOK, per + LOOK):
                        hi_piece(act, At(p0_of, per, i), j)
                if last:
                    for j in range(LOOK, per):
                        hi_piece(act, p0_of + per * n_, j)

            consts()
            at1_consts()
            for j in range(LOOK):
                hi_piece(act, 0, j)
            norm(phases["n1"], x1, ns1, tm1, h1, 2, lambda: act.wait_ge(S["x_in"], 16))
            act.wait_ge(S["cols_taken"], 7)
            act.activation(cT[:].rearrange("p k c -> p c k"), vec[:, 5 * KT:7 * KT].rearrange("p (c k) -> p c k", c=2),
                           ACT.Silu).then_inc(S["silu_c"], 1)
            act.wait_ge(S["silu_c"], 1)
            act.activation(c_in[:, :, 0:2], cT[:], ACT.Copy).then_inc(S["silu_c"], 1)
            gate_up(phases["g1"])
            stream(phases["d1"].pieces, 2, 2 * len(DOWN_MOD))
            norm(phases["n2"], x1, ns1, tm1, h1, 2, lambda: act.wait_ge(S["acc_taken"], phases["n2"].taken))
            stream(phases["i1"].pieces, 9, 16)

            g0 = phases["at1"].groups
            act.wait_ge(S["lam_e"], 1)
            act.activation(lam[:, 2:4], lam[:, 0:2], ACT.Exp).then_inc(S["lam_e"], 1)
            act.wait_ge(S["qk_ss"], 1)
            act.activation(qsd[:], qss[:], ACT.Sqrt).then_inc(S["qk_sd"], 1)
            for g in range(13):
                act.wait_ge(S["cg_done"], g + 1)
                act.activation(qkT[:, 2 * g:2 * g + 2, :], cg[g % 2][:].rearrange("p (k n) -> p k n", n=L),
                               ACT.Copy).then_inc(S["cg_taken"], 1)

            def exps(q):
                act.wait_ge(S["m_ready"], q + 1)
                if q >= 2:
                    act.wait_ge(S["cg_done"], 13 + (q - 1 if q - 2 < 8 else 8 + (q - 8) // 2))
                for t in range(2):
                    ins = act.activation(pr1[:, q % 2, t], acc[q % 2][:, t * L:(t + 1) * L], ACT.Exp,
                                         bias=nm[:, q % 2, t:t + 1], scale=SCALE, accum_out=sm[:, q % 2, t:t + 1])
                ins.then_inc(S["p_made"], 1)

            def pt_copy(k):
                act.wait_ge(S["cg_done"], 14 + k)
                if k >= 2:
                    act.wait_ge(S["o_done"], k - 1)
                act.activation(pt1[:, k % 2], cg[(13 + k) % 2][:].rearrange("p (k n) -> p k n", n=L),
                               ACT.Copy).then_inc(S["cg_taken"], 1)

            def head_hi(q):
                group_hi(g0 + q, h1[0][:, q, :], tm1[:, q % 2, 0:L])

            exps(0)
            for q in range(8):
                exps(q + 1)
                pt_copy(q)
                if q:
                    head_hi(q - 1)
            exps(9)
            head_hi(7)
            for h in range(B_HEADS):
                pt_copy(8 + h)
                if h + 1 < B_HEADS:
                    exps(10 + 2 * h)
                    exps(11 + 2 * h)
            act.wait_ge(S["ob_made"], 1)
            act.activation(obs[:], obs[:], ACT.Sqrt).then_inc(S["qk_sd"], 1)
            for h in range(B_HEADS):
                group_hi(g0 + 8 + h, h1[0][:, 8 + 2 * h:10 + 2 * h, :], tm1[:, h % 2].rearrange("p (k n) -> p k n", n=L))
            stream(phases["o1"].pieces, 4, 16)
            norm(phases["n3"], x1, ns1, tm1, h1, 2, lambda: act.wait_ge(S["acc_taken"], phases["n3"].taken))
            gate_up(phases["g2"])
            stream(phases["d2"].pieces, 2, 88)
            root(x1, ns1, 2, lambda: act.wait_ge(S["acc_taken"], phases["n40"].taken))
            units = 0
            cgs = 13 + 12
            for ly in range(2):
                nt = NT[ly]

                def x_ready(ly=ly):
                    if ly == 0:
                        act.wait_ge(S["x4_in"], 2)
                    else:
                        act.wait_ge(S["acc_taken"], phases["n41"].taken)
                norm(phases[f"n4{ly}"], x4, ns2, tm2, hT, 4, x_ready, ly == 0)
                stream(phases[f"ca{ly}"].pieces, 5, 16)
                act.wait_ge(S["acc_taken"], phases[f"ca{ly}"].taken + 5 * nt)
                act.activation(ca[:, 1, 0:nt], ca[:, 1, 0:nt], ACT.Sigmoid).then_inc(S["gates_made"], 1)
                act.activation(gC[:, 0:nt], ca[:, 2, 0:nt], ACT.Silu).then_inc(S["gates_made"], 1)
                act.activation(ca[:, 4, 0:nt], ca[:, 4, 0:nt], ACT.Silu).then_inc(S["gates_made"], 1)
                act.wait_ge(S["pad_made"], 2 * (ly + 1))
                for c in range(4):
                    act.wait_ge(S["yt_done"], 4 * ly + c + 1)
                    act.activation(yT[:, c, 0:nt // 2, PAD:PAD + L],
                                   tp[c % 2][:, 0:nt * P].rearrange("p (s n) -> p s n", n=L),
                                   ACT.Copy).then_inc(S["yt_taken"], 1)
                for g in range(4):
                    act.wait_ge(S["pl_done"], 4 * ly + g + 1)
                    act.activation(pdT[:, g, 0:nt * P], cg[g % 2][:, 0:nt * P], ACT.Copy).then_inc(S["pl_taken"], 1)
                for nm_, _, n_, _ in SEGS[ly]:
                    stream(phases[f"s{ly}{nm_}"].pieces, n_, 16)

                act.wait_ge(S["z_made"], (5 if ly else 0) + 1)
                act.activation(sv[:, 0:nt], sv[:, 0:nt], ACT.Sqrt).then_inc(S["cf_sd"], 1)
                for t in range(nt):
                    k = (4 if ly else 0) + t
                    act.wait_ge(S["cz_done"], k + 1)
                    if t >= 2:
                        act.wait_ge(S["pw_done"], k - 1)
                    for c in range(4):
                        ins = act.activation(sT[:, t % 2, c * P:(c + 1) * P], cg[t % 2][:, c * P:(c + 1) * P], ACT.Silu,
                                             scale=cvec[:, 8 + 4 * ly + c:9 + 4 * ly + c],
                                             bias=cvec[:, 16 + 4 * ly + c:17 + 4 * ly + c])
                    ins.then_inc(S["s_made"], 1)

                act.wait_ge(S["acc_taken"], phases[f"mx{ly}"].taken)
                act.activation(qkvg[:, 3, 0:nt], qkvg[:, 3, 0:nt], ACT.Silu).then_inc(S["gates_made"], 1)
                U = 6 if nt == 4 else 4
                u0, kinds = units, kinds_of(nt)
                def stage_ctx(lap, n):
                    act.wait_ge(S["cg_done"], lap * 2 + (cgs + 2 * n))
                    cols = pair_cols(lap, n, 0, P)
                    ins = act.activation(st[:, 4:6], qkvg[:, 1, 2:4, cols], ACT.Copy)
                    if nt == 4:
                        ins = act.activation(st[:, 6:8], qkvg[:, 0, 2:4, cols], ACT.Copy)
                    ins.then_inc(S["st_act"], 1)

                def take_k(lap, n):
                    act.wait_ge(S["cg_done"], lap * 2 + (cgs + 2 * n + 2))
                    act.activation(T[:, CH:2 * CH], cg[1][:], ACT.Copy).then_inc(S["cg_taken"], 1)

                def na_exp(lap, u):
                    act.wait_ge(S["m_ready"], lap * U + (16 + u0 + u + 1))
                    if kinds[u % U][1] < 2:
                        act.activation(pr[:, u % 2], acc[u % 2][:], ACT.Exp, bias=nm[:, u % 2, 0:1],
                                       accum_out=sm[:, u % 2, 0:1]).then_inc(S["p_made"], 1)
                    else:
                        for t in range(2):
                            ins = act.activation(pr[:, u % 2, t * L:(t + 1) * L], acc[u % 2][:, t * L:(t + 1) * L],
                                                 ACT.Exp, bias=nm[:, u % 2, t:t + 1],
                                                 accum_out=sm[:, u % 2, t:t + 1])
                        ins.then_inc(S["p_made"], 1)

                def na_pt(lap, u):
                    act.wait_ge(S["pt_done"], lap * U + (u0 + u + 1))
                    act.wait_ge(S["o_done"], lap * U + (12 + max(u0 + u - 1, 0)))
                    act.activation(pt[:, u % 2], tp[u % 2][:], ACT.Copy).then_inc(S["pt_taken"], 1)

                def step(lap, k, end):
                    if k == 1 and end > U:
                        stage_ctx(lap, 1)
                    if k + 1 < end:
                        na_exp(lap, k + 1)
                    if k == U - 2 and end > U:
                        take_k(lap, 1)
                    if k < end:
                        na_pt(lap, k)

                stage_ctx(0, 0)
                take_k(0, 0)
                na_exp(0, 0)
                na_exp(0, 1)
                na_pt(0, 0)
                na_laps(act, step, nt)
                units += 8 * U
                cgs += 16
                g0 = phases[f"mx{ly}"].groups
                for t in range(nt):
                    for g in range(4):
                        group_hi(g0 + 4 * t + g, hT[0][:, 4 * g:4 * g + 4, t * P:(t + 1) * P],
                                 tm2[:, g % 2].rearrange("p (k n) -> p k n", n=P))
                for k in range(2 * nt):
                    act.wait_ge(S["gs_done"], 8 * ly + k + 1)
                    act.activation(gatb[:, k // 4, k % 4 * CH:(k % 4 + 1) * CH], cg[k % 2][:],
                                   ACT.Copy).then_inc(S["gs_taken"], 1)
                stream(phases[f"o2{ly}"].pieces, 4, 16, last=ly == 1)
            root(x4, ns2, 2, lambda: act.wait_ge(S["acc_taken"], phases["end"].taken))
            act.wait_ge(S["y_made"], 1)
            act.dma_start(out_v, x4[:, 0:2, :]).then_inc(S["y_out"], 16)
            act.wait_ge(S["y_out"], 16)

        @block.vector
        def _(dve):
            link = Link(dve, S["dve_step"])
            norms = [0, 0]

            def var_root(nt):
                norms[0] += 1
                norms[1] += nt
                dve.wait_ge(S["ss_made"], norms[1])
                dve.tensor_scalar(rs[:, 0:nt], ss[:, 0:nt], 1.0 / D, EPS, ALU.mult, ALU.add).then_inc(S["var_made"], 1)
                dve.wait_ge(S["sd_made"], norms[0])
                dve.reciprocal(rs[:, 0:nt], sd[:, 0:nt]).then_inc(S["rs_made"], 1)

            def group_lo(g, dst, dst_hi, src):
                dve.wait_ge(S["tg_hi"], num(g + 1))
                dve.tensor_tensor(dst, src, dst_hi, ALU.subtract).then_inc(S["tg_lo"], 1)

            def take(turns, g, k, tm, gain, shift):
                dve.wait_ge(S["tp_done"], turns)
                wait(dve, "tg_lo", g - 1)
                src = tp[k % 2][:].rearrange("p (k n) -> p k n", n=P)
                tv = tm[:, k % 2].rearrange("p (k n) -> p k n", n=P)
                if gain is None:
                    dve.tensor_copy(tv, src).then_inc(S["tg_full"], 1)
                    return
                if shift is None:
                    ins = dve.tensor_tensor(tv, src, gain[:, 4 * k:4 * k + 4].unsqueeze(2).broadcast_to([P, 4, P]),
                                            ALU.mult)
                else:
                    for kt in range(4 * k, 4 * k + 4):
                        ins = dve.tensor_scalar(tv[:, kt % 4], src[:, kt % 4], gain[:, kt:kt + 1], shift[:, kt:kt + 1],
                                                ALU.mult, ALU.add)
                ins.then_inc(S["tg_full"], 1)

            def groups(ph, nt, tm, dst, gain_of):
                g0 = ph.groups

                def rest(m):
                    t, k = divmod(m, 4)
                    s = slice(4 * k, 4 * k + 4)
                    group_lo(g0 + m, dst[1][:, s, t * P:(t + 1) * P], dst[0][:, s, t * P:(t + 1) * P].bitcast(F32),
                             tm[:, k % 2].rearrange("p (k n) -> p k n", n=P))
                for m in range(4 * nt):
                    t, k = divmod(m, 4)
                    take(turned(ph) + m + 1, g0 + m, k, tm, *gain_of(t))
                    if m:
                        rest(m - 1)
                rest(4 * nt - 1)

            def norm(ph, tm, dst, nt, gain_of):
                var_root(nt)
                groups(ph, nt, tm, dst, gain_of)

            def gate_up(ph, gates, ly, rows):
                def u_part(c, off, part):
                    if part == 4:
                        first = 48 * ly + 4 * off
                        mod_cols(dve, lap_at(rows + off, 1, c), modT[:, first + 4 * c:first + 4 * c + 4, :]
                                 if isinstance(c, int) else modT[:, bass.ds(c * 4 + first, 4), :])
                        return
                    f = part % 2
                    if part < 2:
                        dve.wait_ge(S["tp_done"], num(lap_at(turned(ph) + 2 * off + f + 1, 2, c)))
                        dve.wait_ge(S["tg_lo"], num(lap_at(ph.groups + 2 * off + f - 1, 2, c)))
                        dve.tensor_copy(tm1[:, f], tp[f][:]).then_inc(S["tg_full"], 1)
                        return
                    cols = slice(4 * (c + off) + 2 * f, 4 * (c + off) + 2 * f + 2) if isinstance(c, int) else \
                        bass.ds(c * 4 + (4 * off + 2 * f), 2)
                    group_lo(lap_at(ph.groups + 2 * off + f, 2, c), uT[1][:, cols, :],
                             uT[0][:, cols, :].bitcast(F32), tm1[:, f].rearrange("p (k n) -> p k n", n=L))

                def products(c):
                    for t in range(2):
                        dve.wait_ge(S["gate_act"], num(lap_at(gates + t + 1, 2, c)))
                        pair_done(dve, ph, 48, c, 1, t)
                        dve.tensor_tensor(ub[:, t], ub[:, t], acc[2 + t][:], ALU.mult).then_inc(S["acc_taken"], 1)
                    mod_row(dve, GATE_UP, lap_at(ph.pieces, 48, c), lap_at(rows, 1, c))

                for j in range(LOOK, 48 + LOOK):
                    lo_piece(dve, ph.pieces, j)
                products(0)
                with dve.Fori(1, FC) as i:
                    p0 = At(ph.pieces, 48, i)
                    for j in range(LOOK, 48 + LOOK):
                        lo_piece(dve, p0, j)
                        if j in (5, 6, 8, 10, 12):
                            u_part(i, -1, (5, 6, 8, 10, 12).index(j))
                    products(i)
                for part in range(5):
                    u_part(FC - 1, 0, part)

            def down_proj(ph, order):
                per = 2 * len(order)
                with dve.Fori(0, 2) as i:
                    p0 = At(ph.pieces, per, i)
                    for j in range(LOOK, per + LOOK):
                        lo_piece(dve, p0, j)
                    if order is DOWN_MOD:
                        mod_row(dve, order, p0, At(FC, 1, i))
                    for b in range(4):
                        pair_done(dve, ph, per, i, b // 2, b % 2)
                        xv = x1[:, b % 2, bass.ds(i * (2 * CH) + b // 2 * CH, CH)]
                        dve.scalar_tensor_tensor(out=xv, in0=acc[b][:], scalar=0.5, in1=xv, op0=ALU.mult,
                                                 op1=ALU.add).then_inc(S["acc_taken"], 1)
                    if order is DOWN_MOD:
                        mod_cols(dve, At(FC, 1, i), modT[:, bass.ds(i * 48 + 4 * FC, 4), :])

            def stream(ph, laps, nt, evac, last=False, extra=None):
                n_ = laps - 1 if last else laps

                def one(i, ahead):
                    for j in range(LOOK, 16 + LOOK if ahead else 16):
                        lo_piece(dve, At(ph.pieces, 16, i) if not isinstance(i, int) else ph.pieces + 16 * i, j)
                        if extra:
                            extra(i, j - LOOK)
                    for t in range(nt):
                        bank_done(dve, ph, nt, i, t)
                        evac(i, t)
                with dve.Fori(0, n_) as i:
                    one(i, True)
                if last:
                    one(n_, False)

            dve.memset(ones[:], 1.0).then_inc(S["cols_taken"], 1)
            dve.memset(dw[:], 0.0).then_inc(S["cols_taken"], 1)
            dve.wait_ge(S["cols_taken"], 2)
            for k, (dst, c0, c1) in enumerate(((vec[:], 0, NV), (bmod[:], 0, 96), (cvec[:], 96, 120),
                                               (dw[:, 0, 0:124], 0, 124), (dw[:, 1, 0:124], 0, 124))):
                bank = acc[(0, 1, 1, 2, 3)[k]]
                dve.wait_ge(S["cols_made"], (1, 2, 2, 3, 4)[k])
                dve.tensor_copy(dst, bank[:, c0:c1]).then_inc(S["cols_taken"], 1)
            for j in range(LOOK):
                lo_piece(dve, 0, j)
            dve.wait_ge(S["cols_taken"], 7)
            norm(phases["n1"], tm1, h1, 2, lambda t: (vec[:, 0:KT], None))
            dve.wait_ge(S["silu_c"], 2)
            dve.tensor_tensor(c_in[:, :, 2:4], cT[:], c_in[:, :, 0:2].bitcast(F32), ALU.subtract).then_inc(S["c_split"], 1)
            gate_up(phases["g1"], 0, 0, 0)
            down_proj(phases["d1"], DOWN_MOD)
            norm(phases["n2"], tm1, h1, 2, lambda t: (vec[:, KT:2 * KT], None))

            def proj_take(i, t):
                dve.tensor_copy(proj[:, t, bass.ds(i * CH, CH)], acc[t][:]).then_inc(S["acc_taken"], 1)
            stream(phases["i1"], 9, 2, proj_take)

            dve.wait_ge(S["rope_in"], 16 * 13)
            for k in range(2):
                ins = dve.tensor_tensor_reduce(rt[:, 0, 0:P], lamv[:, 2 * k], lamv[:, 2 * k + 1], 1.0, 0.0, ALU.mult,
                                               ALU.add, lam[:, k:k + 1])
                if k == 0:
                    link(ins)
            ins.then_inc(S["lam_e"], 1)
            dve.wait_ge(S["lam_e"], 1)
            dve.wait_ge(S["acc_taken"], phases["at1"].taken)
            parts = ((0, 10, 0), (B_COL, 16, 10))
            for t in range(2):
                for c0, nh, s0 in parts:
                    xv = proj[:, t, c0:c0 + nh * HD].rearrange("p (h d) -> p h d", d=HD)
                    sq = rt[:, 0, 0:nh * HD].rearrange("p (h d) -> p h d", d=HD)
                    link(dve.tensor_tensor(sq, xv, xv, ALU.mult))
                    link(dve.tensor_reduce(qss[:, t, s0:s0 + nh], sq, AX, ALU.add))
            dve.tensor_scalar(qss[:], qss[:], 1.0 / HD, EPS, ALU.mult, ALU.add).then_inc(S["qk_ss"], 1)
            dve.wait_ge(S["qk_sd"], 1)
            link(dve.reciprocal(qsd[:], qsd[:]))
            for t in range(2):
                for c0, nh, s0 in parts:
                    xv = proj[:, t, c0:c0 + nh * HD].rearrange("p (h d) -> p h d", d=HD)
                    link(dve.tensor_tensor(xv, xv, qsd[:, t, s0:s0 + nh].unsqueeze(2).broadcast_to([P, nh, HD]), ALU.mult))
                    nq = 8
                    for k, (ha, hb) in enumerate(((0, nq), (nq, nh))):
                        g = gbc[:, (0 if s0 == 0 else 2) + k].unsqueeze(1).broadcast_to([P, hb - ha, HD])
                        link(dve.tensor_tensor(xv[:, ha:hb], xv[:, ha:hb], g, ALU.mult))
                    w = HD if s0 == 0 else 32
                    nb, half = (2, 32) if s0 == 0 else (1, 16)
                    cs = ropa if s0 == 0 else ropb
                    r1 = rt[:, 0, 0:nh * w].rearrange("p (h d) -> p h d", d=w)
                    r2 = rt[:, 1, 0:nh * w].rearrange("p (h d) -> p h d", d=w)
                    xw = xv[:, :, 0:w]
                    link(dve.tensor_tensor(r1, xw, cs[:, 0, t].unsqueeze(1).broadcast_to([P, nh, w]), ALU.mult))
                    for blk in range(nb):
                        for s in range(2):
                            d0 = blk * 2 * half + s * half
                            s1 = blk * 2 * half + (1 - s) * half
                            link(dve.tensor_tensor(r2[:, :, d0:d0 + half], xw[:, :, s1:s1 + half],
                                                   cs[:, 1, t, d0:d0 + half].unsqueeze(1).broadcast_to([P, nh, half]),
                                                   ALU.mult))
                    ins = dve.tensor_tensor(xw, r1, r2, ALU.add)
                    if (t, s0) == (1, 10):
                        ins.then_inc(S["roped"], 1)
                    else:
                        link(ins)
            link(dve.tensor_scalar(sub_bc[:], sub_bc[:], 1.0 - LAMBDA_INIT, None, ALU.mult))
            dve.wait_ge(S["lam_e"], 2)
            link(dve.tensor_tensor(lam[:, 0:1], lam[:, 3:4], lam[:, 2:3], ALU.subtract))
            link(dve.tensor_scalar(lam[:, 0:1], lam[:, 0:1], LAMBDA_INIT, None, ALU.subtract))

            def maxes(q):
                dve.wait_ge(S["s_done"], q + 1)
                link(dve.tensor_reduce(mx[:, q % 2], acc[q % 2][:].rearrange("p (t n) -> p t n", n=L), AX, ALU.max))
                dve.tensor_scalar(nm[:, q % 2], mx[:, q % 2], -SCALE, None, ALU.mult).then_inc(S["m_ready"], 1)

            g0 = phases["at1"].groups
            def normalise(q):
                dve.wait_ge(S["p_made"], q + 1)
                link(dve.reciprocal(rr[:, q % 2], sm[:, q % 2]))
                dve.tensor_tensor(pr1[:, q % 2], pr1[:, q % 2], rr[:, q % 2].unsqueeze(2).broadcast_to([P, 2, L]),
                                  ALU.mult).then_inc(S["pn_made"], 1)

            def head_out(q):
                dve.wait_ge(S["o_done"], q + 1)
                dve.wait_ge(S["tg_lo"], g0 + q - 1)
                dve.tensor_copy(tm1[:, q % 2, 0:L], acc[2 + q % 2][:, 0:L]).then_inc(S["tg_full"], 1)
                group_lo(g0 + q, h1[1][:, q], h1[0][:, q].bitcast(F32), tm1[:, q % 2, 0:L])

            def difference(h):
                dve.wait_ge(S["p_made"], 10 + 2 * h)
                link(dve.reciprocal(rr[:], sm[:]))
                link(dve.tensor_scalar(rr[:, 1], rr[:, 1], lam[:, 0:1], None, ALU.mult))
                for t in range(2):
                    link(dve.tensor_scalar(pr1[:, 1, t], pr1[:, 1, t], rr[:, 1, t:t + 1], None, ALU.mult))
                    ins = dve.scalar_tensor_tensor(out=pr1[:, 0, t], in0=pr1[:, 0, t], scalar=rr[:, 0, t:t + 1],
                                                   in1=pr1[:, 1, t], op0=ALU.mult, op1=ALU.add)
                    if t == 0:
                        link(ins)
                ins.then_inc(S["pn_made"], 1)

            def diff_out(h):
                dve.wait_ge(S["o_done"], 9 + h)
                dve.tensor_copy(ob[:, h], acc[2 + h % 2][:].rearrange("p (t n) -> p t n", n=L)).then_inc(S["o_taken"], 1)
                dve.wait_ge(S["o_taken"], h + 1)
                for t in range(2):
                    link(dve.tensor_tensor_reduce(rt[:, 1, 0:L], ob[:, h, t], ob[:, h, t], 1.0, 0.0, ALU.mult, ALU.add,
                                                  obs[:, 2 * h + t:2 * h + t + 1]))

            maxes(0)
            for q in range(8):
                maxes(q + 1)
                normalise(q)
                if q:
                    head_out(q - 1)
            maxes(9)
            head_out(7)
            for h in range(B_HEADS):
                difference(h)
                if h + 1 < B_HEADS:
                    maxes(10 + 2 * h)
                    maxes(11 + 2 * h)
                if h:
                    diff_out(h - 1)
            diff_out(B_HEADS - 1)
            dve.tensor_scalar(obs[:], obs[:], 1.0 / L, EPS, ALU.mult, ALU.add).then_inc(S["ob_made"], 1)
            dve.wait_ge(S["qk_sd"], 2)
            link(dve.reciprocal(obs[:], obs[:]))
            for h in range(B_HEADS):
                for t in range(2):
                    ins = dve.scalar_tensor_tensor(out=ob[:, h, t], in0=ob[:, h, t],
                                                   scalar=obs[:, 2 * h + t:2 * h + t + 1], in1=sub_bc[:], op0=ALU.mult,
                                                   op1=ALU.mult)
                ins.then_inc(S["ob_made"], 1)
            for h in range(B_HEADS):
                dve.wait_ge(S["tp_done"], g0 + h + 1)
                dve.wait_ge(S["tg_lo"], g0 + 8 + h - 1)
                dve.tensor_copy(tm1[:, h % 2], tp[h % 2][:]).then_inc(S["tg_full"], 1)
                ks = slice(8 + 2 * h, 10 + 2 * h)
                group_lo(g0 + 8 + h, h1[1][:, ks, :], h1[0][:, ks, :].bitcast(F32),
                         tm1[:, h % 2].rearrange("p (k n) -> p k n", n=L))

            def x_add(i, t):
                xv = x1[:, t, bass.ds(i * CH, CH)]
                dve.tensor_tensor(xv, acc[t][:], xv, ALU.add).then_inc(S["acc_taken"], 1)
            stream(phases["o1"], 4, 2, x_add)
            norm(phases["n3"], tm1, h1, 2, lambda t: (vec[:, 2 * KT:3 * KT], None))
            gate_up(phases["g2"], 2 * FC, 1, FC + 2)
            down_proj(phases["d2"], DOWN)
            var_root(2)
            dve.wait_ge(S["rs_made"], norms[0])
            dve.wait_ge(S["fin_in"], 16)
            for t in range(2):
                dve.scalar_tensor_tensor(out=x4[:, t], in0=x1[:, t], scalar=rs[:, t:t + 1], in1=ogain[:], op0=ALU.mult,
                                         op1=ALU.mult).then_inc(S["x4_in"], 1)

            units = 0
            for ly in range(2):
                nt = NT[ly]
                dve.wait_ge(S["mt_taken"], 24)
                for c in range(2):
                    b0 = 48 * ly
                    mod = modT[:, b0:b0 + 48, c]
                    link(dve.tensor_tensor(mB[:, c], mod[:, 0:KT], bmod[:, b0:b0 + KT], ALU.add))
                    link(dve.tensor_tensor(mG[:, c], mod[:, 2 * KT:3 * KT], bmod[:, b0 + 2 * KT:b0 + 3 * KT], ALU.add))
                    link(dve.tensor_tensor(mA[:, c], mod[:, KT:2 * KT], bmod[:, b0 + KT:b0 + 2 * KT], ALU.add))
                    link(dve.scalar_tensor_tensor(out=mA[:, c], in0=mA[:, c], scalar=1.0,
                                                  in1=vec[:, (3 + ly) * KT:(4 + ly) * KT], op0=ALU.add, op1=ALU.mult))
                norm(phases[f"n4{ly}"], tm2, hT, 4, lambda t: (mA[:, t // 2], mB[:, t // 2]))

                dve.wait_ge(S["xs_out"], 16 * (ly + 1))

                def ca_take(i, t):
                    dve.tensor_copy(ca[:, i, t], acc[t][:]).then_inc(S["acc_taken"], 1)
                stream(phases[f"ca{ly}"], 5, nt, ca_take)
                dve.wait_ge(S["gates_made"], 4 * ly + 1)
                dve.tensor_tensor(ca[:, 0, 0:nt], ca[:, 0, 0:nt], ca[:, 1, 0:nt], ALU.mult).then_inc(S["glu_made"], 1)
                for c in range(4):
                    dve.memset(cv[:, c], 0.0).then_inc(S["conv_step"], 1)
                dve.wait_ge(S["ca_const_in"], 48 * (ly + 1))
                dve.wait_ge(S["gates_made"], 4 * ly + 3)
                for t in range(nt):
                    dve.wait_ge(S["py_done"], (4 if ly else 0) + t + 1)
                    link(dve.tensor_tensor(ya[:, t], acc[t][:], psc[:], ALU.mult))
                    dve.tensor_tensor(ya[:, t], ya[:, t], ca[:, 4, t], ALU.mult).then_inc(S["py_taken"], 1)
                dve.wait_ge(S["py_taken"], (4 if ly else 0) + nt)
                dve.wait_ge(S["yt_taken"], 4 * ly + 4)
                ns_ = nt // 2
                for nm_, c0, n_, snt in SEGS[ly]:
                    def tap(i, s, c0=c0):
                        j = i + c0
                        dve.wait_ge(S["conv_step"], j * 16 + (132 * ly + s + 1))
                        c, kk = s % 4, s // 4
                        yv = yT[:, c, 0:ns_, bass.ds(j * 4 + kk, L)]
                        av = cv[:, c, 0:nt * P].rearrange("p (s n) -> p s n", n=L)
                        dve.scalar_tensor_tensor(out=av, in0=yv, scalar=dw[:, ly, bass.ds(j * 16 + s, 1)], in1=av,
                                                 op0=ALU.mult, op1=ALU.add).then_inc(S["conv_step"], 1)

                    def take4(i, t, c0=c0):
                        dve.tensor_copy(qkvg[:, c0 // 2, t, bass.ds(i * CH, CH)], acc[t][:]).then_inc(S["acc_taken"], 1)
                    stream(phases[f"s{ly}{nm_}"], n_, snt, take4, extra=tap)

                dve.wait_ge(S["conv_step"], 132 * (ly + 1))
                for c in range(4):
                    av = cv[:, c, 0:nt * P]
                    dve.tensor_scalar(av, av, cvec[:, 4 * ly + c:4 * ly + c + 1], None, ALU.add).then_inc(S["cf_b"], 1)
                for t in range(nt):
                    dve.wait_ge(S["cf_done"], (4 if ly else 0) + t + 1)
                    link(dve.bn_stats(bn[:, t], acc[t][:]))
                for t in range(nt):
                    ins = dve.bn_aggr(mv[:, t], bn[:, t])
                link(ins)
                dve.tensor_scalar(sv[:, 0:nt], mv[:, 0:nt, 1], LN_EPS, None, ALU.add).then_inc(S["z_made"], 1)
                dve.wait_ge(S["cf_sd"], ly + 1)
                link(dve.reciprocal(sv[:, 0:nt], sv[:, 0:nt]))

                def conv_gate(t):
                    dve.wait_ge(S["pw_done"], (4 if ly else 0) + t + 1)
                    dve.tensor_tensor(gC[:, t], tp[t % 2][:], gC[:, t], ALU.mult).then_inc(S["yc_made"], 1)
                for t in range(nt):
                    if t >= 2:
                        dve.wait_ge(S["cz_done"], (4 if ly else 0) + t - 1)
                    dve.tensor_scalar(zb[:, t % 2], acc[t][:], mv[:, t, 0:1], sv[:, t:t + 1], ALU.subtract,
                                      ALU.mult).then_inc(S["z_made"], 1)
                    if t >= 1:
                        conv_gate(t - 1)
                conv_gate(nt - 1)

                U = 6 if nt == 4 else 4
                u0, kinds = units, kinds_of(nt)
                ot0 = B_HEADS + u0
                dve.wait_ge(S["na_in"], 64 * (ly + 1))
                dve.wait_ge(S["gates_made"], 4 * ly + 4)
                dve.wait_ge(S["acc_taken"], phases[f"mx{ly}"].taken)
                cg0 = 25 + 16 * ly
                def rope(lap, n, s):
                    if s == 0:
                        dve.wait_ge(S["cg_done"], lap * 2 + (cg0 + 2 * n))
                    xv = qkvg[:, s, 0:2, pair_cols(lap, n, 0, P)]
                    link(dve.tensor_tensor(rn[:, 0], xv, ropn[:, 0], ALU.mult))
                    xh, rh, sh = (v.rearrange("p t (b h n) -> p t b h n", h=2, n=16) for v in (xv, rn[:, 1], ropn[:, 1]))
                    for hf in range(2):
                        link(dve.tensor_tensor(rh[:, :, :, hf, :], xh[:, :, :, 1 - hf, :], sh[:, :, :, hf, :], ALU.mult))
                    ins = dve.tensor_tensor(st[:, 2 * s:2 * s + 2], rn[:, 0], rn[:, 1], ALU.add)
                    if s == 0:
                        link(ins)
                    else:
                        ins.then_inc(S["st_dve"], 1)

                def take_q(lap, n):
                    dve.wait_ge(S["cg_done"], lap * 2 + (cg0 + 2 * n + 1))
                    dve.tensor_scalar(T[:, 0:nt * P], cg[0][:, 0:nt * P], NA_D ** -0.5, None,
                                      ALU.mult).then_inc(S["cg_taken"], 1)

                def na_max(lap, u):
                    dve.wait_ge(S["s_done"], lap * U + (16 + u0 + u + 1))
                    if kinds[u % U][1] < 2:
                        link(dve.tensor_reduce(mx[:, u % 2, 0:1], acc[u % 2][:], AX, ALU.max))
                        dve.tensor_scalar(nm[:, u % 2, 0:1], mx[:, u % 2, 0:1], -1.0, None,
                                          ALU.mult).then_inc(S["m_ready"], 1)
                    else:
                        link(dve.tensor_reduce(mx[:, u % 2], acc[u % 2][:].rearrange("p (t n) -> p t n", n=L), AX,
                                               ALU.max))
                        dve.tensor_scalar(nm[:, u % 2], mx[:, u % 2], -1.0, None, ALU.mult).then_inc(S["m_ready"], 1)

                def na_sum(lap, u):
                    dve.wait_ge(S["p_made"], lap * U + (16 + u0 + u + 1))
                    dve.wait_ge(S["o_taken"], lap * U + (ot0 + u - 1))
                    link(dve.reciprocal(rr[:, u % 2], sm[:, u % 2]) if kinds[u % U][1] == 2 else
                         dve.reciprocal(rr[:, u % 2, 0:1], sm[:, u % 2, 0:1]))

                def na_out(lap, u):
                    e, t = kinds[u % U]
                    dve.wait_ge(S["o_done"], lap * U + (12 + u0 + u + 1))
                    for k, tt in enumerate((2, 3) if t == 2 else (t,)):
                        gv = qkvg[:, 3, tt, pair_cols(lap, u // U, e * NA_D, NA_D)]
                        ins = dve.scalar_tensor_tensor(out=gv, in0=acc[2 + u % 2][:, k * NA_D:(k + 1) * NA_D],
                                                       scalar=rr[:, u % 2, k:k + 1], in1=gv, op0=ALU.mult, op1=ALU.mult)
                    ins.then_inc(S["o_taken"], 1)

                def step(lap, k, end):
                    na_sum(lap, k - 1)
                    if k == 1 and end > U:
                        rope(lap, 1, 0)
                    if k + 1 < end:
                        na_max(lap, k + 1)
                    if k == U - 2 and end > U:
                        take_q(lap, 1)
                    na_out(lap, k - 1)
                    if k == 1 and end > U:
                        rope(lap, 1, 1)

                rope(0, 0, 0)
                rope(0, 0, 1)
                take_q(0, 0)
                na_max(0, 0)
                na_max(0, 1)
                na_laps(dve, step, nt, link)
                units += 8 * U
                groups(phases[f"mx{ly}"], nt, tm2, hT, lambda t: (None, None))
                for k in range(2 * nt):
                    wait(dve, "gs_done", 8 * ly + k - 1)
                    dve.tensor_tensor(dg[:, k % 2].rearrange("p (k n) -> p k n", n=P),
                                      ident[:].unsqueeze(1).broadcast_to([P, 4, P]),
                                      mG[:, k // 4, k % 4 * 4:k % 4 * 4 + 4].unsqueeze(2).broadcast_to([P, 4, P]),
                                      ALU.mult).then_inc(S["gate_diag"], 1)
                dve.wait_ge(S["x4r_in"], 32 if ly == 0 else 48)
                dve.wait_ge(S["gs_taken"], 8 * ly + 2 * nt)

                def add_gated(i, t):
                    cols = bass.ds(i * CH, CH)
                    dve.wait_ge(S["acc_taken"], num(lap_at(phases[f"o2{ly}"].taken + t - 1, nt, i)))
                    dve.tensor_tensor(tm2[:, t % 2], acc[t][:], gatb[:, t // 2, cols], ALU.mult)\
                       .then_inc(S["tmp_made"], 1)
                    v = lap_at((16 if ly else 0) + t + 1, nt, i)
                    dve.wait_ge(S["tmp_made"], num(v))
                    xv = x4[:, t, cols]
                    dve.tensor_tensor(xv, tm2[:, t % 2], xv, ALU.add).then_inc(S["acc_taken"], 1)
                stream(phases[f"o2{ly}"], 4, nt, add_gated, last=ly == 1)
            var_root(2)
            dve.wait_ge(S["rs_made"], norms[0])
            dve.wait_ge(S["fin_in"], 32)
            for t in range(2):
                ins = dve.scalar_tensor_tensor(out=x4[:, t], in0=x4[:, t], scalar=rs[:, t:t + 1], in1=fgain[:],
                                               op0=ALU.mult, op1=ALU.mult)
                if t == 0:
                    link(ins)
            ins.then_inc(S["y_made"], 1)

        @block.tensor
        def _(pe):
            def bank_free(g, m):
                wait(pe, "tg_full", g - 1 if m >= 2 else g)

            def turn4(g, m, src):
                for k in range(4):
                    ins = pe.transpose(tp[m % 2][:, k * P:(k + 1) * P], src(k), ident[:])
                ins.then_inc(S["tp_done"], 1)

            scaled = [0]

            def norm(ph, ns, nt):
                for t in range(nt):
                    scaled[0] += 1
                    pe.wait_ge(S["scaled"], scaled[0])
                    for g in range(4):
                        bank_free(ph.groups + 4 * t + g, 4 * t + g)
                        turn4(0, g, lambda k: ns[:, t % 2, (4 * g + k) * P:(4 * g + k + 1) * P])

            def begin(ph):
                pe.wait_ge(S["tg_lo"], ph.groups)
                wait(pe, "acc_taken", ph.taken)

            def gate_up(ph, gates, rows):
                begin(ph)

                def u_turn(c, off):
                    pe.wait_ge(S["acc_taken"], num(lap_at(ph.taken + 2 * off + 2, 2, c)))
                    pe.wait_ge(S["tg_full"], num(lap_at(ph.groups + 2 * off, 2, c)))
                    for f in range(2):
                        for k in range(2):
                            for t in range(2):
                                ins = pe.transpose(tp[f][:, k * L + t * P:k * L + (t + 1) * P],
                                                   ub[:, t, (2 * f + k) * P:(2 * f + k + 1) * P], ident[:])
                        ins.then_inc(S["tp_done"], 1)
                    mod_turn(pe, lap_at(rows + off, 1, c))

                pair_pieces(pe, GATE_UP, h1, KT, ph.pieces, range(48), lambda half, t: None, rows)
                with pe.Fori(1, FC) as i:
                    def bank_free(half, t):
                        if half == 0:
                            pe.wait_ge(S["gate_act"], num(At(gates + t - 1, 2, i)))
                        else:
                            pe.wait_ge(S["acc_taken"], num(At(ph.taken + t - 1, 2, i)))
                    p0 = At(ph.pieces, 48, i)
                    pair_pieces(pe, GATE_UP, h1, KT, p0, range(4), bank_free)
                    u_turn(i, -1)
                    pair_pieces(pe, GATE_UP, h1, KT, p0, range(4, 48), bank_free, At(rows, 1, i))
                u_turn(FC - 1, 0)

            def down_proj(ph, order):
                begin(ph)
                per = 2 * len(order)
                with pe.Fori(0, 2) as i:
                    pair_pieces(pe, order, uT, FT, At(ph.pieces, per, i), range(per), lambda half, t: pe.wait_ge(
                        S["acc_taken"], num(At(ph.taken + 2 * half + t + 1 - 4, 4, i))), At(FC, 1, i))
                    if order is DOWN_MOD:
                        mod_turn(pe, At(FC, 1, i))

            def stream(ph, src, laps, nt):
                begin(ph)
                with pe.Fori(0, laps) as i:
                    chunk_pieces(pe, src, nt, At(ph.pieces, 16, i), At(ph.taken, nt, i), range(16))

            pe.wait_ge(S["const_in"], 16 * 9)
            for k, (src, rows) in enumerate(((vrow[:], NV), (brow[:], 120), (drow[:, 0], 124), (drow[:, 1], 124))):
                pe.transpose(acc[k][:, 0:rows], src, ident[0:rows, 0:rows]).then_inc(S["cols_made"], 1)
            norm(phases["n1"], ns1, 2)
            pe.wait_ge(S["cols_taken"], 7)
            pe.wait_ge(S["c_split"], 1)
            gate_up(phases["g1"], 0, 0)
            down_proj(phases["d1"], DOWN_MOD)
            norm(phases["n2"], ns1, 2)
            stream(phases["i1"], h1, 9, 2)

            pe.wait_ge(S["roped"], 1)

            def head_cols(hh):
                return hh * HD if hh < 10 else B_COL + (hh - 10) * HD
            for g in range(13):
                if g >= 2:
                    pe.wait_ge(S["cg_taken"], g - 1)
                for e in range(2):
                    for t in range(2):
                        c0 = head_cols(2 * g + e)
                        ins = pe.transpose(cg[g % 2][:, e * L + t * P:e * L + (t + 1) * P], proj[:, t, c0:c0 + HD], ident[:])
                ins.then_inc(S["cg_done"], 1)
            pe.wait_ge(S["cg_taken"], 13)
            wait(pe, "acc_taken", phases["at1"].taken)

            def scores(q):
                if q >= 2:
                    pe.wait_ge(S["p_made"], q - 1)
                qh, kh = (q, 8 + q // 4) if q < 8 else (10 + q - 8, 18 + q - 8)
                for t in range(2):
                    ins = pe.matmul(acc[q % 2][:, t * L:(t + 1) * L], qkT[:, qh, t * P:(t + 1) * P], qkT[:, kh, :],
                                    start=True, stop=True)
                ins.then_inc(S["s_done"], 1)

            def turn_p(k, pv):
                pe.wait_ge(S["pn_made"], k + 1)
                pe.wait_ge(S["cg_taken"], 12 + k)
                for j in range(2):
                    for t in range(2):
                        ins = pe.transpose(cg[(13 + k) % 2][:, j * L + t * P:j * L + (t + 1) * P],
                                           pv[:, t, j * P:(j + 1) * P], ident[:])
                ins.then_inc(S["cg_done"], 1)

            g0 = phases["at1"].groups
            def head_values(q):
                pe.wait_ge(S["cg_taken"], 14 + q)
                if q >= 2:
                    pe.wait_ge(S["tg_full"], g0 + q - 1)
                c0 = VA_COL + q // 4 * HD
                for j in range(2):
                    ins = pe.matmul(acc[2 + q % 2][:, 0:L], proj[:, j, c0:c0 + HD], pt1[:, q % 2, j],
                                    start=(j == 0), stop=(j == 1))
                ins.then_inc(S["o_done"], 1)

            def diff_values(h):
                pe.wait_ge(S["cg_taken"], 22 + h)
                if h < 2:
                    pe.wait_ge(S["tg_full"], g0 + 7 + h)
                else:
                    pe.wait_ge(S["o_taken"], h - 1)
                for t in range(2):
                    for j in range(2):
                        ins = pe.matmul(acc[2 + h % 2][:, t * L:(t + 1) * L], pt1[:, h % 2, j, t * P:(t + 1) * P],
                                        proj[:, j, VD_COL + h * L:VD_COL + (h + 1) * L], start=(j == 0), stop=(j == 1))
                ins.then_inc(S["o_done"], 1)

            scores(0)
            for q in range(8):
                scores(q + 1)
                turn_p(q, pr1[:, q % 2])
                if q:
                    head_values(q - 1)
            scores(9)
            head_values(7)
            for h in range(B_HEADS):
                if h + 1 < B_HEADS:
                    scores(10 + 2 * h)
                    scores(11 + 2 * h)
                turn_p(8 + h, pr1[:, 0])
                if h:
                    diff_values(h - 1)
            diff_values(B_HEADS - 1)
            for h in range(B_HEADS):
                pe.wait_ge(S["ob_made"], h + 2)
                if h >= 2:
                    pe.wait_ge(S["tg_full"], g0 + 8 + h - 1)
                for f in range(2):
                    for t in range(2):
                        ins = pe.transpose(tp[h % 2][:, f * L + t * P:f * L + (t + 1) * P],
                                           ob[:, h, t, f * P:(f + 1) * P], ident[:])
                ins.then_inc(S["tp_done"], 1)
            stream(phases["o1"], h1, 4, 2)
            norm(phases["n3"], ns1, 2)
            gate_up(phases["g2"], 2 * FC, FC + 2)
            down_proj(phases["d2"], DOWN)

            units, cgs = 0, 25
            for ly in range(2):
                nt = NT[ly]
                norm(phases[f"n4{ly}"], ns2, 4)
                stream(phases[f"ca{ly}"], hT, 5, nt)
                pe.wait_ge(S["glu_made"], ly + 1)
                wait(pe, "tg_full", phases[f"ca{ly}"].groups)
                for c in range(4):
                    if c >= 2:
                        pe.wait_ge(S["yt_taken"], 4 * ly + c - 1)
                    for t in range(nt):
                        ins = pe.transpose(tp[c % 2][:, t * P:(t + 1) * P], ca[:, 0, t, c * P:(c + 1) * P], ident[:])
                    ins.then_inc(S["yt_done"], 1)
                pe.wait_ge(S["ca_const_in"], 48 * (ly + 1))
                pe.wait_ge(S["acc_taken"], phases[f"ca{ly}"].taken + 5 * nt)
                for g in range(4):
                    if g >= 2:
                        pe.wait_ge(S["pl_taken"], 4 * ly + g - 1)
                    for s in range(nt // 2):
                        for j in range(2):
                            ins = pe.matmul(cg[g % 2][:, s * L:(s + 1) * L], ca[:, 3, 2 * s + j, g * P:(g + 1) * P],
                                            pmat[:, j, g, :], start=(j == 0), stop=(j == 1))
                    ins.then_inc(S["pl_done"], 1)
                pe.wait_ge(S["pl_taken"], 4 * ly + 4)
                for t in range(nt):
                    for g in range(4):
                        ins = pe.matmul(acc[t][:, g * P:(g + 1) * P], pdT[:, g, t * P:(t + 1) * P], wpool[:, g, :],
                                        start=True, stop=True)
                    ins.then_inc(S["py_done"], 1)
                pe.wait_ge(S["py_taken"], (4 if ly else 0) + nt)
                for nm_, _, n_, snt in SEGS[ly]:
                    stream(phases[f"s{ly}{nm_}"], hT, n_, snt)

                pe.wait_ge(S["cf_b"], 4 * (ly + 1))
                pe.wait_ge(S["cf_in"], 32 * (ly + 1))
                wait(pe, "acc_taken", phases[f"mx{ly}"].taken)
                pe.wait_ge(S["yt_taken"], 4 * (ly + 1))

                for t in range(nt):
                    for c in range(4):
                        ins = pe.transpose(acc[t][:, c * P:(c + 1) * P], cv[:, c, t * P:(t + 1) * P], ident[:])
                    ins.then_inc(S["cf_done"], 1)

                def normed_turn(t):
                    pe.wait_ge(S["z_made"], (5 if ly else 0) + t + 2)
                    if t >= 2:
                        pe.wait_ge(S["s_made"], (4 if ly else 0) + t - 1)
                    for c in range(4):
                        ins = pe.transpose(cg[t % 2][:, c * P:(c + 1) * P], zb[:, t % 2, c * P:(c + 1) * P], ident[:])
                    ins.then_inc(S["cz_done"], 1)

                def pointwise(t):
                    k = (4 if ly else 0) + t
                    pe.wait_ge(S["s_made"], k + 1)
                    if t >= 2:
                        pe.wait_ge(S["yc_made"], k - 1)
                    for c in range(4):
                        pe.matmul(tp[t % 2][:], sT[:, t % 2, c * P:(c + 1) * P], cpw[:, c, :], start=(c == 0), stop=False)
                    pe.matmul(tp[t % 2][:], ones[0:1, :], cpb[:], start=False, stop=True).then_inc(S["pw_done"], 1)
                normed_turn(0)
                for t in range(nt):
                    if t + 1 < nt:
                        normed_turn(t + 1)
                    pointwise(t)

                pe.wait_ge(S["yc_made"], (4 if ly else 0) + nt)
                pe.wait_ge(S["s_made"], (4 if ly else 0) + nt)
                U = 6 if nt == 4 else 4
                u0, kinds = units, kinds_of(nt)
                def staged(lap, n):
                    pe.wait_ge(S["st_dve"], lap + (8 * ly + n + 1))
                    pe.wait_ge(S["st_act"], lap + (8 * ly + n + 1))
                    pe.wait_ge(S["cg_taken"], lap * 2 + (cgs + 2 * n))
                    for m, tiles in enumerate(((0, 1, 6, 7)[:nt], (2, 3, 4, 5))):
                        for k, tt in enumerate(tiles):
                            ins = pe.transpose(cg[m][:, k * P:(k + 1) * P], st[:, tt], ident[:])
                        ins.then_inc(S["cg_done"], 1)

                def na_scores(lap, u):
                    e, t = kinds[u % U]
                    r = slice(e * NA_D, (e + 1) * NA_D)
                    if u % U == 0:
                        pe.wait_ge(S["cg_taken"], lap * 2 + (cgs + 2 * (u // U) + 2))
                        pe.wait_ge(S["bias_ready"], lap + (8 * ly + u // U + 1))
                    pe.wait_ge(S["p_made"], lap * U + (16 + u0 + u - 1))
                    if t < 2:
                        w = (6 * e + 2 - 2 * t) * GRID
                        pe.matmul(acc[u % 2][:], T[r, t * P:(t + 1) * P], T[r, CH:2 * CH], start=True, stop=False)
                        ins = pe.matmul(acc[u % 2][:, 0:L], turn[:], bias[:].rearrange("p h n -> p (h n)")[:, bass.ds(
                            lap * (12 * GRID) + (u // U * 12 * GRID + w), L)], start=False, stop=True)
                    else:
                        for tt in range(2):
                            ins = pe.matmul(acc[u % 2][:, tt * L:(tt + 1) * L], T[r, L + tt * P:L + (tt + 1) * P],
                                            T[r, CH + L:2 * CH], start=True, stop=True)
                    ins.then_inc(S["s_done"], 1)

                def na_turn(lap, u):
                    pe.wait_ge(S["p_made"], lap * U + (16 + u0 + u + 1))
                    for j in range(4):
                        src = pr[:, u % 2, j * P:(j + 1) * P] if kinds[u % U][1] < 2 else \
                            pr[:, u % 2, (j % 2) * L + j // 2 * P:(j % 2) * L + j // 2 * P + P]
                        ins = pe.transpose(tp[u % 2][:, j * P:(j + 1) * P], src, ident[:])
                    ins.then_inc(S["pt_done"], 1)

                def na_values(lap, u):
                    e, t = kinds[u % U]
                    pe.wait_ge(S["pt_taken"], lap * U + (u0 + u + 1))
                    pe.wait_ge(S["o_taken"], lap * U + (B_HEADS + u0 + u - 1))
                    for k in range(1 if t < 2 else 2):
                        js = range(4) if t < 2 else range(2)
                        for j in js:
                            lh = pt[:, u % 2, j * P:(j + 1) * P] if t < 2 else \
                                pt[:, u % 2, j * L + k * P:j * L + (k + 1) * P]
                            ins = pe.matmul(acc[2 + u % 2][:, k * NA_D:(k + 1) * NA_D], lh,
                                            qkvg[:, 2, j if t < 2 else 2 + j, pair_cols(lap, u // U, e * NA_D, NA_D)],
                                            start=(j == 0), stop=(j == js[-1]))
                    ins.then_inc(S["o_done"], 1)

                def step(lap, k, end):
                    if k + 1 < end:
                        na_scores(lap, k + 1)
                    if k == U - 2 and end > U:
                        staged(lap, 1)
                    if k < end:
                        na_turn(lap, k)
                    na_values(lap, k - 1)

                staged(0, 0)
                na_scores(0, 0)
                na_scores(0, 1)
                na_turn(0, 0)
                na_laps(pe, step, nt)
                units += 8 * U
                cgs += 16
                pe.wait_ge(S["o_taken"], B_HEADS + units)
                pe.wait_ge(S["pt_taken"], units)
                ph = phases[f"mx{ly}"]
                for t in range(nt):
                    for g in range(4):
                        m = 4 * t + g
                        bank_free(ph.groups + m, m)
                        src = (ya[:, t], qkvg[:, 3, t, 0:CH], qkvg[:, 3, t, CH:2 * CH], gC[:, t])[g]
                        turn4(0, g, lambda k: src[:, k * P:(k + 1) * P])
                for k in range(2 * nt):
                    pe.wait_ge(S["gate_diag"], 8 * ly + k + 1)
                    wait(pe, "gs_taken", 8 * ly + k - 1)
                    pe.matmul(cg[k % 2][:], ones[:], dg[:, k % 2], start=True, stop=True).then_inc(S["gs_done"], 1)
                stream(phases[f"o2{ly}"], hT, 4, nt)

        @block.gpsimd
        def _(pool):
            pool.wait_ge(S["pieces_used"], phases["n40"].pieces)
            pool.dma_start(ogain[:], row_bc(a["out_norm"], D)).then_inc(S["fin_in"], 16)
            pool.dma_start(x4[:, 2:4, :], ctx_v).then_inc(S["ctx_in"], 16)
            for ly in range(2):
                nt = NT[ly]
                if ly == 0:
                    pool.wait_ge(S["x4_in"], 2)
                else:
                    pool.wait_ge(S["acc_taken"], phases["n41"].taken)
                pool.dma_start(xs_v, x4[:, 0:2, :]).then_inc(S["xs_out"], 16)
                if ly == 1:
                    pool.wait_ge(S["conv_step"], 132)
                pool.memset(yT[:, :, :, 0:PAD], 0.0).then_inc(S["pad_made"], 1)
                pool.memset(yT[:, :, :, PAD + L:YW], 0.0).then_inc(S["pad_made"], 1)
                pool.wait_ge(S["na_in"], 64 * (ly + 1))
                pool.wait_ge(S["bias_in"], 12 * 16 * (ly + 1))
                for pair in range(NA_H // 2):
                    bv = bias[:, 2 * pair:2 * pair + 2].rearrange("p h (r n) -> p (h r) n", n=GRID)
                    pool.tensor_tensor(bv, bv, mask[:].unsqueeze(1).broadcast_to([P, 12, GRID]), ALU.add)\
                        .then_inc(S["bias_ready"], 1)
            pool.wait_ge(S["acc_taken"], phases["end"].taken)
            pool.dma_start(fgain[:], row_bc(a["final_norm_g_2"], D)).then_inc(S["fin_in"], 16)


def kinds_of(nt):
    return [(e, t) for e in range(2) for t in ((0, 1, 2) if nt == 4 else (0, 1))]


def kernel(**inputs):
    import concourse.bacc as bacc
    from concourse.bass_utils import run_bass_kernel_spmd

    cosa, sina, cosb, sinb, cosn, sinn = rope_tables()
    arrays = {k: np.ascontiguousarray(v) for k, v in inputs.items()}
    arrays["vrows"] = np.concatenate([np.asarray(inputs[k]).reshape(-1, P) for k in (
        "ffn1_norm", "mix_norm", "ffn2_norm", "norm_g_2", "c_2", "c_ctx_2")])
    arrays.update(cosa=cosa, sina=sina, cosb=cosb, sinb=sinb, cosn=cosn, sinn=sinn, pmat=pool_matrices(),
                  mask=window_mask(), turn=np.kron(np.eye(2), np.eye(GRID)[::-1]).astype(np.float32), ident=np.eye(P, dtype=np.float32),
                  sel=np.tile(np.eye(2, dtype=np.float32), (2, 1)))
    nc = bacc.Bacc("TRN2", target_bir_lowering=False, num_devices=1)
    aps = {k: nc.dram_tensor(k, v.shape, F32, kind="ExternalInput").ap() for k, v in arrays.items()}
    out = nc.dram_tensor("y", (1, L, D), F32, kind="ExternalOutput").ap()
    xs = nc.dram_tensor("x_rest", (L, D), F32, kind="Internal").ap()
    build(nc, aps, out, xs)
    r = run_bass_kernel_spmd(nc, [arrays], core_ids=[0])
    return r.results[0]["y"]
```
